# Optimizing a Trainium2 kernel written in Bass

```python
import math
import numpy as np
import jax, jax.numpy as jnp
from jax import lax

D_MODEL = 2048
BATCH = 1
SEQ = 1024
DEPTH = 1
DEC_BATCH = 8
DEC_SEQ = 8
PAST_LEN = 1024
PAGE_SIZE = 128

HEAD_DIM = 128
DIL_PAIRS = ((128, 1), (512, 4), (2048, 16))
N_GROUPS_A = len(DIL_PAIRS)
HEADS_PER_GROUP_A = 4
N_QH_A = N_GROUPS_A * HEADS_PER_GROUP_A
N_KVH_A = HEADS_PER_GROUP_A
WIDTH_A = HEADS_PER_GROUP_A * HEAD_DIM
WINDOW_MAX = 2048
N_QH_B = 8
N_KVH_B = 2
WIDTH_B = N_QH_B * HEAD_DIM
N_IDX_HEADS = 4
IDX_DIM = 64
TOPK_MAX = 256
BLOCK = 128
ROPE_THETA = 10000.0
EPS = 1e-6
SPLIT_SIZES = (N_QH_A * HEAD_DIM, N_KVH_A * HEAD_DIM, N_KVH_A * HEAD_DIM, WIDTH_A,
               N_QH_B * HEAD_DIM, N_KVH_B * HEAD_DIM, N_KVH_B * HEAD_DIM, WIDTH_B,
               N_IDX_HEADS * IDX_DIM, IDX_DIM, N_IDX_HEADS, D_MODEL, D_MODEL)
D_IN = sum(SPLIT_SIZES)

kernel_name = 'hybrid_dilated_dsa_gated_decode_step'

def rmsnorm(x, g):
    xf = x.astype(jnp.float32)
    y = xf * lax.rsqrt(jnp.mean(xf * xf, axis=-1, keepdims=True) + EPS)
    return (y * g.astype(jnp.float32)).astype(x.dtype)

def rope(x, pos):
    half = x.shape[-1] // 2
    inv = jnp.exp(jnp.arange(half, dtype=jnp.float32) * (-math.log(ROPE_THETA) / half))
    ang = pos.astype(jnp.float32)[:, None] * inv[None, :]
    cos, sin = jnp.cos(ang)[:, None, :], jnp.sin(ang)[:, None, :]
    xf = x.astype(jnp.float32)
    x1, x2 = xf[..., :half], xf[..., half:]
    return jnp.concatenate([x1 * cos - x2 * sin, x2 * cos + x1 * sin], axis=-1).astype(x.dtype)

def modulate(x, c, g_norm, w_ada, b_ada):
    mod = jax.nn.silu(c) @ w_ada + b_ada
    shift, scale, gate = jnp.split(mod, 3, axis=-1)
    h = rmsnorm(x, g_norm) * (1 + scale[:, None, :]) + shift[:, None, :]
    return h, gate[:, None, :]

def in_proj(h, w_in, pos):
    B, T = h.shape[:2]
    offs = np.cumsum(SPLIT_SIZES)[:-1].tolist()
    (q_a, k_a, v_a, z_a, q_b, k_b, v_b, z_b, q_i, k_i, w_i, g_a, g_b) = jnp.split(h @ w_in, offs, axis=-1)
    q_a = rope(q_a.reshape(B, T, N_QH_A, HEAD_DIM), pos)
    k_a = rope(k_a.reshape(B, T, N_KVH_A, HEAD_DIM), pos)
    v_a = v_a.reshape(B, T, N_KVH_A, HEAD_DIM)
    q_b = rope(q_b.reshape(B, T, N_QH_B, HEAD_DIM), pos)
    k_b = rope(k_b.reshape(B, T, N_KVH_B, HEAD_DIM), pos)
    v_b = v_b.reshape(B, T, N_KVH_B, HEAD_DIM)
    q_i = rope(q_i.reshape(B, T, N_IDX_HEADS, IDX_DIM), pos)
    k_i = rope(k_i[:, :, None, :], pos)[:, :, 0, :]
    w_i = w_i * (N_IDX_HEADS ** -0.5)
    return (q_a, k_a, v_a, z_a, q_b, k_b, v_b, z_b, q_i, k_i, w_i, g_a, g_b)

def merge_groups(outs, lses, dtype):
    o = jnp.stack(outs)
    alpha = jax.nn.softmax(jnp.stack(lses), axis=0)
    o = jnp.sum(alpha[..., None] * o, axis=0)
    B, T = o.shape[:2]
    return o.reshape(B, T, WIDTH_A).astype(dtype)

def dilated_band_group(q, k, v, window, dil):
    B, S, H, Dh = q.shape
    L = S // dil
    nb = -(-L // BLOCK)
    Lp = nb * BLOCK
    sub_w = window // dil

    def split(x):
        x = x.reshape(B, L, dil, H, Dh).transpose(0, 2, 1, 3, 4).reshape(B * dil, L, H, Dh)
        x = jnp.pad(x, ((0, 0), (0, Lp - L), (0, 0), (0, 0)))
        return x.reshape(B * dil, nb, BLOCK, H, Dh)

    def with_prev(x):
        prev = jnp.pad(x, ((0, 0), (1, 0), (0, 0), (0, 0), (0, 0)))[:, :-1]
        return jnp.concatenate([prev, x], axis=2)

    def unsplit(x):
        x = x.reshape(B, dil, Lp, *x.shape[3:])[:, :, :L]
        return jnp.swapaxes(x, 1, 2).reshape(B, S, *x.shape[3:])

    qb = split(q)
    kc = with_prev(split(k))
    vc = with_prev(split(v))
    dist = np.arange(BLOCK)[:, None] + BLOCK - np.arange(2 * BLOCK)[None, :]
    band = (dist >= 0) & (dist <= sub_w)
    has_prev = (np.arange(nb) > 0)[:, None, None] | (np.arange(2 * BLOCK) >= BLOCK)[None, None, :]
    mask = band[None] & has_prev
    s = jnp.einsum('nbqhd,nbkhd->nbhqk', qb, kc, preferred_element_type=jnp.float32) * (HEAD_DIM ** -0.5)
    s = jnp.where(mask[None, :, None], s, -jnp.inf)
    m = jnp.max(s, axis=-1, keepdims=True)
    p = jnp.exp(s - m)
    l = jnp.sum(p, axis=-1, keepdims=True)
    o = jnp.einsum('nbhqk,nbkhd->nbqhd', p / l, vc.astype(jnp.float32))
    lse = jnp.swapaxes((m + jnp.log(l))[..., 0], 2, 3)
    return unsplit(o), unsplit(lse)

def dilated_prompt(q_a, k_a, v_a):
    B, S = q_a.shape[:2]
    qg = q_a.reshape(B, S, N_GROUPS_A, HEADS_PER_GROUP_A, HEAD_DIM)
    outs, lses = [], []
    for g, (win, dil) in enumerate(DIL_PAIRS):
        o, lse = dilated_band_group(qg[:, :, g], k_a, v_a, win, dil)
        outs.append(o)
        lses.append(lse)
    return merge_groups(outs, lses, q_a.dtype)

def dilated_gather_group(q, k_new, v_new, k_buf, v_buf, window, dil):
    DB, T, H, Dh = q.shape
    W = k_buf.shape[1]
    n_k = window // dil + 1
    rel = np.arange(T)[:, None] - dil * np.arange(n_k)[None, :]
    buf_ok = (rel < 0) & (rel + W >= 0)
    rows = np.clip(rel + W, 0, W - 1).reshape(-1).astype(np.int32)
    kb = jnp.take(k_buf, rows, axis=1).reshape(DB, T, n_k, H, Dh)
    vb = jnp.take(v_buf, rows, axis=1).reshape(DB, T, n_k, H, Dh)
    d_new = np.arange(T)[:, None] - np.arange(T)[None, :]
    new_ok = (d_new >= 0) & (d_new % dil == 0) & (d_new <= window)
    scale = HEAD_DIM ** -0.5
    s_buf = jnp.einsum('bthd,btjhd->bthj', q, kb, preferred_element_type=jnp.float32) * scale
    s_new = jnp.einsum('bthd,buhd->bthu', q, k_new, preferred_element_type=jnp.float32) * scale
    s = jnp.concatenate([jnp.where(buf_ok[None, :, None, :], s_buf, -jnp.inf),
                         jnp.where(new_ok[None, :, None, :], s_new, -jnp.inf)], axis=-1)
    m = jnp.max(s, axis=-1, keepdims=True)
    p = jnp.exp(s - m)
    l = jnp.sum(p, axis=-1, keepdims=True)
    o = (jnp.einsum('bthj,btjhd->bthd', p[..., :n_k], vb.astype(jnp.float32))
         + jnp.einsum('bthu,buhd->bthd', p[..., n_k:], v_new.astype(jnp.float32))) / l
    return o, (m + jnp.log(l))[..., 0]

def dilated_sample(q_a, k_a, v_a, k_buf, v_buf):
    DB, T = q_a.shape[:2]
    qg = q_a.reshape(DB, T, N_GROUPS_A, HEADS_PER_GROUP_A, HEAD_DIM)
    outs, lses = [], []
    for g, (win, dil) in enumerate(DIL_PAIRS):
        o, lse = dilated_gather_group(qg[:, :, g], k_a, v_a, k_buf, v_buf, win, dil)
        outs.append(o)
        lses.append(lse)
    return merge_groups(outs, lses, q_a.dtype)

def index_scores(q_i, k_i, w_i):
    s = jnp.einsum('bthd,bsd->bths', q_i, k_i, preferred_element_type=jnp.float32) * (IDX_DIM ** -0.5)
    return jnp.einsum('bths,bth->bts', jax.nn.relu(s), w_i.astype(jnp.float32))

def sparse_attend(q, ks, vs, sel, k_ex=None, v_ex=None, sel_ex=None):
    B, T, Hq, Dh = q.shape
    kvh = ks.shape[-2]
    n = ks.shape[2]
    qg = q.reshape(B, T, kvh, Hq // kvh, Dh)
    scale = HEAD_DIM ** -0.5
    s = jnp.einsum('btkgd,btnkd->btkgn', qg, ks, preferred_element_type=jnp.float32) * scale
    s = jnp.where(sel[:, :, None, None, :], s, -jnp.inf)
    if k_ex is not None:
        s_ex = jnp.einsum('btkgd,bukd->btkgu', qg, k_ex, preferred_element_type=jnp.float32) * scale
        s = jnp.concatenate([s, jnp.where(sel_ex[:, :, None, None, :], s_ex, -jnp.inf)], axis=-1)
    p = jax.nn.softmax(s, axis=-1)
    o = jnp.einsum('btkgn,btnkd->btkgd', p[..., :n], vs.astype(jnp.float32))
    if k_ex is not None:
        o = o + jnp.einsum('btkgu,bukd->btkgd', p[..., n:], v_ex.astype(jnp.float32))
    return o.reshape(B, T, Hq * Dh).astype(q.dtype)

def dsa_prompt(q_b, k_b, v_b, q_i, k_i, w_i):
    B, S = q_b.shape[:2]
    topk = min(TOPK_MAX, S // 4)
    nqb = S // BLOCK
    kpos = jnp.arange(S)

    def blocks(x):
        return jnp.moveaxis(x.reshape(B, nqb, BLOCK, *x.shape[2:]), 1, 0)

    def body(args):
        qb, qib, wib, start = args
        qpos = start + jnp.arange(BLOCK)
        sc = index_scores(qib, k_i, wib)
        sc = jnp.where(kpos[None, None, :] <= qpos[None, :, None], sc, -jnp.inf)
        vals, idx = lax.top_k(sc, topk)
        ks = jax.vmap(lambda kk, ii: kk[ii])(k_b, idx)
        vs = jax.vmap(lambda vv, ii: vv[ii])(v_b, idx)
        return sparse_attend(qb, ks, vs, vals > -jnp.inf)

    out = lax.map(body, (blocks(q_b), blocks(q_i), blocks(w_i), jnp.arange(nqb, dtype=jnp.int32) * BLOCK))
    return jnp.moveaxis(out, 0, 1).reshape(B, S, WIDTH_B)

def dsa_sample(q_b, k_b, v_b, q_i, k_i, w_i, pool_k, pool_v, pool_ik, page_table):
    DB, T = q_b.shape[:2]
    P = page_table.shape[1] * PAGE_SIZE
    topk = min(TOPK_MAX, (P + T) // 4)
    past_ik = pool_ik[page_table].reshape(DB, P, IDX_DIM)
    causal = np.tril(np.ones((T, T), dtype=bool))
    sc = jnp.concatenate([index_scores(q_i, past_ik, w_i),
                          jnp.where(causal[None], index_scores(q_i, k_i, w_i), -jnp.inf)], axis=-1)
    vals, idx = lax.top_k(sc, topk)
    valid = vals > -jnp.inf
    pidx = jnp.minimum(idx, P - 1)
    phys = page_table[jnp.arange(DB)[:, None, None], pidx // PAGE_SIZE]
    off = pidx % PAGE_SIZE
    ks = pool_k[phys, off]
    vs = pool_v[phys, off]
    sel_new = jnp.any((idx[..., None] == (P + jnp.arange(T))) & valid[..., None], axis=2)
    return sparse_attend(q_b, ks, vs, valid & (idx < P), k_b, v_b, sel_new)

def branch_out(o_a, o_b, z_a, z_b, g_a, g_b, w_pa, w_pb, w_out):
    u_a = (o_a * jax.nn.silu(z_a)) @ w_pa
    u_b = (o_b * jax.nn.silu(z_b)) @ w_pb
    return (jax.nn.sigmoid(g_a) * u_a + jax.nn.sigmoid(g_b) * u_b) @ w_out

def setup_inputs(seed: int = 0) -> dict:
    key = jax.random.key(seed)
    ks = jax.random.split(key, 20)
    n_pages = PAST_LEN // PAGE_SIZE
    n_pool = (5 * DEC_BATCH * n_pages + 3) // 4
    win_buf = min(WINDOW_MAX, PAST_LEN)

    def nrm(k, shape, s=1.0):
        return s * jax.random.normal(k, shape, jnp.float32)

    page_table = jax.random.permutation(ks[7], n_pool)[: DEC_BATCH * n_pages].reshape(DEC_BATCH, n_pages).astype(jnp.int32)
    return {
        'x_prompt': nrm(ks[0], (BATCH, SEQ, D_MODEL)),
        'x_sample': nrm(ks[1], (DEC_BATCH, DEC_SEQ, D_MODEL)),
        'cache_win_k': nrm(ks[2], (DEPTH, DEC_BATCH, win_buf, N_KVH_A, HEAD_DIM)),
        'cache_win_v': nrm(ks[3], (DEPTH, DEC_BATCH, win_buf, N_KVH_A, HEAD_DIM)),
        'cache_k': nrm(ks[4], (DEPTH, n_pool, PAGE_SIZE, N_KVH_B, HEAD_DIM)),
        'cache_v': nrm(ks[5], (DEPTH, n_pool, PAGE_SIZE, N_KVH_B, HEAD_DIM)),
        'cache_idx_k': nrm(ks[6], (DEPTH, n_pool, PAGE_SIZE, IDX_DIM)),
        'page_table': page_table,
        'c_prompt': nrm(ks[8], (BATCH, D_MODEL)),
        'c_sample': nrm(ks[9], (DEC_BATCH, D_MODEL)),
        'g_norm': 1.0 + nrm(ks[10], (DEPTH, D_MODEL), 0.02),
        'w_ada': nrm(ks[11], (DEPTH, D_MODEL, 3 * D_MODEL), D_MODEL ** -0.5),
        'b_ada': nrm(ks[12], (DEPTH, 3 * D_MODEL), 0.02),
        'w_in': nrm(ks[13], (DEPTH, D_MODEL, D_IN), D_MODEL ** -0.5),
        'w_pa': nrm(ks[14], (DEPTH, WIDTH_A, D_MODEL), WIDTH_A ** -0.5),
        'w_pb': nrm(ks[15], (DEPTH, WIDTH_B, D_MODEL), WIDTH_B ** -0.5),
        'w_out': nrm(ks[16], (DEPTH, D_MODEL, D_MODEL), D_MODEL ** -0.5),
        'g_final': 1.0 + nrm(ks[17], (D_MODEL,), 0.02),
    }

def reference(x_prompt, x_sample, cache_win_k, cache_win_v, cache_k, cache_v, cache_idx_k, page_table,
              c_prompt, c_sample, g_norm, w_ada, b_ada, w_in, w_pa, w_pb, w_out, g_final):
    pos_p = jnp.arange(SEQ, dtype=jnp.int32)
    pos_s = PAST_LEN + jnp.arange(DEC_SEQ, dtype=jnp.int32)
    win_p = min(WINDOW_MAX, SEQ)
    xp, xs = x_prompt, x_sample
    wk_p, wv_p, k_p, v_p, ik_p = [], [], [], [], []
    wk_s, wv_s, k_s, v_s, ik_s = [], [], [], [], []
    for l in range(DEPTH):
        h, gate = modulate(xp, c_prompt, g_norm[l], w_ada[l], b_ada[l])
        (q_a, k_a, v_a, z_a, q_b, k_b, v_b, z_b, q_i, k_i, w_i, g_a, g_b) = in_proj(h, w_in[l], pos_p)
        o_a = dilated_prompt(q_a, k_a, v_a)
        o_b = dsa_prompt(q_b, k_b, v_b, q_i, k_i, w_i)
        xp = xp + gate * branch_out(o_a, o_b, z_a, z_b, g_a, g_b, w_pa[l], w_pb[l], w_out[l])
        wk_p.append(k_a[:, SEQ - win_p:])
        wv_p.append(v_a[:, SEQ - win_p:])
        k_p.append(k_b)
        v_p.append(v_b)
        ik_p.append(k_i)
        h, gate = modulate(xs, c_sample, g_norm[l], w_ada[l], b_ada[l])
        (q_a, k_a, v_a, z_a, q_b, k_b, v_b, z_b, q_i, k_i, w_i, g_a, g_b) = in_proj(h, w_in[l], pos_s)
        o_a = dilated_sample(q_a, k_a, v_a, cache_win_k[l], cache_win_v[l])
        o_b = dsa_sample(q_b, k_b, v_b, q_i, k_i, w_i, cache_k[l], cache_v[l], cache_idx_k[l], page_table)
        xs = xs + gate * branch_out(o_a, o_b, z_a, z_b, g_a, g_b, w_pa[l], w_pb[l], w_out[l])
        wk_s.append(k_a)
        wv_s.append(v_a)
        k_s.append(k_b)
        v_s.append(v_b)
        ik_s.append(k_i)
    y_prompt = rmsnorm(xp, g_final)
    y_sample = rmsnorm(xs, g_final)
    return (y_prompt, y_sample,
            jnp.stack(wk_p), jnp.stack(wv_p), jnp.stack(k_p), jnp.stack(v_p), jnp.stack(ik_p),
            jnp.stack(wk_s), jnp.stack(wv_s), jnp.stack(k_s), jnp.stack(v_s), jnp.stack(ik_s))


_drawn_inputs = setup_inputs


def setup_inputs(seed=0):
    import zlib

    import numpy as np

    out = dict(_drawn_inputs(seed))
    spreads = {}
    factors = {'g_norm': 3.166, 'g_final': 2.826}
    for name, (base, spread) in spreads.items():
        noise = np.random.default_rng([zlib.crc32(name.encode()), seed]).standard_normal(out[name].shape)
        drawn = base * np.exp(spread * noise) if base else spread * noise
        out[name] = __import__('jax').numpy.asarray(drawn.astype(out[name].dtype))
    for name, factor in factors.items():
        out[name] = (out[name] * factor).astype(out[name].dtype)
    return out
```

```python
from contextlib import ExitStack

import numpy as np
import concourse.bass as bass
from concourse import mybir

F32 = mybir.dt.float32
F32R = mybir.dt.float32r
BF16 = mybir.dt.bfloat16
I32 = mybir.dt.int32
ALU = mybir.AluOpType
ACT = mybir.ActivationFunctionType
AX = mybir.AxisListType.X

P = 128
D = 2048
KT = D // P
SEQ = 1024
NB, NT = 8, 8
SMP = NB * NT
TOK = SEQ + SMP
QT = SEQ // P
TT = QT + 1
PAST = 1024
PAGES = PAST // P
POOL_PAGES = 80
HD = 128
HA, HB, KVB, GRP = 4, 8, 2, 3
IH, ID = 4, 64
TOPK = 256
EPS = 1e-6
SCALE = HD ** -0.5
BIG = 2.0 ** 100
TAKEN = -3.0e38
CHUNKS = ((0, 384), (384, 736), (736, 1088))
DILS = ((128, 1), (512, 4), (2048, 16))

N_IDX = 3
N_MAIN = 44
N_GATE = 32
COL_QI, COL_KI, COL_G = 5632, 5888, 5956
T_QA, T_KA, T_VA, T_ZA = N_IDX, N_IDX + 12, N_IDX + 16, N_IDX + 20
T_QB, T_KB, T_VB, T_ZB = N_IDX + 24, N_IDX + 32, N_IDX + 34, N_IDX + 36
T_G = N_IDX + N_MAIN
N_PROJ = T_G + N_GATE
ADA_C = 256
ADA_N = 3 * D // ADA_C


def shape_tables():
    pos = np.concatenate([np.arange(SEQ), np.tile(PAST + np.arange(NT), NB)]).astype(np.float32)

    def rot(dim):
        half = dim // 2
        inv = np.exp(np.arange(half, dtype=np.float32) * np.float32(-np.log(10000.0) / half)).astype(np.float32)
        ang = (pos[None, :] * inv[:, None]).astype(np.float32)
        c, s = np.cos(ang).astype(np.float32), np.sin(ang).astype(np.float32)
        reps = P // dim
        return np.concatenate([np.concatenate([c, c])] * reps), np.concatenate([np.concatenate([s, -s])] * reps)

    t = {}
    t["rot"] = np.stack([*rot(HD), *rot(ID)]).astype(np.float32)
    p, c = np.arange(P)[:, None], np.arange(P)[None, :]
    blocks = []
    for n_blk, (win, dil) in zip((8, 5, 2), DILS[::-1]):
        for b in range(n_blk):
            dist = (n_blk - 1 - b) * P + p - c
            blocks.append((dist >= 0) & (dist % dil == 0) & (dist <= win))
    ok = np.concatenate(blocks, 1)
    t["mask_p"] = np.where(ok, 0.0, -BIG).astype(np.float32)
    rows = np.arange(96)
    g, tq = rows // 32, rows % NT
    key = np.arange(PAST)
    ma = np.zeros((96, PAST), bool)
    mn = np.zeros((96, NB, SMP), bool)
    for r in range(96):
        win, dil = DILS[g[r]]
        dist = PAST + tq[r] - key
        ma[r] = (dist % dil == 0) & (dist <= win)
        for b in range(NB):
            u = np.arange(SMP)
            d2 = tq[r] - u % NT
            mn[r, b] = (u // NT == b) & (d2 >= 0) & (d2 % dil == 0) & (d2 <= win)
    t["mask_s"] = np.where(np.concatenate([ma, mn.reshape(96, -1)], 1), 0.0, -BIG).astype(np.float32)
    r64 = np.arange(SMP)
    u = np.arange(SMP)
    ok = (u[None] // NT == r64[:, None] // NT) & (u[None] <= r64[:, None])
    t["mask_i"] = np.where(ok, 0.0, -BIG).astype(np.float32)
    rep = np.zeros((SMP, NB, SMP), np.float32)
    for b in range(NB):
        for r in range(SMP):
            rep[b * NT + r % NT, b, r] = 1.0
    t["rep"] = rep
    same = (np.arange(96)[:, None] % 32 == np.arange(96)[None] % 32)
    t["same"] = same.astype(np.float32)
    return t


def need(eng, sem, value):
    if not (isinstance(value, int) and value <= 0):
        eng.wait_ge(sem, value)


def decode_step(nc, ins, outs, scr):
    ctx = ExitStack()
    with ctx:
        base = (nc.sbuf_base + 63) // 64 * 64

        def at(name, shape, dt, off):
            return nc.alloc_sbuf_tensor_at(name, shape, dt, offset=base + off)

        def sem(name):
            return ctx.enter_context(nc.semaphore(name))

        banks = ctx.enter_context(nc.psum_tensor("banks", [P, 8, 512], F32))

        ident = at("ident", [P, P], F32, 0)
        identb = at("identb", [P, P], BF16, 512)
        mod_t = at("mod_t", [P, 48, 9], F32, 768)
        gmod = at("gmod", [P, KT, 9], F32, 2496)
        bada_t = at("bada_t", [P, 48], F32, 3072)
        gn_t = at("gn_t", [P, KT], F32, 3264)
        ssum = at("ssum", [P, 16], F32, 3328)
        rstd = at("rstd", [P, 16], F32, 3392)
        epst = at("epst", [P, 1], F32, 3456)
        c_t = at("c_t", [P, KT, 9], F32, 3488)
        H_HI, H_LO = 4352, 4352 + KT * TOK * 4
        h_hi = at("h_hi", [P, KT, TOK], F32R, H_HI)
        h_lo = at("h_lo", [P, KT, TOK], F32R, H_LO)
        xn_t = at("xn_t", [P, KT, TOK], F32, H_LO)
        ada_w = at("ada_w", [P, 2, KT, ADA_C], F32, H_HI)
        c_rows = at("c_rows", [9, D], F32, H_HI + 32768)
        c_silu = at("c_silu", [9, D], F32, H_HI + 40960)
        bada_r = at("bada_r", [48, P], F32, H_HI + 49152)
        gn_r = at("gn_r", [KT, P], F32, H_HI + 49664)
        W0 = H_LO + KT * TOK * 4
        w_hi = at("w_hi", [P, 2, KT, P], F32R, W0)
        w_lo = at("w_lo", [P, 2, KT, P], F32R, W0 + 16384)
        w_raw = at("w_raw", [P, KT, P], F32, W0 + 32768)
        rot_cos = at("rot_cos", [P, TOK], F32, W0 + 40960)
        rot_sin = at("rot_sin", [P, TOK], F32, W0 + 45312)
        col = at("col", [P, 2, TOK], F32, W0 + 49664)
        rot_a = at("rot_a", [P, 2, 384], F32, W0 + 58368)
        rot_b = at("rot_b", [P, 2, 384], F32, W0 + 61440)
        work = at("work", [P, TOK], F32, W0 + 64512)
        best8 = at("best8", [P, 8], F32, W0 + 68864)
        pages_i = at("pages_i", [P, PAGES, NB, ID], F32, W0)
        past_t = at("past_t", [P, NB // 2, PAST], F32, W0 + 16384)
        ki_hi = at("ki_hi", [P, TOK], F32, W0 + 32768)
        ki_lo = at("ki_lo", [P, TOK], F32, W0 + 37120)
        qi_t = at("qi_t", [P, 2, TOK], F32, W0 + 41472)
        qi_pair = at("qi_pair", [P, IH, NB // 2, SMP], F32, W0 + 50176)
        relu_s = at("relu_s", [P, 2, TOK], F32, W0 + 54272)
        wi_r = at("wi_r", [IH, TOK], F32, W0 + 62976)
        wi_tok = at("wi_tok", [P, TT, IH], F32, W0 + 67328)
        diag = at("diag", [P, P], F32, W0 + 67488)
        mask_i = at("mask_i", [SMP, SMP], F32, W0 + 68000)
        acc = at("acc", [P, 2, TOK], F32, W0)
        pages_n = at("pages_n", [1, NB * PAGES], I32, 4064)
        x_in = at("x_in", [P, 2, D], F32, W0)
        x_sq = at("x_sq", [P, D], F32, W0 + 16384)
        h_f = at("h_f", [P, 2, TOK], F32, W0 + 16384)

        small_in = sem("small_in")
        ident_set = sem("ident_set")
        c_act = sem("c_act")
        c_turned = sem("c_turned")
        c_copied = sem("c_copied")
        x_landed = [sem(f"x_landed{i}") for i in range(2)]
        x_ssum = sem("x_ssum")
        x_root = sem("x_root")
        x_rstd = sem("x_rstd")
        x_scaled = sem("x_scaled")
        x_turned_bank = sem("x_turned_bank")
        x_copied = sem("x_copied")
        ada_landed = [sem(f"ada_landed{i}") for i in range(2)]
        ada_used = sem("ada_used")
        mod_set = sem("mod_set")
        gmod_set = sem("gmod_set")
        hp_set = sem("hp_set")
        hs_mul = sem("hs_mul")
        hs_set = sem("hs_set")
        hi_set = sem("hi_set")
        lo_set = sem("lo_set")
        w_landed = sem("w_landed")
        w_hi_set = sem("w_hi_set")
        w_lo_set = sem("w_lo_set")
        chunk_done = sem("chunk_done")
        chunk_free = sem("chunk_free")
        rot_ready = sem("rot_ready")
        rot_set = sem("rot_set")
        idx_landed = sem("idx_landed")
        idx_pages = sem("idx_pages")
        idx_zeroed = sem("idx_zeroed")
        idx_turned = sem("idx_turned")
        idx_copied = sem("idx_copied")
        idx_pair_set = sem("idx_pair_set")
        score_done = sem("score_done")
        relu_set = sem("relu_set")
        acc_step = sem("acc_step")
        acc_set = sem("acc_set")
        acc_fill = sem("acc_fill")
        acc_stored = [sem(f"acc_stored{i}") for i in range(2)]
        work_landed = sem("work_landed")
        mask_picked = sem("mask_picked")
        mask_stored = sem("mask_stored")
        col_stored = [sem(f"col_stored{i}") for i in range(2)]

        x_tiles = [(ins["x_prompt"][0, t * P:(t + 1) * P, :], P) for t in range(QT)]
        x_tiles.append((ins["x_sample"].rearrange("b t d -> (b t) d"), SMP))
        w_in = ins["w_in"][0]
        w_ada = ins["w_ada"][0]

        def load_tile(sp, t, src, width=P):
            need(sp, w_lo_set, t)
            sp.dma_start(w_raw[:, :, 0:width], src.rearrange("(k p) n -> p k n", p=P)).then_inc(w_landed, 16)

        def split_hi(act, t, par, width=P):
            act.wait_ge(w_landed, 16 * (t + 1))
            need(act, chunk_done, 3 * (t - 1))
            nc.scalar.copy(w_hi[:, par, :, 0:width], w_raw[:, :, 0:width]).then_inc(w_hi_set, 1)

        def split_lo(dve, t, par, width=P):
            dve.wait_ge(w_hi_set, t + 1)
            nc.vector.tensor_tensor(w_lo[:, par, :, 0:width], w_raw[:, :, 0:width], w_hi[:, par, :, 0:width],
                                    ALU.subtract).then_inc(w_lo_set, 1)

        def products(pe, t, par, width=P):
            pe.wait_ge(w_lo_set, t + 1)
            for c, (a, b) in enumerate(CHUNKS):
                need(pe, chunk_free, 3 * t + c - 2)
                for k in range(KT):
                    dst = banks[0:width, c, 0:b - a]
                    nc.tensor.matmul(dst, w_hi[:, par, k, 0:width], h_hi[:, k, a:b], start=(k == 0), stop=False)
                    nc.tensor.matmul(dst, w_hi[:, par, k, 0:width], h_lo[:, k, a:b], start=False, stop=False)
                    mm = nc.tensor.matmul(dst, w_lo[:, par, k, 0:width], h_hi[:, k, a:b], start=False,
                                          stop=(k == KT - 1))
                mm.then_inc(chunk_done, 1)

        def leave_act(act, t, par, earlier, func):
            need(act, col_stored[par], 16 * earlier)
            for c, (a, b) in enumerate(CHUNKS):
                act.wait_ge(chunk_done, 3 * t + c + 1)
                act.wait_ge(chunk_free, 3 * t + c)
                nc.scalar.activation(col[:, par, a:b], banks[:, c, 0:b - a], func).then_inc(chunk_free, 1)

        def leave_rotated(dve, t, par, earlier, rotated, half, rows=P, plain=0, between=None):
            need(dve, col_stored[par], 16 * earlier)
            for c, (a, b) in enumerate(CHUNKS):
                n, s = b - a, (par + c) % 2
                need(dve, rot_set, rotated + c - 1)
                dve.wait_ge(chunk_done, 3 * t + c + 1)
                need(dve, chunk_free, 3 * t + c)
                if plain:
                    nc.vector.tensor_copy(col[rows:rows + plain, par, a:b], banks[rows:rows + plain, c, 0:n])
                for q in range(0, rows, half):
                    o = q + half if q // half % 2 == 0 else q - half
                    nc.vector.tensor_tensor(rot_b[o:o + half, s, 0:n], banks[q:q + half, c, 0:n],
                                            rot_sin[q:q + half, a:b], ALU.mult)
                nc.vector.tensor_tensor(rot_a[0:rows, s, 0:n], banks[0:rows, c, 0:n], rot_cos[0:rows, a:b],
                                        ALU.mult).then_inc(chunk_free, 1)
                dve.wait_ge(chunk_free, 3 * t + c + 1)
                nc.vector.tensor_tensor(col[0:rows, par, a:b], rot_a[0:rows, s, 0:n], rot_b[0:rows, s, 0:n],
                                        ALU.add).then_inc(rot_set, 1)
                if between:
                    between(dve)

        IDX_SRC = [(w_in[:, COL_QI:COL_QI + P], P), (w_in[:, COL_QI + P:COL_QI + 2 * P], P),
                   (w_in[:, COL_KI:COL_KI + ID + IH], ID + IH)]
        RUNS = [(T_QA, 4, "rot", True), (T_QA + 8, 4, "rot", True), (T_VA, 2, ACT.Copy, False),
                (T_ZA, 2, ACT.Silu, False), (T_QB, 5, "rot", False), (T_VB, 1, ACT.Copy, False),
                (T_ZB, 4, ACT.Silu, True), *[(T_G + 8 * n, 4, ACT.Sigmoid, True) for n in range(4)]]
        ROUNDS = TOPK // 8 // 8
        PICKS = [*range(2, QT), QT]
        ROWS_OF = lambda t: SMP if t == QT else P
        WIDTH_OF = lambda t: TOK if t == QT else (t + 1) * P

        A0 = H_HI
        k_t = at("k_t", [P, HA + KVB, TOK], F32, A0)
        VW = (HA + KVB) * HD
        v_tok = at("v_tok", [P, TT, VW], F32, A0 + 26112)
        q_tile = at("q_tile", [P, 2, GRP * HA + HB, P], F32, A0 + 53760)
        p_buf = at("p_buf", [P, 2, 15 * P], F32, A0 + 74240)
        p_t = at("p_t", [P, 2, SEQ], F32, A0 + 89600)
        o_tok = at("o_tok", [P, 2, (HA + HB) * HD], F32, A0 + 97792)
        o_t = at("o_t", [P, 2, HA + HB, P], F32, A0 + 110080)
        mask_b = at("mask_b", [P, 15 * P], BF16, A0 + 122368)
        keep_f = at("keep_f", [P, SEQ], F32, A0 + 126208)
        keep_b = at("keep_b", [P, 2, SEQ], BF16, A0 + 130304)
        mx = at("mx", [P, 96], F32, A0 + 134400)
        nmx = at("nmx", [P, 96], F32, A0 + 134784)
        lsum = at("lsum", [P, 96], F32, A0 + 135168)
        rinv = at("rinv", [P, 96], F32, A0 + 135552)
        v_t = at("v_t", [P, HA + KVB, TOK], F32, A0 + 135936)
        kiT = at("kiT", [ID, TOK], F32, A0 + 162048)
        k_tok = at("k_tok", [P, TT, VW], F32, A0 + 166400)
        ki_tok = at("ki_tok", [P, TT, ID], F32, A0 + 194048)
        mask_f = at("mask_f", [P, 15 * P], F32, A0 + 196352)

        kv_landed = sem("kv_landed")
        kv_turned = sem("kv_turned")
        kv_act = sem("kv_act")
        kv_dve = sem("kv_dve")
        kv_stored = sem("kv_stored")
        mask_cast = sem("mask_cast")
        q_landed = [sem(f"q_landed{i}") for i in range(2)]
        keep_landed = sem("keep_landed")
        keep_cast = sem("keep_cast")
        s_done = sem("s_done")
        mx_set = sem("mx_set")
        nmx_set = sem("nmx_set")
        exp_done = sem("exp_done")
        groups_added = sem("groups_added")
        rinv_set = sem("rinv_set")
        t_done = sem("t_done")
        t_out = sem("t_out")
        pv_done = sem("pv_done")
        o_out = sem("o_out")
        o_t_set = sem("o_t_set")
        att_stored = [sem(f"att_stored{i}") for i in range(2)]

        JOBS = []
        for i in range(QT):
            for a in range(HA):
                JOBS += [("A", i, a), ("B", i, 2 * a), ("B", i, 2 * a + 1)]
        NJ = len(JOBS)
        PER = HA + HB
        blocks_of = lambda n: JOBS[n][1] + 1
        SEG = lambda i: ((2, i + 1, 0), (1, min(5, i + 1), 8), (0, min(2, i + 1), 13))
        width_of = lambda n: (sum(s[1] for s in SEG(JOBS[n][1])) if JOBS[n][0] == "A" else JOBS[n][1] + 1) * P
        s_bank = lambda n: 0 if JOBS[n][0] == "A" else 4
        exps_before = lambda n, kind: max([m + 1 for m in range(n) if JOBS[m][0] == kind], default=0)
        a_jobs = lambda n: sum(JOBS[m][0] == "A" for m in range(n))
        T_BANK, O_BANK = 6, 7
        USES = []
        for n in range(NJ + 4):
            if 1 <= n <= NJ:
                USES.append(("w", n - 1, 0))
                if blocks_of(n - 1) > 4:
                    USES.append(("w", n - 1, 1))
            if n >= 3 and (n - 3) % PER == PER - 1:
                USES += [("o", (n - 3) // PER, g) for g in range(3)]
        use_no = {u: x for x, u in enumerate(USES)}

        def flat(bank, rows, width):
            return banks[0:rows, bank:bank + (width + 511) // 512, :].rearrange("p b n -> p (b n)")[:, 0:width]

        def sp_attention(sp):
            sp.wait_ge(chunk_done, 3 * N_PROJ)
            sp.wait_ge(col_stored[0], 16 * ((N_PROJ + 1) // 2))
            sp.wait_ge(col_stored[1], 16 * (N_PROJ // 2))
            sp.wait_ge(mask_stored, 16 * len(PICKS))
            proj = scr["proj"]
            tiles = lambda t, n: proj[t:t + n].rearrange("m p n -> p m n")
            sp.dma_start(k_t[:, 0:HA, :], tiles(T_KA, HA)).then_inc(kv_landed, 16)
            sp.dma_start(v_t[:, 0:HA, :], tiles(T_VA, HA)).then_inc(kv_landed, 16)
            sp.dma_start(k_t[:, HA:, :], tiles(T_KB, KVB)).then_inc(kv_landed, 16)
            sp.dma_start(v_t[:, HA:, :], tiles(T_VB, KVB)).then_inc(kv_landed, 16)
            sp.dma_start(kiT[:], proj[2, 0:ID, :]).then_inc(kv_landed, 16)
            sp.dma_start(mask_f[:], ins["mask_p"]).then_inc(kv_landed, 16)

            def store_outputs(i):
                sp.wait_ge(t_out, use_no["o", i, 2] + 1)
                sp.dma_start(scr["att"][:, :, i * P:(i + 1) * P].rearrange("m p n -> p m n"), o_t[:, i % 2])\
                    .then_inc(att_stored[i % 2], 16)

            for i in range(QT):
                need(sp, s_done, PER * (i - 1))
                for dst, first, n in ((0, T_QA, GRP * HA), (GRP * HA, T_QB, HB)):
                    sp.dma_start(q_tile[:, i % 2, dst:dst + n, :],
                                 proj[first:first + n, :, i * P:(i + 1) * P].rearrange("m p n -> p m n"))\
                        .then_inc(q_landed[i % 2], 16)
                if i >= 2:
                    need(sp, keep_cast, i - 2)
                    sp.dma_start(keep_f[:, 0:(i + 1) * P], scr["keep"][i - 2][:, 0:(i + 1) * P]).then_inc(keep_landed, 16)
                if i >= 2:
                    store_outputs(i - 2)
            store_outputs(QT - 2)
            store_outputs(QT - 1)
            sp_sample(sp)

        def act_attention(act):
            for t in range(TT):
                rows = ROWS_OF(t)
                act.wait_ge(kv_turned, t + 1)
                b0 = 4 * (t % 2)
                nc.scalar.copy(k_tok[0:rows, t, 0:HA * HD], banks[0:rows, b0, :]).then_inc(kv_act, 1)
                nc.scalar.copy(v_tok[0:rows, t, 0:HA * HD], banks[0:rows, b0 + 1, :]).then_inc(kv_act, 1)
            act.wait_ge(kv_act, 2 * TT)
            act.wait_ge(kv_dve, 3 * TT)
            for src, cols, big, small in ((k_tok, (0, 512), "win_k_prompt", "win_k_sample"),
                                          (v_tok, (0, 512), "win_v_prompt", "win_v_sample"),
                                          (k_tok, (512, 768), "k_prompt", "k_sample"),
                                          (v_tok, (512, 768), "v_prompt", "v_sample"),
                                          (ki_tok, (0, ID), "idx_k_prompt", "idx_k_sample")):
                a, b = cols
                act.dma_start(flat_rows(outs[big]).rearrange("(t p) n -> p t n", p=P), src[:, 0:QT, a:b])\
                    .then_inc(kv_stored, 16)
                act.dma_start(flat_rows(outs[small]), src[0:SMP, QT, a:b]).then_inc(kv_stored, 16)
            for n in range(NJ + 4):
                if n < NJ:
                    act.wait_ge(nmx_set, n + 1)
                    need(act, t_done, 0 if n < 2 else last_use(n - 2) + 1)
                    nc.scalar.activation(p_buf[:, n % 2, 0:width_of(n)], flat(s_bank(n), P, width_of(n)), ACT.Exp,
                                         bias=nmx[:, n:n + 1], scale=SCALE, accum_out=lsum[:, n:n + 1])\
                        .then_inc(exp_done, 1)
                if ("w", n - 1, 1) in use_no:
                    x = use_no["w", n - 1, 1]
                    act.wait_ge(t_done, x + 1)
                    nc.scalar.copy(p_t[:, (n - 1) % 2, 512:blocks_of(n - 1) * P],
                                   banks[:, T_BANK, 0:(blocks_of(n - 1) - 4) * P]).then_inc(t_out, 1)
            act_sample(act)

        def last_use(n):
            return use_no["w", n, 1] if blocks_of(n) > 4 else use_no["w", n, 0]

        def flat_rows(ap):
            return ap.rearrange("l b t n -> (l b t) n" if len(ap.shape) == 4 else "l b t h d -> (l b t) (h d)")

        def pool_attention(pool):
            def cast_keep(i):
                pool.wait_ge(keep_landed, 16 * (i - 1))
                need(pool, s_done, PER * (i - 1))
                nc.gpsimd.tensor_copy(keep_b[:, i % 2, 0:(i + 1) * P], keep_f[:, 0:(i + 1) * P]).then_inc(keep_cast, 1)

            pool.wait_ge(kv_landed, 6 * 16)
            nc.gpsimd.tensor_copy(mask_b[:], mask_f[:]).then_inc(mask_cast, 1)
            for n in range(NJ):
                kind, i, _ = JOBS[n]
                if n % PER == 0 and 2 <= i + 1 < QT:
                    cast_keep(i + 1)
                if kind == "A":
                    pool.wait_ge(exp_done, n + 1)
                    off = (i + 1) * P
                    for seg in SEG(i)[1:]:
                        w = seg[1] * P
                        dst = p_buf[:, n % 2, (i + 1) * P - w:(i + 1) * P]
                        nc.gpsimd.tensor_tensor(dst, dst, p_buf[:, n % 2, off:off + w], ALU.add)\
                            .then_inc(groups_added, 1)
                        off += w
                        pool.wait_ge(groups_added, 2 * a_jobs(n) + seg_no(seg))
            pool_sample(pool)

        def seg_no(seg):
            return 2 - seg[0]

        def dve_attention(dve):
            for t in range(TT):
                rows = ROWS_OF(t)
                dve.wait_ge(kv_turned, t + 1)
                b0 = 4 * (t % 2) + 2
                nc.vector.tensor_copy(k_tok[0:rows, t, 512:768], banks[0:rows, b0, 0:256]).then_inc(kv_dve, 1)
                nc.vector.tensor_copy(v_tok[0:rows, t, 512:768], banks[0:rows, b0, 256:512]).then_inc(kv_dve, 1)
                nc.vector.tensor_copy(ki_tok[0:rows, t, :], banks[0:rows, b0 + 1, 0:ID]).then_inc(kv_dve, 1)
            for n in range(NJ + 4):
                if n < NJ:
                    dve.wait_ge(s_done, n + 1)
                    nc.vector.tensor_reduce(mx[:, n:n + 1], flat(s_bank(n), P, width_of(n)), AX, ALU.max)\
                        .then_inc(mx_set, 1)
                    dve.wait_ge(mx_set, n + 1)
                    nc.vector.tensor_scalar(nmx[:, n:n + 1], mx[:, n:n + 1], -SCALE, None, ALU.mult).then_inc(nmx_set, 1)
                m = n - 1
                if 0 <= m < NJ:
                    dve.wait_ge(t_done, use_no["w", m, 0] + 1)
                    need(dve, pv_done, m - 1)
                    w = min(4, blocks_of(m)) * P
                    nc.vector.tensor_copy(p_t[:, m % 2, 0:w], banks[:, T_BANK, 0:w]).then_inc(t_out, 1)
                    dve.wait_ge(exp_done, m + 1)
                    nc.vector.reciprocal(rinv[:, m:m + 1], lsum[:, m:m + 1]).then_inc(rinv_set, 1)
                m = n - 2
                if 0 <= m < NJ:
                    kind, i, h = JOBS[m]
                    dve.wait_ge(pv_done, m + 1)
                    dve.wait_ge(rinv_set, m + 1)
                    need(dve, t_done, 0 if i < 2 else use_no["o", i - 2, 2] + 1)
                    c0 = (h if kind == "A" else HA + h) * HD
                    nc.vector.tensor_scalar(o_tok[:, i % 2, c0:c0 + HD], banks[:, O_BANK, 0:HD], rinv[:, m:m + 1],
                                            None, ALU.mult).then_inc(o_out, 1)
                if n >= 3 and (n - 3) % PER == PER - 1:
                    i = (n - 3) // PER
                    need(dve, att_stored[i % 2], 16 * (i // 2))
                    for g in range(3):
                        dve.wait_ge(t_done, use_no["o", i, g] + 1)
                        nc.vector.tensor_copy(o_t[:, i % 2, 4 * g:4 * g + 4, :],
                                              banks[:, T_BANK, :].rearrange("p (m n) -> p m n", m=4)).then_inc(t_out, 1)
            dve_sample(dve)

        def pe_attention(pe):
            pe.wait_ge(kv_landed, 6 * 16)
            pe.wait_ge(chunk_free, 3 * N_PROJ)
            for t in range(TT):
                rows = ROWS_OF(t)
                if t >= 2:
                    pe.wait_ge(kv_act, 2 * (t - 1))
                    pe.wait_ge(kv_dve, 3 * (t - 1))
                b0 = 4 * (t % 2)
                for bank, src, h0, n, c0 in ((0, k_t, 0, HA, 0), (1, v_t, 0, HA, 0), (2, k_t, HA, KVB, 0),
                                             (2, v_t, HA, KVB, 256)):
                    for h in range(n):
                        nc.tensor.transpose(banks[0:rows, b0 + bank, c0 + h * P:c0 + (h + 1) * P],
                                            src[:, h0 + h, t * P:t * P + rows], ident[:])
                nc.tensor.transpose(banks[0:rows, b0 + 3, 0:ID], kiT[:, t * P:t * P + rows], ident[0:ID, 0:ID])\
                    .then_inc(kv_turned, 1)
            pe.wait_ge(kv_act, 2 * TT)
            pe.wait_ge(kv_dve, 3 * TT)
            pe.wait_ge(mask_cast, 1)

            def pieces(start, width):
                a = start
                while a < start + width:
                    b = min(start + width, (a // 512 + 1) * 512)
                    yield a, b
                    a = b

            def scores(n):
                kind, i, h = JOBS[n]
                if n % PER == 0:
                    pe.wait_ge(q_landed[i % 2], 32 * (i // 2 + 1))
                    if i >= 2:
                        pe.wait_ge(keep_cast, i - 1)
                need(pe, exp_done, exps_before(n, kind))
                if kind == "A":
                    strips = [(q_tile[:, i % 2, g * HA + h, :], h, (i + 1 - nb) * P, nb * P,
                               mask_b[:, (m0 + (8, 5, 2)[2 - g] - nb) * P:(m0 + (8, 5, 2)[2 - g]) * P])
                              for g, nb, m0 in SEG(i)]
                else:
                    mask = keep_b[:, i % 2, 0:(i + 1) * P] if i >= 2 else None
                    strips = [(q_tile[:, i % 2, GRP * HA + h, :], HA + h // (HB // KVB), 0, (i + 1) * P, mask)]
                at_col = 0
                for lhs, kh, key0, width, mask in strips:
                    for a, b in pieces(at_col, width):
                        dst = banks[:, s_bank(n) + a // 512, a % 512:a % 512 + b - a]
                        nc.tensor.matmul(dst, lhs, k_t[:, kh, key0 + a - at_col:key0 + b - at_col], start=True,
                                         stop=False)
                        if mask is not None:
                            mm = nc.tensor.matmul(dst, identb[:], mask[:, a - at_col:b - at_col], start=False, stop=True)
                        else:
                            mm = nc.tensor.matmul(dst[:, width - P:width], identb[:], mask_b[:, 14 * P:15 * P],
                                                  start=False, stop=True)
                    at_col += width
                mm.then_inc(s_done, 1)

            def turn_weights(n, half):
                x = use_no["w", n, half]
                if JOBS[n][0] == "A":
                    pe.wait_ge(groups_added, 2 * a_jobs(n + 1))
                else:
                    pe.wait_ge(exp_done, n + 1)
                need(pe, t_out, x)
                for b in range(4 * half, min(4 * half + 4, blocks_of(n))):
                    tr = nc.tensor.transpose(banks[:, T_BANK, b % 4 * P:(b % 4 + 1) * P],
                                             p_buf[:, n % 2, b * P:(b + 1) * P], ident[:])
                tr.then_inc(t_done, 1)

            def values(n):
                kind, i, h = JOBS[n]
                pe.wait_ge(t_out, last_use(n) + 1)
                need(pe, o_out, n)
                c0 = h * HD if kind == "A" else (HA + h // (HB // KVB)) * HD
                for b in range(blocks_of(n)):
                    mm = nc.tensor.matmul(banks[:, O_BANK, 0:HD], p_t[:, n % 2, b * P:(b + 1) * P],
                                          v_tok[:, b, c0:c0 + HD], start=(b == 0), stop=(b == blocks_of(n) - 1))
                mm.then_inc(pv_done, 1)

            for n in range(NJ + 4):
                if n < NJ:
                    scores(n)
                if 1 <= n <= NJ:
                    turn_weights(n - 1, 0)
                if 2 <= n < NJ + 2:
                    values(n - 2)
                if ("w", n - 1, 1) in use_no:
                    turn_weights(n - 1, 1)
                if n >= 3 and (n - 3) % PER == PER - 1:
                    i = (n - 3) // PER
                    pe.wait_ge(o_out, PER * (i + 1))
                    for g in range(3):
                        need(pe, t_out, use_no["o", i, g])
                        for m in range(4 * g, 4 * g + 4):
                            tr = nc.tensor.transpose(banks[:, T_BANK, m % 4 * P:(m % 4 + 1) * P],
                                                     o_tok[:, i % 2, m * P:(m + 1) * P], ident[:])
                        tr.then_inc(t_done, 1)
            pe_sample(pe)

        S0 = A0 + 53760
        NK = PAST + SMP
        win_k = at("win_k", [P, 2, PAGES, HA * HD], F32, S0)
        win_v = at("win_v", [P, 2, PAGES, HA * HD], F32, S0 + 32768)
        pool_k = at("pool_k", [P, 2, PAGES, KVB * HD], F32, S0 + 65536)
        pool_v = at("pool_v", [P, 2, PAGES, KVB * HD], F32, S0 + 81920)
        kp_t = at("kp_t", [P, HA + KVB, PAST], F32, S0 + 98304)
        mask_sf = at("mask_sf", [96, PAST + NB * SMP], F32, S0 + 98304)
        rep_f = at("rep_f", [SMP, NB, SMP], F32, S0 + 104448)
        keep_sf = at("keep_sf", [SMP, NK], F32, S0 + 106496)
        q_s = at("q_s", [P, GRP * HA + HB, SMP], F32, S0 + 122880)
        qa_pad = at("qa_pad", [P, 2, HA, 96], F32, S0 + 128000)
        qb_own = at("qb_own", [P, 2, HB, NT], F32, S0 + 131072)
        pa_s = at("pa_s", [96, NK], F32, S0 + 131584)
        pb_s = at("pb_s", [SMP, NK], F32, S0 + 135936)
        pa_t = at("pa_t", [P, PAGES + 1, 32], F32, S0 + 140288)
        pb_t = at("pb_t", [P, PAGES + 1, SMP], F32, S0 + 141440)
        mask_sb = at("mask_sb", [96, PAST + NB * SMP], BF16, S0 + 143744)
        rep_b = at("rep_b", [SMP, NB, SMP], BF16, S0 + 146816)
        keep_sb = at("keep_sb", [SMP, NK], BF16, S0 + 147840)
        same = at("same", [96, 96], F32, S0 + 150016)
        o_s = at("o_s", [P, HA + HB, SMP], F32, S0 + 150400)
        maskn = at("maskn", [96, 2, SMP], BF16, S0 + 153472)
        rep_own = at("rep_own", [SMP, 2, SMP], BF16, S0 + 153728)
        row_s = at("row_s", [P, 16], F32, S0 + 153984)
        MXA, MXB, MX3, MXC, NMA, NMB, LA, LB, RA, RB = 0, 1, 2, 5, 6, 7, 8, 9, 10, 11

        smp_landed = sem("smp_landed")
        smp_cast = sem("smp_cast")
        raw_landed = [sem(f"raw_landed{i}") for i in range(2)]
        prep_set = sem("prep_set")
        st_done = sem("st_done")
        st_out = [sem(f"st_out{i}") for i in range(2)]
        sa_done = sem("sa_done")
        sb_done = sem("sb_done")
        sa_step = sem("sa_step")
        sb_step = sem("sb_step")
        nma_set = sem("nma_set")
        nmb_set = sem("nmb_set")
        ea_done = sem("ea_done")
        eb_done = sem("eb_done")
        la_sum = sem("la_sum")
        ra_set = sem("ra_set")
        rb_set = sem("rb_set")
        pa_set = sem("pa_set")
        pb_set = sem("pb_set")
        so_done = sem("so_done")
        so_out = sem("so_out")
        o_s_stored = sem("o_s_stored")
        RAW = 16 * (2 + 2 * PAGES)
        KU, SU = 12, 16

        def each_sequence(eng, body):
            body(0, 0, 0, False)
            with eng.Fori(0, NB // 2 - 1) as i:
                body(2 * i + 1, 1, i, False)
                body(2 * i + 2, 0, i + 1, False)
            body(NB - 1, 1, NB // 2 - 1, True)

        def sp_sample(sp):
            sp.wait_ge(o_out, NJ)
            sp.wait_ge(att_stored[0], 16 * QT // 2)
            sp.wait_ge(att_stored[1], 16 * QT // 2)
            sp.wait_ge(kv_stored, 16 * 10)
            proj = scr["proj"]
            for dst, first, n in ((0, T_QA, GRP * HA), (GRP * HA, T_QB, HB)):
                sp.dma_start(q_s[:, dst:dst + n, :], proj[first:first + n, :, SEQ:TOK].rearrange("m p n -> p m n"))\
                    .then_inc(smp_landed, 16)
            sp.dma_start(mask_sf[:], ins["mask_s"]).then_inc(smp_landed, 16)
            sp.dma_start(rep_f[:], ins["rep"]).then_inc(smp_landed, 16)
            sp.dma_start(keep_sf[:], scr["keep"][len(PICKS) - 1, 0:SMP, :]).then_inc(smp_landed, 16)
            sp.dma_start(same[:], ins["same"]).then_inc(smp_landed, 16)

            def load_sequence(b, par, half, last):
                if not isinstance(b, int) or b >= 2:
                    sp.wait_ge(so_done, b - 1)
                for dst, name in ((win_k, "cache_win_k"), (win_v, "cache_win_v")):
                    src = ins[name][0, bass.ds(b, 1)][0]
                    sp.dma_start(dst[:, par], src.rearrange("(c p) h d -> p c (h d)", p=P)).then_inc(raw_landed[par], 16)
                for j in range(PAGES):
                    page = sp.value_load(pages_n[0:1, bass.ds(b * PAGES + j, 1)], min_val=0, max_val=POOL_PAGES - 1)
                    for dst, name in ((pool_k, "cache_k"), (pool_v, "cache_v")):
                        src = ins[name][0, bass.ds(page, 1)][0]
                        sp.dma_start(dst[:, par, j, :], src.rearrange("p h d -> p (h d)")).then_inc(raw_landed[par], 16)

            load_sequence(0, 0, 0, False)
            load_sequence(1, 1, 0, False)
            with sp.Fori(1, NB // 2) as i:
                load_sequence(2 * i, 0, i, False)
                load_sequence(2 * i + 1, 1, i, False)
            sp.wait_ge(so_out, NB)
            sp.dma_start(scr["att"][:, :, SEQ:TOK].rearrange("m p n -> p m n"), o_s[:]).then_inc(o_s_stored, 16)
            sp_merge(sp)

        def pool_sample(pool):
            pool.wait_ge(smp_landed, 16 * 6)
            nc.gpsimd.memset(qa_pad[:], 0.0).then_inc(smp_cast, 1)
            nc.gpsimd.tensor_copy(mask_sb[:], mask_sf[:]).then_inc(smp_cast, 1)
            nc.gpsimd.tensor_copy(rep_b[:], rep_f[:]).then_inc(smp_cast, 1)
            nc.gpsimd.tensor_copy(keep_sb[:], keep_sf[:]).then_inc(smp_cast, 1)
            pool.wait_ge(smp_cast, 4)

            def prepare(b, par, half, last):
                if not isinstance(b, int) or b >= 2:
                    pool.wait_ge(sb_done, b - 1)
                t0 = b * NT
                by_group = q_s[:, 0:GRP * HA, :].rearrange("p (g h) n -> p g h n", g=GRP)
                for h in range(HA):
                    dst = qa_pad[:, par, h, :].rearrange("p (g r) -> p g r", g=GRP)[:, :, h * NT:(h + 1) * NT]
                    nc.gpsimd.tensor_copy(dst, by_group[:, :, h, bass.ds(t0, NT)]).then_inc(prep_set, 1)
                nc.gpsimd.tensor_copy(qb_own[:, par], q_s[:, GRP * HA:, bass.ds(t0, NT)]).then_inc(prep_set, 1)
                nc.gpsimd.tensor_copy(maskn[:, par, :], mask_sb[:, bass.ds(b * SMP + PAST, SMP)]).then_inc(prep_set, 1)
                nc.gpsimd.tensor_copy(rep_own[:, par, :],
                                      rep_b[:, bass.ds(b, 1), :].rearrange("p o n -> p (o n)")).then_inc(prep_set, 1)

            prepare(0, 0, 0, False)
            prepare(1, 1, 0, False)
            with pool.Fori(1, NB // 2) as i:
                prepare(2 * i, 0, i, False)
                prepare(2 * i + 1, 1, i, False)
            pool_merge(pool)

        def key_group(j):
            return j // 2, j % 2

        def act_sample(act):
            def keys_out(base):
                for j in range(1, KU, 2):
                    h, half = key_group(j)
                    act.wait_ge(st_done, base + j + 1)
                    nc.scalar.copy(kp_t[:, h, half * 512:(half + 1) * 512], banks[:, 7, :]).then_inc(st_out[1], 1)

            act.wait_ge(smp_cast, 4)
            keys_out(0)

            def body(b, par, half, last):
                act.wait_ge(nma_set, b + 1)
                if not isinstance(b, int) or b >= 1:
                    act.wait_ge(so_done, b)
                nc.scalar.activation(pa_s[:], flat(0, 96, NK), ACT.Exp, bias=row_s[0:96, NMA:NMA + 1], scale=SCALE,
                                     accum_out=row_s[0:96, LA:LA + 1]).then_inc(ea_done, 1)
                act.wait_ge(nmb_set, b + 1)
                nc.scalar.activation(pb_s[:], flat(3, SMP, NK), ACT.Exp, bias=row_s[0:SMP, NMB:NMB + 1], scale=SCALE,
                                     accum_out=row_s[0:SMP, LB:LB + 1]).then_inc(eb_done, 1)
                base = b * SU + KU
                if not last:
                    keys_out(base)
                else:
                    base = base - KU
                act.wait_ge(st_done, base + KU + 3)
                nc.scalar.copy(pb_t[:, 0:PAGES, :], banks[:, 6, :].rearrange("p (c r) -> p c r", c=PAGES))\
                    .then_inc(st_out[0], 1)
                act.wait_ge(st_done, base + KU + 4)
                nc.scalar.copy(pb_t[0:SMP, PAGES, :], banks[0:SMP, 7, 0:SMP]).then_inc(st_out[1], 1)

            each_sequence(act, body)
            act_merge(act)

        def dve_sample(dve):
            def keys_out(base):
                for j in range(0, KU, 2):
                    h, half = key_group(j)
                    dve.wait_ge(st_done, base + j + 1)
                    nc.vector.tensor_copy(kp_t[:, h, half * 512:(half + 1) * 512], banks[:, 6, :])\
                        .then_inc(st_out[0], 1)

            dve.wait_ge(smp_cast, 4)
            keys_out(0)

            def body(b, par, half, last):
                col1 = lambda c, r0=0, r1=96: row_s[r0:r1, c:c + 1]

                def link(ins_, sem_, per, k):
                    ins_.then_inc(sem_, 1)
                    dve.wait_ge(sem_, b * per + k)

                dve.wait_ge(sa_done, b + 1)
                link(nc.vector.tensor_reduce(col1(MXA), flat(0, 96, NK), AX, ALU.max), sa_step, 3, 1)
                for g in range(GRP):
                    last_i = nc.vector.tensor_copy(row_s[0:32, MX3 + g:MX3 + g + 1], col1(MXA, 32 * g, 32 * g + 32))
                link(last_i, sa_step, 3, 2)
                link(nc.vector.tensor_reduce(row_s[0:32, MXC:MXC + 1], row_s[0:32, MX3:MX3 + GRP], AX, ALU.max),
                     sa_step, 3, 3)
                for g in range(GRP):
                    last_i = nc.vector.tensor_scalar(col1(NMA, 32 * g, 32 * g + 32), row_s[0:32, MXC:MXC + 1], -SCALE,
                                                     None, ALU.mult)
                last_i.then_inc(nma_set, 1)
                dve.wait_ge(sb_done, b + 1)
                link(nc.vector.tensor_reduce(col1(MXB, 0, SMP), flat(3, SMP, NK), AX, ALU.max), sb_step, 1, 1)
                nc.vector.tensor_scalar(col1(NMB, 0, SMP), col1(MXB, 0, SMP), -SCALE, None, ALU.mult)\
                    .then_inc(nmb_set, 1)
                base = b * SU + KU
                if not last:
                    keys_out(base)
                else:
                    base = base - KU
                dve.wait_ge(la_sum, b + 1)
                nc.vector.reciprocal(col1(RA), banks[0:96, 2, 256:257]).then_inc(ra_set, 1)
                dve.wait_ge(ra_set, b + 1)
                nc.vector.tensor_scalar(pa_s[:], pa_s[:], col1(RA), None, ALU.mult).then_inc(pa_set, 1)
                dve.wait_ge(eb_done, b + 1)
                nc.vector.reciprocal(col1(RB, 0, SMP), col1(LB, 0, SMP)).then_inc(rb_set, 1)
                dve.wait_ge(rb_set, b + 1)
                nc.vector.tensor_scalar(pb_s[:], pb_s[:], col1(RB, 0, SMP), None, ALU.mult).then_inc(pb_set, 1)
                by_group = lambda rows, bank, a, c: banks[0:rows, bank, a:a + 96 * c].rearrange(
                    "p (c g r) -> p c r g", c=c, g=GRP)
                dve.wait_ge(st_done, base + KU + 1)
                nc.vector.tensor_reduce(pa_t[:, 0:5, :], by_group(P, 6, 0, 5), AX, ALU.add).then_inc(st_out[0], 1)
                dve.wait_ge(st_done, base + KU + 2)
                nc.vector.tensor_reduce(pa_t[:, 5:8, :], by_group(P, 7, 0, 3), AX, ALU.add)
                nc.vector.tensor_reduce(pa_t[0:SMP, 8:9, :], by_group(SMP, 7, 288, 1), AX, ALU.add)\
                    .then_inc(st_out[1], 1)
                dve.wait_ge(so_done, b + 1)
                nc.vector.tensor_copy(o_s[:, :, bass.ds(b * NT, NT)],
                                      banks[:, 2, 128:224].rearrange("p (m n) -> p m n", n=NT)).then_inc(so_out, 1)

            each_sequence(dve, body)
            dve_merge(dve)

        def pe_sample(pe):
            def turn_keys(base, earlier, par):
                for j in range(KU):
                    h, half = key_group(j)
                    if not isinstance(earlier, int) or earlier + j // 2 > 0:
                        pe.wait_ge(st_out[j % 2], earlier + j // 2)
                    src = win_k[:, par] if h < HA else pool_k[:, par]
                    c0 = (h if h < HA else h - HA) * HD
                    for q in range(4):
                        tr = nc.tensor.transpose(banks[:, 6 + j % 2, q * P:(q + 1) * P],
                                                 src[:, 4 * half + q, c0:c0 + HD], ident[:])
                    tr.then_inc(st_done, 1)

            pe.wait_ge(smp_cast, 4)
            pe.wait_ge(t_out, len(USES))
            pe.wait_ge(raw_landed[0], RAW)
            turn_keys(0, 0, 0)

            def strips():
                return (0, 512, 0), (512, 1024, 1), (1024, NK, 2)

            def body(b, par, half, last):
                pe.wait_ge(prep_set, 7 * b + 7)
                earlier = b * (SU // 2) + KU // 2
                pe.wait_ge(st_out[0], earlier)
                pe.wait_ge(st_out[1], earlier)
                if not isinstance(b, int) or b >= 1:
                    pe.wait_ge(so_out, b)
                    pe.wait_ge(eb_done, b)
                for a, z, bank in strips():
                    dst = banks[0:96, bank, 0:z - a]
                    for h in range(HA):
                        keys = kp_t[:, h, a:z] if a < PAST else k_t[:, h, SEQ:TOK]
                        nc.tensor.matmul(dst, qa_pad[:, par, h, :], keys, start=(h == 0), stop=False)
                    mask = mask_sb[:, a:z] if a < PAST else maskn[:, par, :]
                    mm = nc.tensor.matmul(dst, identb[0:96, 0:96], mask, start=False, stop=True)
                mm.then_inc(sa_done, 1)
                for a, z, bank in strips():
                    for kv in range(KVB):
                        keys = kp_t[:, HA + kv, a:z] if a < PAST else k_t[:, HA + kv, SEQ:TOK]
                        nc.tensor.matmul(banks[32 * kv:32 * kv + 32, 3 + bank, 0:z - a],
                                         qb_own[:, par, 4 * kv:4 * kv + 4, :].rearrange("p h t -> p (h t)"), keys,
                                         start=True, stop=False, skip_group_check=True)
                    mm = nc.tensor.matmul(banks[0:SMP, 3 + bank, 0:z - a], rep_own[:, par, :], keep_sb[:, a:z],
                                          start=False, stop=True, skip_group_check=True)
                mm.then_inc(sb_done, 1)
                if not last:
                    pe.wait_ge(raw_landed[1 - par], (half + (1 + par)) * RAW)
                    turn_keys(b * SU + KU, earlier, 1 - par)
                    used = KU // 2
                else:
                    used = 0
                pe.wait_ge(ea_done, b + 1)
                nc.tensor.matmul(banks[0:96, 2, 256:257], same[:], row_s[0:96, LA:LA + 1], start=True, stop=True)\
                    .then_inc(la_sum, 1)
                pe.wait_ge(pa_set, b + 1)
                for x, tiles in ((0, range(0, 5)), (1, range(5, 9))):
                    pe.wait_ge(st_out[x], earlier + used)
                    for c in tiles:
                        n = min(P, NK - c * P)
                        tr = nc.tensor.transpose(banks[0:n, 6 + x, (c - tiles[0]) * 96:(c - tiles[0] + 1) * 96],
                                                 pa_s[:, c * P:c * P + n], ident[0:96, 0:96])
                    tr.then_inc(st_done, 1)
                pe.wait_ge(st_out[0], earlier + used + 1)
                pe.wait_ge(st_out[1], earlier + used + 1)
                pe.wait_ge(pb_set, b + 1)
                for h in range(HA):
                    dst = banks[:, 2, 128 + h * NT:128 + (h + 1) * NT]
                    for c in range(PAGES + 1):
                        v = win_v[:, par, c, h * HD:(h + 1) * HD] if c < PAGES else v_tok[0:SMP, QT, h * HD:(h + 1) * HD]
                        w = pa_t[0:P if c < PAGES else SMP, c, h * NT:(h + 1) * NT]
                        nc.tensor.matmul(dst, v, w, start=(c == 0), stop=(c == PAGES))
                for x, tiles in ((0, range(0, 8)), (1, range(8, 9))):
                    for c in tiles:
                        n = min(P, NK - c * P)
                        tr = nc.tensor.transpose(banks[0:n, 6 + x, (c - tiles[0]) * SMP:(c - tiles[0] + 1) * SMP],
                                                 pb_s[:, c * P:c * P + n], ident[0:SMP, 0:SMP])
                    tr.then_inc(st_done, 1)
                pe.wait_ge(st_out[0], earlier + used + 2)
                pe.wait_ge(st_out[1], earlier + used + 2)
                for kv in range(KVB):
                    dst = banks[:, 2, 160 + kv * 32:160 + (kv + 1) * 32]
                    c0 = (HA + kv) * HD
                    for c in range(PAGES + 1):
                        v = pool_v[:, par, c, kv * HD:(kv + 1) * HD] if c < PAGES else v_tok[0:SMP, QT, c0:c0 + HD]
                        w = pb_t[0:P if c < PAGES else SMP, c, kv * 32:(kv + 1) * 32]
                        mm = nc.tensor.matmul(dst, v, w, start=(c == 0), stop=(c == PAGES))
                mm.then_inc(so_done, 1)

            each_sequence(pe, body)
            pe_merge(pe)

        KA, KB_ = HA, HB
        KO = KA + KB_
        o_hi = at("o_hi", [P, KO, TOK], F32R, A0)
        o_lo = at("o_lo", [P, KO, TOK], F32R, A0 + 52224)
        o_in = at("o_in", [P, 2, TOK], F32, A0 + 104448)
        z_in = at("z_in", [P, 2, TOK], F32, A0 + 113152)
        og = at("og", [P, 2, TOK], F32, A0 + 121856)
        ua_g = at("ua_g", [P, 2, 384], F32, A0 + 130560)
        ub_g = at("ub_g", [P, 2, 384], F32, A0 + 133632)
        gates = at("gates", [P, 2, 2, TOK], F32, W0 + 40960)
        merged = at("merged", [P, 2, TOK], F32, W0 + 58368)
        m_in = at("m_in", [P, 2, TOK], F32, W0 + 40960)
        r_col = at("r_col", [P, 2, TOK], F32, W0 + 49664)
        r_tok = at("r_tok", [P, 2, TT, P], F32, W0 + 58368)
        r_row = at("r_row", [P, 2, D], F32, A0)
        x_row = at("x_row", [P, 2, D], F32, A0 + 16384)
        y_row = at("y_row", [P, 2, D], F32, A0 + 32768)
        y_sq = at("y_sq", [P, D], F32, A0 + 49152)
        g_row = at("g_row", [P, D], F32, A0 + 57344)

        oz_landed = [sem(f"oz_landed{i}") for i in range(2)]
        og_set = sem("og_set")
        o_hi_set = sem("o_hi_set")
        o_lo_set = sem("o_lo_set")
        u_landed = sem("u_landed")
        u_hi_set = sem("u_hi_set")
        u_lo_set = sem("u_lo_set")
        gate_landed = [sem(f"gate_landed{i}") for i in range(2)]
        u_done = sem("u_done")
        u_out = sem("u_out")
        m_set = sem("m_set")
        m_stored = [sem(f"m_stored{i}") for i in range(2)]
        m_landed = [sem(f"m_landed{i}") for i in range(2)]
        m_hi_set = sem("m_hi_set")
        m_lo_set = sem("m_lo_set")
        v_landed = sem("v_landed")
        v_hi_set = sem("v_hi_set")
        v_lo_set = sem("v_lo_set")
        y_done = sem("y_done")
        y_out = sem("y_out")
        r_set = sem("r_set")
        r_turned = sem("r_turned")
        r_copied = sem("r_copied")
        r_stored = [sem(f"r_stored{i}") for i in range(2)]
        row_landed = [sem(f"row_landed{i}") for i in range(2)]
        g_landed = sem("g_landed")
        y_sum = sem("y_sum")
        y_ssum = sem("y_ssum")
        y_root = sem("y_root")
        y_rstd = sem("y_rstd")
        y_norm = sem("y_norm")
        y_stored = [sem(f"y_stored{i}") for i in range(2)]

        def column_tiles(eng, body):
            body(0, 0, 0)
            body(1, 1, 0)
            with eng.Fori(1, KT // 2) as i:
                body(2 * i, 0, i)
                body(2 * i + 1, 1, i)

        w_pa, w_pb, w_out = ins["w_pa"][0], ins["w_pb"][0], ins["w_out"][0]
        y_tiles = [(outs["y_prompt"][0, t * P:(t + 1) * P, :], P) for t in range(QT)]
        y_tiles.append((outs["y_sample"].rearrange("b t d -> (b t) d"), SMP))

        def sp_merge(sp):
            sp.wait_ge(o_s_stored, 16)
            for k in range(KO):
                need(sp, og_set, k - 1)
                z = T_ZA + k if k < KA else T_ZB + k - KA
                sp.dma_start(o_in[:, k % 2, :], scr["att"][k]).then_inc(oz_landed[k % 2], 16)
                sp.dma_start(z_in[:, k % 2, :], scr["proj"][z]).then_inc(oz_landed[k % 2], 16)

            def load_merge(c, par, half):
                cols = bass.ds(c * P, P)
                need(sp, u_lo_set, c)
                sp.dma_start(w_raw[:, 0:KA, :], w_pa[:, cols].rearrange("(k p) n -> p k n", p=P)).then_inc(u_landed, 16)
                sp.dma_start(w_raw[:, KA:KO, :], w_pb[:, cols].rearrange("(k p) n -> p k n", p=P)).then_inc(u_landed, 16)
                need(sp, m_set, (c - 1) * 3)
                for x in range(2):
                    sp.dma_start(gates[:, par, x, :], scr["proj"][bass.ds(c + (T_G + x * KT), 1)][0])\
                        .then_inc(gate_landed[par], 16)

            column_tiles(sp, load_merge)
            sp.wait_ge(u_done, 3 * KT)
            sp.wait_ge(m_set, 3 * KT)
            for i in range(2):
                sp.wait_ge(m_stored[i], 16 * KT // 2)
            sp.dma_start(w_raw[:], w_out[:, 0:P].rearrange("(k p) n -> p k n", p=P)).then_inc(v_landed, 16)
            for k in range(KT):
                need(sp, m_lo_set, k - 1)
                sp.dma_start(m_in[:, k % 2, :], scr["merged"][k]).then_inc(m_landed[k % 2], 16)

            with sp.Fori(1, KT) as c:
                sp.wait_ge(v_lo_set, c)
                sp.dma_start(w_raw[:], w_out[:, bass.ds(c * P, P)].rearrange("(k p) n -> p k n", p=P))\
                    .then_inc(v_landed, 16)
            sp.wait_ge(y_done, 3 * KT)
            sp.dma_start(g_row[:], ins["g_final"].rearrange("(o n) -> o n", o=1).to_broadcast([P, D])).then_inc(g_landed, 16)
            for i in range(2):
                sp.wait_ge(r_stored[i], 32 * (KT // 2))
            for t in range(TT):
                rows = ROWS_OF(t)
                need(sp, y_sum, t - 1)
                sp.dma_start(r_row[0:rows, t % 2, :], scr["resid"][t * P:t * P + rows, :]).then_inc(row_landed[t % 2], 16)
                sp.dma_start(x_row[0:rows, t % 2, :], x_tiles[t][0]).then_inc(row_landed[t % 2], 16)

        def pool_merge(pool):
            def store_merged(c, par, half):
                pool.wait_ge(m_set, 3 * c + 3)
                pool.dma_start(scr["merged"][bass.ds(c, 1)][0], merged[:, par, :]).then_inc(m_stored[par], 16)

            column_tiles(pool, store_merged)

            def store_resid(c, par, half):
                pool.wait_ge(r_copied, 3 * c + 3)
                cols = bass.ds(c * P, P)
                pool.dma_start(scr["resid"][0:SEQ, cols].rearrange("(t p) n -> p t n", p=P), r_tok[:, par, 0:QT, :])\
                    .then_inc(r_stored[par], 16)
                pool.dma_start(scr["resid"][SEQ:TOK, cols], r_tok[0:SMP, par, QT, :]).then_inc(r_stored[par], 16)

            column_tiles(pool, store_resid)
            for t in range(TT):
                rows = ROWS_OF(t)
                pool.wait_ge(y_norm, t + 1)
                pool.dma_start(y_tiles[t][0], y_row[0:rows, t % 2, :]).then_inc(y_stored[t % 2], 16)
            pool.wait_ge(y_stored[0], 16 * ((TT + 1) // 2))
            pool.wait_ge(y_stored[1], 16 * (TT // 2))
            pool.wait_ge(kv_stored, 16 * 10)

        def act_merge(act):
            for k in range(KO):
                act.wait_ge(og_set, k + 1)
                nc.scalar.copy(o_hi[:, k, :], og[:, k % 2, :]).then_inc(o_hi_set, 1)

            def split_merge(c, par, half):
                act.wait_ge(u_landed, 32 * c + 32)
                need(act, u_done, (c - 1) * 3)
                nc.scalar.copy(w_hi[:, par, 0:KO, :], w_raw[:, 0:KO, :]).then_inc(u_hi_set, 1)

            column_tiles(act, split_merge)
            for k in range(KT):
                act.wait_ge(m_landed[k % 2], 16 * (k // 2 + 1))
                nc.scalar.copy(h_hi[:, k, :], m_in[:, k % 2, :]).then_inc(m_hi_set, 1)
            act.wait_ge(v_landed, 16)
            nc.scalar.copy(w_hi[:, 0], w_raw[:]).then_inc(v_hi_set, 1)

            def turned_out(c, par, half):
                if not isinstance(c, int) or c >= 2:
                    act.wait_ge(r_stored[par], half * 32)
                for x in range(3):
                    act.wait_ge(r_turned, 3 * c + (x + 1))
                    rows, n = (P, 4) if x < 2 else (SMP, 1)
                    nc.scalar.copy(r_tok[0:rows, par, 4 * x:4 * x + n, :],
                                   banks[0:rows, 3 + x, 0:n * P].rearrange("p (t n) -> p t n", n=P)).then_inc(r_copied, 1)

            def split_out(c, par):
                act.wait_ge(v_landed, c * 16 + 16)
                need(act, y_done, (c - 1) * 3)
                nc.scalar.copy(w_hi[:, par], w_raw[:]).then_inc(v_hi_set, 1)

            def out_step(c, par, half):
                split_out(c + 1, 1 - par)
                turned_out(c, par, half)

            out_step(0, 0, 0)
            out_step(1, 1, 0)
            with act.Fori(1, KT // 2 - 1) as i:
                out_step(2 * i, 0, i)
                out_step(2 * i + 1, 1, i)
            out_step(KT - 2, 0, KT // 2 - 1)
            turned_out(KT - 1, 1, KT // 2 - 1)
            for t in range(TT):
                rows = ROWS_OF(t)
                act.wait_ge(y_sum, t + 1)
                nc.scalar.activation(y_sq[0:rows, :], y_row[0:rows, t % 2, :], ACT.Square,
                                     accum_out=ssum[0:rows, t:t + 1]).then_inc(y_ssum, 1)
                act.wait_ge(y_ssum, t + 1)
                nc.scalar.activation(rstd[0:rows, t:t + 1], ssum[0:rows, t:t + 1], ACT.Sqrt, bias=epst[0:rows, :],
                                     scale=1.0 / D).then_inc(y_root, 1)

        def dve_merge(dve):
            for k in range(KO + 1):
                if k < KO:
                    dve.wait_ge(oz_landed[k % 2], 32 * (k // 2 + 1))
                    need(dve, o_lo_set, k - 1)
                    nc.vector.tensor_tensor(og[:, k % 2, :], o_in[:, k % 2, :], z_in[:, k % 2, :], ALU.mult)\
                        .then_inc(og_set, 1)
                if k >= 1:
                    dve.wait_ge(o_hi_set, k)
                    nc.vector.tensor_tensor(o_lo[:, k - 1, :], og[:, (k - 1) % 2, :], o_hi[:, k - 1, :], ALU.subtract)\
                        .then_inc(o_lo_set, 1)

            def split_merge(c, par):
                dve.wait_ge(u_hi_set, c + 1)
                nc.vector.tensor_tensor(w_lo[:, par, 0:KO, :], w_raw[:, 0:KO, :], w_hi[:, par, 0:KO, :], ALU.subtract)\
                    .then_inc(u_lo_set, 1)

            def merge(c, par, half):
                dve.wait_ge(gate_landed[par], half * 32 + 32)
                if not isinstance(c, int) or c >= 2:
                    dve.wait_ge(m_stored[par], half * 16)
                for x, (a, b) in enumerate(CHUNKS):
                    n, s = b - a, (par + x) % 2
                    dve.wait_ge(u_done, 3 * c + (x + 1))
                    need(dve, m_set, 3 * c + (x - 1))
                    nc.vector.tensor_tensor(ua_g[:, s, 0:n], banks[:, x, 0:n], gates[:, par, 0, a:b], ALU.mult)
                    nc.vector.tensor_tensor(ub_g[:, s, 0:n], banks[:, 3 + x, 0:n], gates[:, par, 1, a:b], ALU.mult)\
                        .then_inc(u_out, 1)
                    dve.wait_ge(u_out, 3 * c + (x + 1))
                    nc.vector.tensor_tensor(merged[:, par, a:b], ua_g[:, s, 0:n], ub_g[:, s, 0:n], ALU.add)\
                        .then_inc(m_set, 1)

            def merge_step(c, par, half):
                split_merge(c + 1, 1 - par)
                merge(c, par, half)

            split_merge(0, 0)
            merge_step(0, 0, 0)
            merge_step(1, 1, 0)
            with dve.Fori(1, KT // 2 - 1) as i:
                merge_step(2 * i, 0, i)
                merge_step(2 * i + 1, 1, i)
            merge_step(KT - 2, 0, KT // 2 - 1)
            merge(KT - 1, 1, KT // 2 - 1)
            for k in range(KT):
                dve.wait_ge(m_hi_set, k + 1)
                nc.vector.tensor_tensor(h_lo[:, k, :], m_in[:, k % 2, :], h_hi[:, k, :], ALU.subtract)\
                    .then_inc(m_lo_set, 1)

            def split_out(c, par):
                dve.wait_ge(v_hi_set, c + 1)
                nc.vector.tensor_tensor(w_lo[:, par], w_raw[:], w_hi[:, par], ALU.subtract).then_inc(v_lo_set, 1)

            def gated(c, par, half):
                need(dve, r_turned, 3 * (c - 1))
                for x, (a, b) in enumerate(CHUNKS):
                    dve.wait_ge(y_done, 3 * c + (x + 1))
                    z = min(b, SEQ)
                    gate = mod_t[:, bass.ds(c + 2 * KT, 1), :].rearrange("p o n -> p (o n)")
                    if x == 2:
                        nc.vector.tensor_tensor(
                            r_col[:, par, SEQ:TOK].rearrange("p (b t) -> p b t", b=NB),
                            banks[:, x, SEQ - a:TOK - a].rearrange("p (b t) -> p b t", b=NB),
                            gate[:, 0:NB, None].to_broadcast([P, NB, NT]), ALU.mult)
                    last = nc.vector.tensor_scalar(r_col[:, par, a:z], banks[:, x, 0:z - a], gate[:, 8:9], None,
                                                   ALU.mult)
                    last.then_inc(y_out, 1)
                    if x == 2:
                        dve.wait_ge(y_out, 3 * c + 3)

            def out_step(c, par, half):
                split_out(c + 1, 1 - par)
                gated(c, par, half)

            split_out(0, 0)
            out_step(0, 0, 0)
            out_step(1, 1, 0)
            with dve.Fori(1, KT // 2 - 1) as i:
                out_step(2 * i, 0, i)
                out_step(2 * i + 1, 1, i)
            out_step(KT - 2, 0, KT // 2 - 1)
            gated(KT - 1, 1, KT // 2 - 1)
            dve.wait_ge(g_landed, 16)

            def add_rows(t):
                rows = ROWS_OF(t)
                dve.wait_ge(row_landed[t % 2], 32 * (t // 2 + 1))
                need(dve, y_stored[t % 2], 16 * (t // 2))
                nc.vector.tensor_tensor(y_row[0:rows, t % 2, :], r_row[0:rows, t % 2, :], x_row[0:rows, t % 2, :],
                                        ALU.add).then_inc(y_sum, 1)

            add_rows(0)
            for t in range(TT):
                rows = ROWS_OF(t)
                if t + 1 < TT:
                    add_rows(t + 1)
                dve.wait_ge(y_root, t + 1)
                nc.vector.reciprocal(rstd[0:rows, t:t + 1], rstd[0:rows, t:t + 1]).then_inc(y_rstd, 1)
                dve.wait_ge(y_rstd, t + 1)
                nc.vector.scalar_tensor_tensor(out=y_row[0:rows, t % 2, :], in0=y_row[0:rows, t % 2, :],
                                               scalar=rstd[0:rows, t:t + 1], in1=g_row[0:rows, :], op0=ALU.mult,
                                               op1=ALU.mult).then_inc(y_norm, 1)

        def pe_merge(pe):
            def three_passes(dst, par, ks, a, b, hi, lo):
                for k in ks:
                    nc.tensor.matmul(dst, w_hi[:, par, k, :], hi[:, k, a:b], start=(k == ks[0]), stop=False)
                    nc.tensor.matmul(dst, w_hi[:, par, k, :], lo[:, k, a:b], start=False, stop=False)
                    mm = nc.tensor.matmul(dst, w_lo[:, par, k, :], hi[:, k, a:b], start=False, stop=(k == ks[-1]))
                return mm

            pe.wait_ge(o_lo_set, KO)
            pe.wait_ge(so_out, NB)

            def merge(c, par, half):
                pe.wait_ge(u_lo_set, c + 1)
                for x, (a, b) in enumerate(CHUNKS):
                    need(pe, u_out, 3 * c + (x - 2))
                    three_passes(banks[:, x, 0:b - a], par, range(KA), a, b, o_hi, o_lo)
                    three_passes(banks[:, 3 + x, 0:b - a], par, range(KA, KO), a, b, o_hi, o_lo).then_inc(u_done, 1)

            column_tiles(pe, merge)
            pe.wait_ge(m_lo_set, KT)

            def project(c, par):
                pe.wait_ge(v_lo_set, c + 1)
                for x, (a, b) in enumerate(CHUNKS):
                    need(pe, y_out, 3 * c + (x - 2))
                    three_passes(banks[:, x, 0:b - a], par, range(KT), a, b, h_hi, h_lo).then_inc(y_done, 1)

            def turn(c, par):
                pe.wait_ge(y_out, 3 * c + 3)
                need(pe, r_copied, 3 * c)
                for x in range(3):
                    for t in range(4 * x, min(4 * x + 4, TT)):
                        rows = ROWS_OF(t)
                        tr = nc.tensor.transpose(banks[0:rows, 3 + x, (t % 4) * P:(t % 4 + 1) * P],
                                                 r_col[:, par, t * P:t * P + rows], ident[:])
                    tr.then_inc(r_turned, 1)

            pe.wait_ge(u_out, 3 * KT)
            project(0, 0)
            project(1, 1)
            turn(0, 0)
            with pe.Fori(1, KT // 2) as i:
                project(2 * i, 0)
                turn(2 * i - 1, 1)
                project(2 * i + 1, 1)
                turn(2 * i, 0)
            turn(KT - 1, 1)

        block = ctx.enter_context(nc.Block())

        def pick_round(dve):
            nc.vector.max(best8[:], work[:])
            dve.drain()
            nc.vector.match_replace(work[:], best8[:], work[:], TAKEN)
            dve.drain()

        def picked(dve, picks):
            nc.vector.tensor_scalar(work[:], work[:], TAKEN, None, ALU.not_equal).then_inc(mask_picked, 1)
            dve.wait_ge(mask_picked, 2 * picks - 1)
            nc.vector.tensor_scalar(work[:], work[:], -BIG, None, ALU.mult).then_inc(mask_picked, 1)

        def index_scores(dve):
            dve.wait_ge(chunk_done, 3 * N_IDX)
            dve.wait_ge(rot_set, 3 * N_IDX)
            dve.wait_ge(col_stored[0], 32)
            dve.wait_ge(col_stored[1], 16)
            nc.vector.memset(ki_hi[ID:P, :], 0.0)
            nc.vector.memset(ki_lo[0:ID, :], 0.0)
            nc.vector.memset(qi_pair[:], 0.0).then_inc(idx_zeroed, 1)
            dve.wait_ge(idx_zeroed, 1)
            dve.wait_ge(idx_landed, 6 * 16)
            for h in range(IH):
                src = qi_t[ID * (h % 2):ID * (h % 2) + ID, h // 2, SEQ:TOK].rearrange(
                    "p (j b t) -> p j b t", b=2, t=NT)
                for b in range(2):
                    for j in range(NB // 2):
                        c0 = (2 * j + b) * NT
                        last = nc.vector.tensor_copy(qi_pair[ID * b:ID * b + ID, h, j, c0:c0 + NT], src[:, j, b, :])
            last.then_inc(idx_pair_set, 1)
            dve.wait_ge(idx_turned, 1)
            nc.vector.tensor_copy(wi_tok[:], banks[:, 6, 0:TT * IH].rearrange("p (t h) -> p t h", h=IH))\
                .then_inc(idx_pair_set, 1)
            dve.wait_ge(idx_pair_set, 2)
            dve.wait_ge(idx_copied, 8)
            n = 0
            for j, t in enumerate(PICKS):
                rows, width = ROWS_OF(t), WIDTH_OF(t)
                need(dve, acc_stored[j % 2], 16 * (j // 2))
                nc.vector.memset(acc[:, j % 2, :], -BIG).then_inc(acc_fill, 1)
                dve.wait_ge(acc_fill, j + 1)
                out = acc[0:rows, j % 2, 0:width]
                for h in range(IH):
                    dve.wait_ge(relu_set, n + 1)
                    need(dve, acc_step, n)
                    if h == 0:
                        nc.vector.tensor_scalar(out, relu_s[0:rows, n % 2, 0:width], wi_tok[0:rows, t, h:h + 1], None,
                                                ALU.mult).then_inc(acc_step, 1)
                    else:
                        nc.vector.scalar_tensor_tensor(out=out, in0=relu_s[0:rows, n % 2, 0:width],
                                                       scalar=wi_tok[0:rows, t, h:h + 1], in1=out, op0=ALU.mult,
                                                       op1=ALU.add).then_inc(acc_step, 1)
                    n += 1
                tail = acc[0:rows, j % 2, width - rows:width]
                dve.wait_ge(acc_step, n)
                nc.vector.tensor_tensor(tail, tail, mask_i[:] if t == QT else diag[:], ALU.add).then_inc(acc_set, 1)

        @block.sync
        def _(sp):
            sp.dma_start(c_rows[0:8, :], ins["c_sample"]).then_inc(small_in, 16)
            sp.dma_start(c_rows[8:9, :], ins["c_prompt"]).then_inc(small_in, 16)
            sp.dma_start(bada_r[:], ins["b_ada"][0].rearrange("(k p) -> k p", p=P)).then_inc(small_in, 16)
            sp.dma_start(gn_r[:], ins["g_norm"][0].rearrange("(k p) -> k p", p=P)).then_inc(small_in, 16)
            sp.dma_start(pages_n[:], ins["page_table"].rearrange("(o b) n -> o (b n)", o=1)).then_inc(small_in, 16)
            for t, (src, rows) in enumerate(x_tiles):
                need(sp, x_turned_bank, 4 * (t - 1))
                sp.dma_start(x_in[0:rows, t % 2, :], src).then_inc(x_landed[t % 2], 16)
                if t < 2:
                    sp.dma_start(ada_w[:, t], w_ada[:, t * ADA_C:(t + 1) * ADA_C].rearrange(
                        "(k p) n -> p k n", p=P)).then_inc(ada_landed[t], 16)
            sp.dma_start(rot_cos[:], ins["rot"][2]).then_inc(rot_ready, 16)
            sp.dma_start(rot_sin[:], ins["rot"][3]).then_inc(rot_ready, 16)
            with sp.Fori(1, ADA_N // 2) as i:
                for u in range(2):
                    sp.wait_ge(ada_used, 2 * i + u - 1)
                    sp.dma_start(ada_w[:, u], w_ada[:, bass.ds(i * (2 * ADA_C) + u * ADA_C, ADA_C)].rearrange(
                        "(k p) n -> p k n", p=P)).then_inc(ada_landed[u], 16)
            for t, (src, width) in enumerate(IDX_SRC):
                load_tile(sp, t, src, width)
            sp.wait_ge(chunk_done, 3 * N_IDX)
            sp.wait_ge(rot_set, 3 * N_IDX)
            sp.wait_ge(col_stored[0], 32)
            sp.wait_ge(col_stored[1], 16)
            sp.dma_start(qi_t[:], scr["proj"][0:2].rearrange("m p n -> p m n")).then_inc(idx_landed, 16)
            sp.dma_start(ki_hi[0:ID, :], scr["proj"][2, 0:ID, :]).then_inc(idx_landed, 16)
            sp.dma_start(ki_lo[ID:P, :], scr["proj"][2, 0:ID, :]).then_inc(idx_landed, 16)
            sp.dma_start(wi_r[:], scr["proj"][2, ID:ID + IH, :]).then_inc(idx_landed, 16)
            sp.dma_start(diag[:], ins["mask_p"][:, 14 * P:15 * P]).then_inc(idx_landed, 16)
            sp.dma_start(mask_i[:], ins["mask_i"]).then_inc(idx_landed, 16)
            sp.wait_ge(small_in, 80)
            for b in range(NB):
                with sp.Fori(0, PAGES) as j:
                    page = sp.value_load(pages_n[0:1, bass.ds(j + b * PAGES, 1)], min_val=0, max_val=POOL_PAGES - 1)
                    sp.dma_start(pages_i[:, bass.ds(j, 1), b, :].rearrange("p o d -> p (o d)"),
                                 ins["cache_idx_k"][0, bass.ds(page, 1)][0]).then_inc(idx_pages, 16)
            sp.wait_ge(acc_stored[0], 16 * 4)
            sp.wait_ge(acc_stored[1], 16 * 3)
            load_tile(sp, N_IDX, w_in[:, 0:P])
            sp.dma_start(rot_cos[:], ins["rot"][0]).then_inc(rot_ready, 16)
            sp.dma_start(rot_sin[:], ins["rot"][1]).then_inc(rot_ready, 16)
            load_tile(sp, N_IDX + 1, w_in[:, P:2 * P])
            with sp.Fori(1, N_MAIN // 2) as i:
                for u in range(2):
                    load_tile(sp, 2 * i + (N_IDX + u), w_in[:, bass.ds(i * (2 * P) + u * P, P)])
            with sp.Fori(0, N_GATE // 2) as i:
                for u in range(2):
                    load_tile(sp, 2 * i + (T_G + u), w_in[:, bass.ds(i * (2 * P) + (COL_G + u * P), P)])
            sp_attention(sp)

        @block.gpsimd
        def _(pool):
            nc.gpsimd.memset(ident[:], 0.0).then_inc(ident_set, 1)
            pool.wait_ge(ident_set, 1)
            nc.gpsimd.affine_select(out=ident[:], in_=ident[:], compare_op=ALU.not_equal, fill=1.0, base=0,
                                    pattern=[[-1, P]], channel_multiplier=1).then_inc(ident_set, 1)
            nc.gpsimd.memset(epst[:], EPS).then_inc(ident_set, 1)
            pool.wait_ge(ident_set, 3)
            nc.gpsimd.tensor_copy(identb[:], ident[:]).then_inc(ident_set, 1)
            for t in range(N_IDX):
                rows = IDX_SRC[t][1]
                pool.wait_ge(rot_set, 3 * (t + 1))
                pool.dma_start(scr["proj"][t, 0:rows, :], col[0:rows, t % 2, :]).then_inc(col_stored[t % 2], 16)
            for j, t in enumerate(PICKS):
                pool.wait_ge(acc_set, j + 1)
                pool.dma_start(scr["score"][j], acc[:, j % 2, :]).then_inc(acc_stored[j % 2], 16)
            rotated = 3 * N_IDX
            picks = 0
            for first, pairs, how, pick in RUNS:
                if pick:
                    if picks:
                        pool.wait_ge(mask_picked, 2 * picks)
                        pool.dma_start(scr["keep"][picks - 1], work[:]).then_inc(mask_stored, 16)
                        pool.wait_ge(mask_stored, 16 * picks)
                    else:
                        pool.wait_ge(acc_stored[0], 16 * 4)
                        pool.wait_ge(acc_stored[1], 16 * 3)
                    pool.dma_start(work[:], scr["score"][picks]).then_inc(work_landed, 16)
                    picks += 1
                with pool.Fori(0, pairs) as i:
                    for u in range(2):
                        par = (first + u) % 2
                        if how == "rot":
                            pool.wait_ge(rot_set, 6 * i + (rotated + 3 * (u + 1)))
                        else:
                            pool.wait_ge(chunk_free, 6 * i + 3 * (first + u + 1))
                        pool.dma_start(scr["proj"][bass.ds(2 * i + (first + u), 1)][0], col[:, par, :])\
                            .then_inc(col_stored[par], 16)
                if how == "rot":
                    rotated += 6 * pairs
            pool.wait_ge(mask_picked, 2 * picks)
            pool.dma_start(scr["keep"][picks - 1], work[:]).then_inc(mask_stored, 16)
            pool_attention(pool)

        @block.scalar
        def _(act):
            act.wait_ge(small_in, 80)
            nc.scalar.activation(c_silu[:], c_rows[:], ACT.Silu).then_inc(c_act, 1)

            def square(t):
                rows = x_tiles[t][1]
                act.wait_ge(x_landed[t % 2], 16 * (t // 2 + 1))
                nc.scalar.activation(x_sq[0:rows, :], x_in[0:rows, t % 2, :], ACT.Square,
                                     accum_out=ssum[0:rows, t:t + 1]).then_inc(x_ssum, 1)
                act.wait_ge(x_ssum, t + 1)
                act.wait_ge(ident_set, 4)
                nc.scalar.activation(rstd[0:rows, t:t + 1], ssum[0:rows, t:t + 1], ACT.Sqrt, bias=epst[0:rows, :],
                                     scale=1.0 / D).then_inc(x_root, 1)

            square(0)
            for t in range(TT):
                rows = x_tiles[t][1]
                if t + 1 < TT:
                    square(t + 1)
                for q in range(4):
                    act.wait_ge(x_turned_bank, 4 * t + q + 1)
                    nc.scalar.copy(xn_t[:, 4 * q:4 * q + 4, t * P:t * P + rows],
                                   banks[:, 4 + q, :].rearrange("p (k r) -> p k r", k=4)[:, :, 0:rows])\
                        .then_inc(x_copied, 1)
            act.wait_ge(gmod_set, 1)
            act.wait_ge(x_copied, 4 * TT)
            for k in range(KT):
                need(act, lo_set, k - 1)
                nc.scalar.activation(h_f[:, k % 2, 0:SEQ], xn_t[:, k, 0:SEQ], ACT.Identity,
                                     bias=mod_t[:, k, 8:9], scale=gmod[:, k, 8:9]).then_inc(hp_set, 1)
                act.wait_ge(hp_set, k + 1)
                act.wait_ge(hs_set, k + 1)
                nc.scalar.copy(h_hi[:, k, :], h_f[:, k % 2, :]).then_inc(hi_set, 1)
            act.wait_ge(lo_set, KT)
            split_hi(act, 0, 0)
            for t in range(1, N_IDX):
                split_hi(act, t, t % 2, IDX_SRC[t][1])
            for n in range(NB // 2 * PAGES // 4):
                act.wait_ge(idx_turned, n + 2)
                nc.scalar.copy(past_t[:, n // 2, n % 2 * 512:(n % 2 + 1) * 512], banks[:, 6 + n % 2, :])\
                    .then_inc(idx_copied, 1)
            n = 0
            for t in PICKS:
                rows, width = ROWS_OF(t), WIDTH_OF(t)
                for h in range(IH):
                    act.wait_ge(score_done, n + 1)
                    need(act, acc_step, n - 1)
                    nc.scalar.activation(relu_s[0:rows, n % 2, 0:width],
                                         banks[0:rows, 3 * (n % 2):3 * (n % 2) + 3, :].rearrange(
                                             "p b n -> p (b n)")[:, 0:width],
                                         ACT.Relu, scale=IH ** -0.5 * ID ** -0.5).then_inc(relu_set, 1)
                    n += 1
            split_hi(act, N_IDX, N_IDX % 2)
            for first, pairs, how, pick in RUNS:
                last = first + 2 * pairs == N_PROJ
                with act.Fori(0, pairs - last) as i:
                    for u in range(2):
                        t, par = 2 * i + (first + u), (first + u) % 2
                        split_hi(act, t + 1, 1 - par)
                        if how != "rot":
                            leave_act(act, t, par, i + (first + u) // 2, how)
            split_hi(act, N_PROJ - 1, (N_PROJ - 1) % 2)
            for t in (N_PROJ - 2, N_PROJ - 1):
                leave_act(act, t, t % 2, t // 2, ACT.Sigmoid)
            act_attention(act)

        @block.vector
        def _(dve):
            dve.wait_ge(c_turned, 1)
            nc.vector.tensor_copy(c_t[:], banks[:, 0, 0:KT * 9].rearrange("p (k n) -> p k n", k=KT)).then_inc(c_copied, 1)
            nc.vector.tensor_copy(bada_t[:], banks[:, 0, 160:208]).then_inc(c_copied, 1)
            nc.vector.tensor_copy(gn_t[:], banks[:, 0, 144:160]).then_inc(c_copied, 1)
            for t in range(TT):
                rows = x_tiles[t][1]
                dve.wait_ge(x_root, t + 1)
                nc.vector.reciprocal(rstd[0:rows, t:t + 1], rstd[0:rows, t:t + 1]).then_inc(x_rstd, 1)
                dve.wait_ge(x_rstd, t + 1)
                nc.vector.tensor_scalar(x_in[0:rows, t % 2, :], x_in[0:rows, t % 2, :], rstd[0:rows, t:t + 1], None,
                                        ALU.mult).then_inc(x_scaled, 1)
            dve.wait_ge(ada_used, ADA_N)
            dve.wait_ge(c_copied, 3)
            nc.vector.tensor_tensor(mod_t[:], banks[:, 1, 0:48 * 9].rearrange("p (k n) -> p k n", k=48),
                                    bada_t[:, :, None].to_broadcast([P, 48, 9]), ALU.add).then_inc(mod_set, 1)
            dve.wait_ge(mod_set, 1)
            nc.vector.scalar_tensor_tensor(out=gmod[:], in0=mod_t[:, KT:2 * KT, :], scalar=1.0,
                                           in1=gn_t[:, :, None].to_broadcast([P, KT, 9]), op0=ALU.add,
                                           op1=ALU.mult).then_inc(gmod_set, 1)
            dve.wait_ge(gmod_set, 1)
            dve.wait_ge(x_copied, 4 * TT)
            for k in range(KT):
                def by_token(small):
                    return small[:, k, 0:NB, None].to_broadcast([P, NB, NT])
                rows_s = h_f[:, k % 2, SEQ:TOK].rearrange("p (b t) -> p b t", b=NB)
                need(dve, lo_set, k - 1)
                nc.vector.tensor_tensor(rows_s, xn_t[:, k, SEQ:TOK].rearrange("p (b t) -> p b t", b=NB),
                                        by_token(gmod), ALU.mult).then_inc(hs_mul, 1)
                dve.wait_ge(hs_mul, k + 1)
                nc.vector.tensor_tensor(rows_s, rows_s, by_token(mod_t), ALU.add).then_inc(hs_set, 1)
                if k >= 1:
                    dve.wait_ge(hi_set, k)
                    nc.vector.tensor_tensor(h_lo[:, k - 1, :], h_f[:, (k - 1) % 2, :], h_hi[:, k - 1, :],
                                            ALU.subtract).then_inc(lo_set, 1)
            dve.wait_ge(hi_set, KT)
            nc.vector.tensor_tensor(h_lo[:, KT - 1, :], h_f[:, (KT - 1) % 2, :], h_hi[:, KT - 1, :],
                                    ALU.subtract).then_inc(lo_set, 1)
            split_lo(dve, 0, 0)
            dve.wait_ge(rot_ready, 32)
            for t in range(N_IDX):
                rows = IDX_SRC[t][1]
                if t + 1 < N_IDX:
                    split_lo(dve, t + 1, (t + 1) % 2, IDX_SRC[t + 1][1])
                leave_rotated(dve, t, t % 2, t // 2, 3 * t, ID // 2, min(rows, P) // ID * ID, rows % ID)
            index_scores(dve)
            split_lo(dve, N_IDX, N_IDX % 2)
            dve.wait_ge(rot_ready, 64)
            rotated = 3 * N_IDX
            picks = 0
            for first, pairs, how, pick in RUNS:
                last = first + 2 * pairs == N_PROJ
                if pick:
                    picks += 1
                    dve.wait_ge(work_landed, 16 * picks)
                with dve.Fori(0, pairs - last) as i:
                    for u in range(2):
                        t, par = 2 * i + (first + u), (first + u) % 2
                        split_lo(dve, t + 1, 1 - par)
                        if how == "rot":
                            leave_rotated(dve, t, par, i + (first + u) // 2, 6 * i + (rotated + 3 * u), HD // 2,
                                          between=pick_round if pick else None)
                        elif pick:
                            for c in range(3):
                                pick_round(dve)
                        if pick:
                            for c in range(ROUNDS - 3):
                                pick_round(dve)
                if how == "rot":
                    rotated += 6 * pairs
                if last:
                    split_lo(dve, N_PROJ - 1, (N_PROJ - 1) % 2)
                    for c in range(2 * ROUNDS):
                        pick_round(dve)
                if pick:
                    picked(dve, picks)
            dve_attention(dve)

        @block.tensor
        def _(pe):
            pe.wait_ge(c_act, 1)
            pe.wait_ge(ident_set, 4)
            pe.wait_ge(small_in, 80)
            for k in range(KT):
                nc.tensor.transpose(banks[:, 0, k * 9:(k + 1) * 9], c_silu[:, k * P:(k + 1) * P], ident[0:9, 0:9])
            nc.tensor.transpose(banks[:, 0, 144:160], gn_r[:], ident[0:KT, 0:KT])
            nc.tensor.transpose(banks[:, 0, 160:208], bada_r[:], ident[0:48, 0:48]).then_inc(c_turned, 1)
            for t in range(TT):
                rows = x_tiles[t][1]
                pe.wait_ge(x_scaled, t + 1)
                for q in range(4):
                    need(pe, x_copied, 4 * (t - 1) + q + 1)
                    for k in range(4 * q, 4 * q + 4):
                        tr = nc.tensor.transpose(banks[:, 4 + q, (k % 4) * P:(k % 4) * P + rows],
                                                 x_in[0:rows, t % 2, k * P:(k + 1) * P], ident[0:rows, 0:rows])
                    tr.then_inc(x_turned_bank, 1)
            pe.wait_ge(c_copied, 3)

            def modulation(slot, chunk, column):
                pe.wait_ge(ada_landed[slot], 16 * (chunk + 1))
                for m in range(ADA_C // P):
                    for k in range(KT):
                        mm = nc.tensor.matmul(column(m), ada_w[:, slot, k, m * P:(m + 1) * P], c_t[:, k, :],
                                              start=(k == 0), stop=(k == KT - 1))
                mm.then_inc(ada_used, 1)

            with pe.Fori(0, ADA_N // 2) as i:
                for u in range(2):
                    modulation(u, i, lambda m: banks[:, 1, bass.ds(i * 36 + (2 * u + m) * 9, 9)])
            pe.wait_ge(lo_set, KT)
            for t in range(N_IDX):
                products(pe, t, t % 2, IDX_SRC[t][1])
            pe.wait_ge(idx_landed, 6 * 16)
            for t in range(TT):
                rows = x_tiles[t][1]
                tr = nc.tensor.transpose(banks[0:rows, 6, t * IH:(t + 1) * IH], wi_r[:, t * P:t * P + rows],
                                         ident[0:IH, 0:IH])
            tr.then_inc(idx_turned, 1)
            pe.wait_ge(idx_pages, 16 * NB * PAGES)
            pe.wait_ge(idx_pair_set, 2)
            for n in range(NB // 2 * PAGES // 4):
                need(pe, idx_copied, n - 1)
                for q in range(4):
                    m = n % 2 * 4 + q
                    tr = nc.tensor.transpose(
                        banks[:, 6 + n % 2, q * P:(q + 1) * P],
                        pages_i[:, m, 2 * (n // 2):2 * (n // 2) + 2, :].rearrange("p b d -> p (b d)"), ident[:])
                tr.then_inc(idx_turned, 1)
            pe.wait_ge(idx_copied, 8)
            n = 0
            for t in PICKS:
                rows, width = ROWS_OF(t), WIDTH_OF(t)
                for h in range(IH):
                    need(pe, relu_set, n - 1)
                    keys = (ki_hi, ki_lo)[h % 2]
                    for a in range(0, width, 512):
                        b = min(a + 512, width)
                        dst = banks[0:rows, 3 * (n % 2) + a // 512, 0:b - a]
                        if t < QT or a == PAST:
                            mm = nc.tensor.matmul(dst, qi_t[:, h // 2, t * P:t * P + rows], keys[:, a:b],
                                                  start=True, stop=True)
                        else:
                            for j in range(NB // 2):
                                mm = nc.tensor.matmul(dst, qi_pair[:, h, j, :], past_t[:, j, a:b], start=(j == 0),
                                                      stop=(j == NB // 2 - 1))
                    mm.then_inc(score_done, 1)
                    n += 1
            pe.wait_ge(relu_set, n)
            with pe.Fori(0, (N_PROJ - N_IDX) // 2) as i:
                for u in range(2):
                    products(pe, 2 * i + (N_IDX + u), (N_IDX + u) % 2)
            pe_attention(pe)


_INS = ["x_prompt", "x_sample", "cache_win_k", "cache_win_v", "cache_k", "cache_v", "cache_idx_k", "page_table",
        "c_prompt", "c_sample", "g_norm", "w_ada", "b_ada", "w_in", "w_pa", "w_pb", "w_out", "g_final"]
_OUTS = [("y_prompt", (1, SEQ, D)), ("y_sample", (NB, NT, D)),
         ("win_k_prompt", (1, 1, SEQ, HA, HD)), ("win_v_prompt", (1, 1, SEQ, HA, HD)),
         ("k_prompt", (1, 1, SEQ, KVB, HD)), ("v_prompt", (1, 1, SEQ, KVB, HD)), ("idx_k_prompt", (1, 1, SEQ, ID)),
         ("win_k_sample", (1, NB, NT, HA, HD)), ("win_v_sample", (1, NB, NT, HA, HD)),
         ("k_sample", (1, NB, NT, KVB, HD)), ("v_sample", (1, NB, NT, KVB, HD)), ("idx_k_sample", (1, NB, NT, ID))]
_SCRATCH = [("proj", (N_PROJ, P, TOK)), ("score", (7, P, TOK)), ("keep", (7, P, TOK)), ("att", (HA + HB, P, TOK)),
            ("merged", (KT, P, TOK)), ("resid", (TOK, D))]


def kernel(**inputs):
    import numpy as _np
    import concourse.bacc as _bacc
    from concourse import mybir as _mybir
    from concourse.bass_utils import run_bass_kernel_spmd as _run

    nc = _bacc.Bacc("TRN2", target_bir_lowering=False, num_devices=1)
    arrays, ins, outs = {}, {}, {}
    given = {name: _np.ascontiguousarray(inputs[name]) for name in _INS}
    given.update(shape_tables())
    for name, a in given.items():
        arrays[f"in_{name}"] = a
        ins[name] = nc.dram_tensor(f"in_{name}", a.shape, _mybir.dt.from_np(a.dtype), kind="ExternalInput").ap()
    for name, shape in _OUTS:
        outs[name] = nc.dram_tensor(f"out_{name}", shape, _mybir.dt.float32, kind="ExternalOutput").ap()
    scr = {name: nc.dram_tensor(f"scratch_{name}", shape, _mybir.dt.float32, kind="Internal").ap()
           for name, shape in _SCRATCH}
    decode_step(nc, ins, outs, scr)
    r = _run(nc, [arrays], core_ids=[0])
    return tuple(r.results[0][f"out_{name}"] for name, _ in _OUTS)
```

```python
from contextlib import ExitStack

import numpy as np
import concourse.bass as bass
from concourse import mybir

F32 = mybir.dt.float32
F32R = mybir.dt.float32r
BF16 = mybir.dt.bfloat16
I32 = mybir.dt.int32
ALU = mybir.AluOpType
ACT = mybir.ActivationFunctionType
AX = mybir.AxisListType.X

P = 128
D = 2048
KT = D // P
SEQ = 1024
NB, NT = 8, 8
SMP = NB * NT
TOK = SEQ + SMP
QT = SEQ // P
TT = QT + 1
PAST = 1024
PAGES = PAST // P
POOL_PAGES = 80
HD = 128
HA, HB, KVB, GRP = 4, 8, 2, 3
IH, ID = 4, 64
TOPK = 256
EPS = 1e-6
SCALE = HD ** -0.5
BIG = 2.0 ** 100
TAKEN = -3.0e38
CHUNKS = ((0, 384), (384, 736), (736, 1088))
DILS = ((128, 1), (512, 4), (2048, 16))

N_IDX = 3
N_MAIN = 44
N_GATE = 32
COL_QI, COL_KI, COL_G = 5632, 5888, 5956
T_QA, T_KA, T_VA, T_ZA = N_IDX, N_IDX + 12, N_IDX + 16, N_IDX + 20
T_QB, T_KB, T_VB, T_ZB = N_IDX + 24, N_IDX + 32, N_IDX + 34, N_IDX + 36
T_G = N_IDX + N_MAIN
N_PROJ = T_G + N_GATE
ADA_C = 256
ADA_N = 3 * D // ADA_C
ADA_S = ADA_N // QT


def shape_tables():
    pos = np.concatenate([np.arange(SEQ), np.tile(PAST + np.arange(NT), NB)]).astype(np.float32)

    def rot(dim):
        half = dim // 2
        inv = np.exp(np.arange(half, dtype=np.float32) * np.float32(-np.log(10000.0) / half)).astype(np.float32)
        ang = (pos[None, :] * inv[:, None]).astype(np.float32)
        c, s = np.cos(ang).astype(np.float32), np.sin(ang).astype(np.float32)
        reps = P // dim
        return np.concatenate([np.concatenate([c, c])] * reps), np.concatenate([np.concatenate([s, -s])] * reps)

    t = {}
    t["rot"] = np.stack([*rot(HD), *rot(ID)]).astype(np.float32)
    p, c = np.arange(P)[:, None], np.arange(P)[None, :]
    blocks = []
    for n_blk, (win, dil) in zip((8, 5, 2), DILS[::-1]):
        for b in range(n_blk):
            dist = (n_blk - 1 - b) * P + p - c
            blocks.append((dist >= 0) & (dist % dil == 0) & (dist <= win))
    ok = np.concatenate(blocks, 1)
    t["mask_p"] = np.where(ok, 0.0, -BIG).astype(np.float32)
    rows = np.arange(96)
    g, tq = rows // 32, rows % NT
    key = np.arange(PAST)
    ma = np.zeros((96, PAST), bool)
    mn = np.zeros((96, NB, SMP), bool)
    for r in range(96):
        win, dil = DILS[g[r]]
        dist = PAST + tq[r] - key
        ma[r] = (dist % dil == 0) & (dist <= win)
        for b in range(NB):
            u = np.arange(SMP)
            d2 = tq[r] - u % NT
            mn[r, b] = (u // NT == b) & (d2 >= 0) & (d2 % dil == 0) & (d2 <= win)
    t["mask_s"] = np.where(np.concatenate([ma, mn.reshape(96, -1)], 1), 0.0, -BIG).astype(np.float32)
    r64 = np.arange(SMP)
    u = np.arange(SMP)
    ok = (u[None] // NT == r64[:, None] // NT) & (u[None] <= r64[:, None])
    t["mask_i"] = np.where(ok, 0.0, -BIG).astype(np.float32)
    rep = np.zeros((SMP, NB, SMP), np.float32)
    for b in range(NB):
        for r in range(SMP):
            rep[b * NT + r % NT, b, r] = 1.0
    t["rep"] = rep
    same = (np.arange(96)[:, None] % 32 == np.arange(P)[None] % 32)
    t["same"] = same.astype(np.float32)
    return t


def need(eng, sem, value):
    if not (isinstance(value, int) and value <= 0):
        eng.wait_ge(sem, value)


def decode_step(nc, ins, outs, scr):
    ctx = ExitStack()
    with ctx:
        base = (nc.sbuf_base + 63) // 64 * 64

        def at(name, shape, dt, off):
            return nc.alloc_sbuf_tensor_at(name, shape, dt, offset=base + off)

        def sem(name):
            return ctx.enter_context(nc.semaphore(name))

        banks = ctx.enter_context(nc.psum_tensor("banks", [P, 8, 512], F32))

        ident = at("ident", [P, P], F32, 0)
        identb = at("identb", [P, P], BF16, 512)
        mod_t = at("mod_t", [P, 48, 9], F32, 768)
        gmod = at("gmod", [P, KT, 9], F32, 2496)
        bada_t = at("bada_t", [P, 48], F32, 3072)
        gn_t = at("gn_t", [P, KT], F32, 3264)
        ssum = at("ssum", [P, 16], F32, 3328)
        rstd = at("rstd", [P, 16], F32, 3392)
        epst = at("epst", [P, 1], F32, 3456)
        H_HI, H_LO = 4352, 4352 + KT * TOK * 4
        h_hi = at("h_hi", [P, KT, TOK], F32R, H_HI)
        h_lo = at("h_lo", [P, KT, TOK], F32R, H_LO)
        xn_t = at("xn_t", [P, KT, TOK], F32, H_LO)
        ada_w = at("ada_w", [P, ADA_S, KT, ADA_C], F32, H_HI)
        ada_hi = at("ada_hi", [P, 2, KT // 2, ADA_C], F32R, H_HI + 50176)
        c_rows = at("c_rows", [9, D], F32, H_HI + 32768)
        c_silu = at("c_silu", [9, D], F32, H_HI + 40960)
        bada_r = at("bada_r", [48, P], F32, H_HI + 49152)
        gn_r = at("gn_r", [KT, P], F32, H_HI + 49664)
        W0 = H_LO + KT * TOK * 4
        w_hi = at("w_hi", [P, 2, KT, P], F32R, W0)
        w_lo = at("w_lo", [P, 2, KT, P], F32R, W0 + 16384)
        w_raw = at("w_raw", [P, KT, P], F32, W0 + 32768)
        rot_cos = at("rot_cos", [P, TOK], F32, W0 + 40960)
        rot_sin = at("rot_sin", [P, TOK], F32, W0 + 45312)
        col = at("col", [P, 2, TOK], F32, W0 + 49664)
        rot_a = at("rot_a", [P, 2, 384], F32, W0 + 58368)
        rot_b = at("rot_b", [P, 2, 384], F32, W0 + 61440)
        work = at("work", [P, TOK], F32, W0 + 64512)
        best8 = at("best8", [P, 8], F32, W0 + 68864)
        pages_i = at("pages_i", [P, PAGES, NB, ID], F32, W0)
        past_t = at("past_t", [P, NB // 2, PAST], F32, W0 + 16384)
        ki_hi = at("ki_hi", [P, TOK], F32, W0 + 32768)
        ki_lo = at("ki_lo", [P, TOK], F32, W0 + 37120)
        qi_t = at("qi_t", [P, 2, TOK], F32, W0 + 41472)
        qi_pair = at("qi_pair", [P, IH, NB // 2, SMP], F32, W0 + 50176)
        relu_s = at("relu_s", [P, 2, TOK], F32, W0 + 54272)
        wi_r = at("wi_r", [IH, TOK], F32, W0 + 62976)
        wi_tok = at("wi_tok", [P, TT, IH], F32, W0 + 67328)
        diag = at("diag", [P, P], F32, W0 + 67488)
        mask_i = at("mask_i", [SMP, SMP], F32, W0 + 68000)
        acc = at("acc", [P, 2, TOK], F32, W0)
        pages_n = at("pages_n", [1, NB * PAGES], I32, 4064)
        x_in = at("x_in", [P, 2, D], F32, W0)
        x_sq = at("x_sq", [P, D], F32, W0 + 16384)
        h_f = at("h_f", [P, 2, TOK], F32, W0 + 49664)
        ada_lo = at("ada_lo", [P, 2, KT // 2, ADA_C], F32R, W0 + 24576)
        c_hl = at("c_hl", [P, KT, 18], F32R, W0 + 49664)
        fold = at("fold", [18, 9], F32, W0 + 50816)
        mod_r = at("mod_r", [18, 2, ADA_C], F32, W0 + 50944)

        small_in = sem("small_in")
        ident_set = sem("ident_set")
        c_act = sem("c_act")
        c_turned = sem("c_turned")
        c_copied = sem("c_copied")
        x_landed = [sem(f"x_landed{i}") for i in range(2)]
        x_ssum = sem("x_ssum")
        x_root = sem("x_root")
        x_rstd = sem("x_rstd")
        x_scaled = sem("x_scaled")
        x_turned_bank = sem("x_turned_bank")
        x_copied = sem("x_copied")
        ada_landed = [sem(f"ada_landed{i}") for i in range(ADA_S)]
        ada_hi_set = sem("ada_hi_set")
        ada_lo_set = sem("ada_lo_set")
        ada_used = sem("ada_used")
        mod_r_set = sem("mod_r_set")
        ada_folded = sem("ada_folded")
        mod_set = sem("mod_set")
        gmod_set = sem("gmod_set")
        hp_set = sem("hp_set")
        hs_mul = sem("hs_mul")
        hs_set = sem("hs_set")
        hi_set = sem("hi_set")
        lo_set = sem("lo_set")
        w_landed = sem("w_landed")
        w_hi_set = sem("w_hi_set")
        w_lo_set = sem("w_lo_set")
        chunk_done = sem("chunk_done")
        chunk_free = sem("chunk_free")
        rot_ready = sem("rot_ready")
        rot_set = sem("rot_set")
        idx_landed = sem("idx_landed")
        idx_copies = sem("idx_copies")
        idx_pages = sem("idx_pages")
        idx_zeroed = sem("idx_zeroed")
        wi_turned = sem("wi_turned")
        idx_turned = sem("idx_turned")
        idx_copied = sem("idx_copied")
        idx_pair_set = sem("idx_pair_set")
        score_done = sem("score_done")
        relu_set = sem("relu_set")
        acc_step = sem("acc_step")
        acc_set = sem("acc_set")
        acc_fill = sem("acc_fill")
        acc_stored = [sem(f"acc_stored{i}") for i in range(2)]
        work_landed = sem("work_landed")
        mask_picked = sem("mask_picked")
        mask_stored = sem("mask_stored")
        col_stored = [sem(f"col_stored{i}") for i in range(2)]

        x_tiles = [(ins["x_prompt"][0, t * P:(t + 1) * P, :], P) for t in range(QT)]
        x_tiles.append((ins["x_sample"].rearrange("b t d -> (b t) d"), SMP))
        w_in = ins["w_in"][0]
        w_ada = ins["w_ada"][0]

        def load_tile(sp, t, src, width=P):
            need(sp, w_lo_set, t)
            sp.dma_start(w_raw[:, :, 0:width], src.rearrange("(k p) n -> p k n", p=P)).then_inc(w_landed, 16)

        def split_hi(act, t, par, width=P):
            act.wait_ge(w_landed, 16 * (t + 1))
            need(act, chunk_done, 3 * (t - 1))
            nc.scalar.copy(w_hi[:, par, :, 0:width], w_raw[:, :, 0:width]).then_inc(w_hi_set, 1)

        def split_lo(dve, t, par, width=P):
            dve.wait_ge(w_hi_set, t + 1)
            nc.vector.tensor_tensor(w_lo[:, par, :, 0:width], w_raw[:, :, 0:width], w_hi[:, par, :, 0:width],
                                    ALU.subtract).then_inc(w_lo_set, 1)

        def products(pe, t, par, width=P):
            pe.wait_ge(w_lo_set, t + 1)
            for c, (a, b) in enumerate(CHUNKS):
                need(pe, chunk_free, 3 * t + c - 2)
                for k in range(KT):
                    dst = banks[0:width, c, 0:b - a]
                    nc.tensor.matmul(dst, w_hi[:, par, k, 0:width], h_hi[:, k, a:b], start=(k == 0), stop=False)
                    nc.tensor.matmul(dst, w_hi[:, par, k, 0:width], h_lo[:, k, a:b], start=False, stop=False)
                    mm = nc.tensor.matmul(dst, w_lo[:, par, k, 0:width], h_hi[:, k, a:b], start=False,
                                          stop=(k == KT - 1))
                mm.then_inc(chunk_done, 1)

        def first_products(pe, weights_set, rows_set, done, order=range(KT)):
            pe.wait_ge(weights_set, 1)
            for x, k in enumerate(order):
                pe.wait_ge(rows_set, x + 1)
                for c, (a, b) in enumerate(CHUNKS):
                    dst = banks[:, c, 0:b - a]
                    nc.tensor.matmul(dst, w_hi[:, 0, k, :], h_hi[:, k, a:b], start=(x == 0), stop=False)
                    nc.tensor.matmul(dst, w_hi[:, 0, k, :], h_lo[:, k, a:b], start=False, stop=False)
                    mm = nc.tensor.matmul(dst, w_lo[:, 0, k, :], h_hi[:, k, a:b], start=False, stop=(x == KT - 1))
                    if x == KT - 1:
                        mm.then_inc(done, 1)

        def leave_act(act, t, par, earlier, func):
            need(act, col_stored[par], 16 * earlier)
            for c, (a, b) in enumerate(CHUNKS):
                act.wait_ge(chunk_done, 3 * t + c + 1)
                act.wait_ge(chunk_free, 3 * t + c)
                nc.scalar.activation(col[:, par, a:b], banks[:, c, 0:b - a], func).then_inc(chunk_free, 1)

        def leave_rotated(dve, t, par, earlier, rotated, half, rows=P, plain=0, between=None):
            need(dve, col_stored[par], 16 * earlier)
            for c, (a, b) in enumerate(CHUNKS):
                n, s = b - a, (par + c) % 2
                need(dve, rot_set, rotated + c - 1)
                dve.wait_ge(chunk_done, 3 * t + c + 1)
                need(dve, chunk_free, 3 * t + c)
                if plain:
                    nc.vector.tensor_copy(col[rows:rows + plain, par, a:b], banks[rows:rows + plain, c, 0:n])
                for q in range(0, rows, half):
                    o = q + half if q // half % 2 == 0 else q - half
                    nc.vector.tensor_tensor(rot_b[o:o + half, s, 0:n], banks[q:q + half, c, 0:n],
                                            rot_sin[q:q + half, a:b], ALU.mult)
                nc.vector.tensor_tensor(rot_a[0:rows, s, 0:n], banks[0:rows, c, 0:n], rot_cos[0:rows, a:b],
                                        ALU.mult).then_inc(chunk_free, 1)
                dve.wait_ge(chunk_free, 3 * t + c + 1)
                nc.vector.tensor_tensor(col[0:rows, par, a:b], rot_a[0:rows, s, 0:n], rot_b[0:rows, s, 0:n],
                                        ALU.add).then_inc(rot_set, 1)
                if between:
                    between(dve)

        IDX_SRC = [(w_in[:, COL_QI:COL_QI + P], P), (w_in[:, COL_QI + P:COL_QI + 2 * P], P),
                   (w_in[:, COL_KI:COL_KI + ID + IH], ID + IH)]
        RUNS = [(T_QA, 4, "rot", True), (T_QA + 8, 4, "rot", True), (T_VA, 2, ACT.Copy, False),
                (T_ZA, 2, ACT.Silu, False), (T_QB, 5, "rot", False), (T_VB, 1, ACT.Copy, False),
                (T_ZB, 4, ACT.Silu, True), *[(T_G + 8 * n, 4, ACT.Sigmoid, True) for n in range(4)]]
        ROUNDS = TOPK // 8 // 8
        PICKS = [*range(2, QT), QT]
        ROWS_OF = lambda t: SMP if t == QT else P
        WIDTH_OF = lambda t: TOK if t == QT else (t + 1) * P

        def first_steps(eng, body):
            body(0, 0, 0)
            body(1, 1, 0)
            with eng.Fori(1, QT // 2) as i:
                body(2 * i, 0, i)
                body(2 * i + 1, 1, i)

        A0 = H_HI
        k_t = at("k_t", [P, HA + KVB, TOK], F32, A0)
        VW = (HA + KVB) * HD
        v_tok = at("v_tok", [P, TT, VW], F32, A0 + 26112)
        q_tile = at("q_tile", [P, 2, GRP * HA + HB, P], F32, A0 + 53760)
        p_buf = [at(f"p_buf{i}", [P, 15 * P], F32, off) for i, off in
                 enumerate((A0 + 74240, A0 + 74240 + 7680, A0 + 196992))]
        p_t = at("p_t", [P, 2, SEQ], F32, A0 + 89600)
        o_tok = at("o_tok", [P, 2, (HA + HB) * HD], F32, A0 + 97792)
        o_t = at("o_t", [P, 2, HA + HB, P], F32, A0 + 110080)
        mask_b = at("mask_b", [P, 15 * P], BF16, A0 + 122368)
        keep_f = at("keep_f", [P, SEQ], F32, A0 + 126208)
        keep_b = at("keep_b", [P, 2, SEQ], BF16, A0 + 130304)
        mx = at("mx", [P, 96], F32, A0 + 134400)
        nmx = at("nmx", [P, 96], F32, A0 + 134784)
        lsum = at("lsum", [P, 96], F32, A0 + 135168)
        rinv = at("rinv", [P, 96], F32, A0 + 135552)
        v_t = at("v_t", [P, HA + KVB, TOK], F32, A0 + 135936)
        kiT = at("kiT", [ID, TOK], F32, A0 + 162048)
        k_tok = at("k_tok", [P, TT, VW], F32, A0 + 166400)
        ki_tok = at("ki_tok", [P, TT, ID], F32, A0 + 194048)
        mask_f = at("mask_f", [P, 15 * P], F32, A0 + 196352)

        KV_PARTS = ((0, 2 * P), (2 * P, 5 * P), (5 * P, TOK))
        kv_landed = [sem(f"kv_landed{i}") for i in range(len(KV_PARTS))]
        mask_landed = sem("mask_landed")
        kv_turned = sem("kv_turned")
        kv_act = sem("kv_act")
        kv_dve = sem("kv_dve")
        kv_stored = sem("kv_stored")
        mask_cast = sem("mask_cast")
        q_landed = [sem(f"q_landed{i}") for i in range(2)]
        keep_landed = sem("keep_landed")
        keep_cast = sem("keep_cast")
        s_done = sem("s_done")
        mx_set = sem("mx_set")
        nmx_set = sem("nmx_set")
        exp_done = sem("exp_done")
        groups_added = sem("groups_added")
        rinv_set = sem("rinv_set")
        t_done = sem("t_done")
        t_out = sem("t_out")
        pv_done = sem("pv_done")
        o_out = sem("o_out")
        att_stored = [sem(f"att_stored{i}") for i in range(2)]

        JOBS = []
        for i in range(QT):
            for a in range(HA):
                JOBS += [("A", i, a), ("B", i, 2 * a), ("B", i, 2 * a + 1)]
        NJ = len(JOBS)
        PER = HA + HB
        blocks_of = lambda n: JOBS[n][1] + 1
        SEG = lambda i: ((2, i + 1, 0), (1, min(5, i + 1), 8), (0, min(2, i + 1), 13))
        width_of = lambda n: (sum(s[1] for s in SEG(JOBS[n][1])) if JOBS[n][0] == "A" else JOBS[n][1] + 1) * P
        s_bank = lambda n: 0 if JOBS[n][0] == "A" else 4 + (JOBS[n][2] % 2 if JOBS[n][1] < 4 else 0)
        s_banks = lambda n: set(range(s_bank(n), s_bank(n) + (width_of(n) + 511) // 512))
        exps_before = lambda n: max([m + 1 for m in range(n) if s_banks(m) & s_banks(n)], default=0)
        a_jobs = lambda n: sum(JOBS[m][0] == "A" for m in range(n))
        T_BANK, O_BANK = 6, 7
        USES = []
        for n in range(NJ + 5):
            if 2 <= n < NJ + 2:
                USES.append(("w", n - 2, 0))
                if blocks_of(n - 2) > 4:
                    USES.append(("w", n - 2, 1))
            if n >= 4 and (n - 4) % PER == PER - 1:
                USES += [("o", (n - 4) // PER, g) for g in range(3)]
        use_no = {u: x for x, u in enumerate(USES)}

        def flat(bank, rows, width):
            return banks[0:rows, bank:bank + (width + 511) // 512, :].rearrange("p b n -> p (b n)")[:, 0:width]

        def columns_stored(eng):
            eng.wait_ge(col_stored[0], 16 * ((N_PROJ + 1) // 2))
            eng.wait_ge(col_stored[1], 16 * (N_PROJ // 2))

        def store_keys_values(sp):
            sp.wait_ge(kv_act, 2 * TT)
            sp.wait_ge(kv_dve, 3 * TT)
            for src, cols, big, small in ((k_tok, (0, 512), "win_k_prompt", "win_k_sample"),
                                          (v_tok, (0, 512), "win_v_prompt", "win_v_sample"),
                                          (k_tok, (512, 768), "k_prompt", "k_sample"),
                                          (v_tok, (512, 768), "v_prompt", "v_sample"),
                                          (ki_tok, (0, ID), "idx_k_prompt", "idx_k_sample")):
                a, b = cols
                sp.dma_start(flat_rows(outs[big]).rearrange("(t p) n -> p t n", p=P), src[:, 0:QT, a:b])\
                    .then_inc(kv_stored, 16)
                sp.dma_start(flat_rows(outs[small]), src[0:SMP, QT, a:b]).then_inc(kv_stored, 16)

        def sp_attention(sp):
            sp.wait_ge(chunk_done, 3 * N_PROJ)
            proj = scr["proj"]
            for x, (a, b) in enumerate(KV_PARTS):
                for dst, first, n in ((k_t[:, 0:HA], T_KA, HA), (v_t[:, 0:HA], T_VA, HA), (k_t[:, HA:], T_KB, KVB),
                                      (v_t[:, HA:], T_VB, KVB)):
                    sp.dma_start(dst[:, :, a:b], proj[first:first + n, :, a:b].rearrange("m p n -> p m n"))\
                        .then_inc(kv_landed[x], 16)
                sp.dma_start(kiT[:, a:b], proj[2, 0:ID, a:b]).then_inc(kv_landed[x], 16)
            columns_stored(sp)
            sp.wait_ge(mask_stored, 16 * len(PICKS))
            sp.dma_start(mask_f[:], ins["mask_p"]).then_inc(mask_landed, 16)

            def store_outputs(i):
                sp.wait_ge(t_out, use_no["o", i, 2] + 1)
                sp.dma_start(scr["att"][:, :, i * P:(i + 1) * P].rearrange("m p n -> p m n"), o_t[:, i % 2])\
                    .then_inc(att_stored[i % 2], 16)

            for i in range(QT):
                need(sp, s_done, PER * (i - 1))
                for dst, first, n in ((0, T_QA, GRP * HA), (GRP * HA, T_QB, HB)):
                    sp.dma_start(q_tile[:, i % 2, dst:dst + n, :],
                                 proj[first:first + n, :, i * P:(i + 1) * P].rearrange("m p n -> p m n"))\
                        .then_inc(q_landed[i % 2], 16)
                if i >= 2:
                    need(sp, keep_cast, i - 2)
                    sp.dma_start(keep_f[:, 0:(i + 1) * P], scr["keep"][i - 2][:, 0:(i + 1) * P]).then_inc(keep_landed, 16)
                if i == 1:
                    store_keys_values(sp)
                if i == 3:
                    sp_sample_early(sp)
                if i == 6:
                    sp_values_early(sp)
                if i >= 2:
                    store_outputs(i - 2)
            store_outputs(QT - 2)
            store_outputs(QT - 1)
            sp_sample(sp)

        def act_attention(act):
            columns_stored(act)
            for t in range(TT):
                rows = ROWS_OF(t)
                act.wait_ge(kv_turned, t + 1)
                b0 = 4 * (t % 2)
                nc.scalar.copy(k_tok[0:rows, t, 0:HA * HD], banks[0:rows, b0, :]).then_inc(kv_act, 1)
                nc.scalar.copy(v_tok[0:rows, t, 0:HA * HD], banks[0:rows, b0 + 1, :]).then_inc(kv_act, 1)
            act.wait_ge(mask_landed, 16)
            nc.scalar.copy(mask_b[:], mask_f[:]).then_inc(mask_cast, 1)
            for n in range(NJ + 5):
                if n < NJ:
                    act.wait_ge(nmx_set, n + 1)
                    need(act, t_done, 0 if n < 3 else last_use(n - 3) + 1)
                    nc.scalar.activation(p_buf[n % 3][:, 0:width_of(n)], flat(s_bank(n), P, width_of(n)), ACT.Exp,
                                         bias=nmx[:, n:n + 1], scale=SCALE, accum_out=lsum[:, n:n + 1])\
                        .then_inc(exp_done, 1)
                m = n - 2
                if ("w", m, 1) in use_no:
                    act.wait_ge(t_done, use_no["w", m, 1] + 1)
                    nc.scalar.copy(p_t[:, m % 2, 512:blocks_of(m) * P], banks[:, T_BANK, 0:(blocks_of(m) - 4) * P]).then_inc(t_out, 1)
            act_sample(act)

        def last_use(n):
            return use_no["w", n, 1] if blocks_of(n) > 4 else use_no["w", n, 0]

        def flat_rows(ap):
            return ap.rearrange("l b t n -> (l b t) n" if len(ap.shape) == 4 else "l b t h d -> (l b t) (h d)")

        def pool_attention(pool):
            def cast_keep(i):
                pool.wait_ge(keep_landed, 16 * (i - 1))
                need(pool, s_done, PER * (i - 1))
                nc.gpsimd.tensor_copy(keep_b[:, i % 2, 0:(i + 1) * P], keep_f[:, 0:(i + 1) * P]).then_inc(keep_cast, 1)

            for n in range(NJ):
                kind, i, _ = JOBS[n]
                if kind == "A":
                    pool.wait_ge(exp_done, n + 1)
                    off = (i + 1) * P
                    for seg in SEG(i)[1:]:
                        w = seg[1] * P
                        dst = p_buf[n % 3][:, (i + 1) * P - w:(i + 1) * P]
                        nc.gpsimd.tensor_tensor(dst, dst, p_buf[n % 3][:, off:off + w], ALU.add)\
                            .then_inc(groups_added, 1)
                        off += w
                        pool.wait_ge(groups_added, 2 * a_jobs(n) + seg_no(seg))
                if n % PER == 0 and 2 <= i + 1 < QT:
                    cast_keep(i + 1)
                if i == 5 and n % PER in (3, 6, 9):
                    cast_sample_mask(pool, n % PER // 3 - 1)
            pool_sample(pool)

        def seg_no(seg):
            return 2 - seg[0]

        def dve_attention(dve):
            columns_stored(dve)
            for t in range(TT):
                rows = ROWS_OF(t)
                dve.wait_ge(kv_turned, t + 1)
                b0 = 4 * (t % 2) + 2
                nc.vector.tensor_copy(k_tok[0:rows, t, 512:768], banks[0:rows, b0, 0:256]).then_inc(kv_dve, 1)
                nc.vector.tensor_copy(v_tok[0:rows, t, 512:768], banks[0:rows, b0, 256:512]).then_inc(kv_dve, 1)
                nc.vector.tensor_copy(ki_tok[0:rows, t, :], banks[0:rows, b0 + 1, 0:ID]).then_inc(kv_dve, 1)
            for n in range(NJ + 5):
                if n < NJ:
                    dve.wait_ge(s_done, n + 1)
                    nc.vector.tensor_reduce(mx[:, n:n + 1], flat(s_bank(n), P, width_of(n)), AX, ALU.max)\
                        .then_inc(mx_set, 1)
                    dve.wait_ge(mx_set, n + 1)
                    nc.vector.tensor_scalar(nmx[:, n:n + 1], mx[:, n:n + 1], -SCALE, None, ALU.mult).then_inc(nmx_set, 1)
                m = n - 2
                if 0 <= m < NJ:
                    dve.wait_ge(t_done, use_no["w", m, 0] + 1)
                    need(dve, pv_done, m - 1)
                    w = min(4, blocks_of(m)) * P
                    nc.vector.tensor_copy(p_t[:, m % 2, 0:w], banks[:, T_BANK, 0:w]).then_inc(t_out, 1)
                    dve.wait_ge(exp_done, m + 1)
                    nc.vector.reciprocal(rinv[:, m:m + 1], lsum[:, m:m + 1]).then_inc(rinv_set, 1)
                m = n - 3
                if 0 <= m < NJ:
                    kind, i, h = JOBS[m]
                    dve.wait_ge(pv_done, m + 1)
                    dve.wait_ge(rinv_set, m + 1)
                    need(dve, t_done, 0 if i < 2 else use_no["o", i - 2, 2] + 1)
                    c0 = (h if kind == "A" else HA + h) * HD
                    nc.vector.tensor_scalar(o_tok[:, i % 2, c0:c0 + HD], banks[:, O_BANK, 0:HD], rinv[:, m:m + 1],
                                            None, ALU.mult).then_inc(o_out, 1)
                if n >= 4 and (n - 4) % PER == PER - 1:
                    i = (n - 4) // PER
                    need(dve, att_stored[i % 2], 16 * (i // 2))
                    for g in range(3):
                        dve.wait_ge(t_done, use_no["o", i, g] + 1)
                        nc.vector.tensor_copy(o_t[:, i % 2, 4 * g:4 * g + 4, :],
                                              banks[:, T_BANK, :].rearrange("p (m n) -> p m n", m=4)).then_inc(t_out, 1)
            dve_sample(dve)

        def pe_attention(pe):
            pe.wait_ge(chunk_free, 3 * N_PROJ)
            for t in range(TT):
                rows = ROWS_OF(t)
                pe.wait_ge(kv_landed[(t >= 2) + (t >= 5)], 5 * 16)
                if t >= 2:
                    pe.wait_ge(kv_act, 2 * (t - 1))
                    pe.wait_ge(kv_dve, 3 * (t - 1))
                b0 = 4 * (t % 2)
                for bank, src, h0, n, c0 in ((0, k_t, 0, HA, 0), (1, v_t, 0, HA, 0), (2, k_t, HA, KVB, 0),
                                             (2, v_t, HA, KVB, 256)):
                    for h in range(n):
                        nc.tensor.transpose(banks[0:rows, b0 + bank, c0 + h * P:c0 + (h + 1) * P],
                                            src[:, h0 + h, t * P:t * P + rows], ident[:])
                nc.tensor.transpose(banks[0:rows, b0 + 3, 0:ID], kiT[:, t * P:t * P + rows], ident[0:ID, 0:ID])\
                    .then_inc(kv_turned, 1)
            pe.wait_ge(kv_act, 2 * TT)
            pe.wait_ge(kv_dve, 3 * TT)
            pe.wait_ge(mask_cast, 1)

            def pieces(start, width):
                a = start
                while a < start + width:
                    b = min(start + width, (a // 512 + 1) * 512)
                    yield a, b
                    a = b

            def scores(n):
                kind, i, h = JOBS[n]
                if n % PER == 0:
                    pe.wait_ge(q_landed[i % 2], 32 * (i // 2 + 1))
                    if i >= 2:
                        pe.wait_ge(keep_cast, i - 1)
                need(pe, exp_done, exps_before(n))
                if kind == "A":
                    strips = [(q_tile[:, i % 2, g * HA + h, :], h, (i + 1 - nb) * P, nb * P,
                               mask_b[:, (m0 + (8, 5, 2)[2 - g] - nb) * P:(m0 + (8, 5, 2)[2 - g]) * P])
                              for g, nb, m0 in SEG(i)]
                else:
                    mask = keep_b[:, i % 2, 0:(i + 1) * P] if i >= 2 else None
                    strips = [(q_tile[:, i % 2, GRP * HA + h, :], HA + h // (HB // KVB), 0, (i + 1) * P, mask)]
                at_col = 0
                for lhs, kh, key0, width, mask in strips:
                    for a, b in pieces(at_col, width):
                        dst = banks[:, s_bank(n) + a // 512, a % 512:a % 512 + b - a]
                        nc.tensor.matmul(dst, lhs, k_t[:, kh, key0 + a - at_col:key0 + b - at_col], start=True,
                                         stop=False)
                        if mask is not None:
                            mm = nc.tensor.matmul(dst, identb[:], mask[:, a - at_col:b - at_col], start=False, stop=True)
                        else:
                            mm = nc.tensor.matmul(dst[:, width - P:width], identb[:], mask_b[:, 14 * P:15 * P],
                                                  start=False, stop=True)
                    at_col += width
                mm.then_inc(s_done, 1)

            def turn_weights(n, half):
                x = use_no["w", n, half]
                if JOBS[n][0] == "A":
                    pe.wait_ge(groups_added, 2 * a_jobs(n + 1))
                else:
                    pe.wait_ge(exp_done, n + 1)
                need(pe, t_out, x)
                for b in range(4 * half, min(4 * half + 4, blocks_of(n))):
                    tr = nc.tensor.transpose(banks[:, T_BANK, b % 4 * P:(b % 4 + 1) * P],
                                             p_buf[n % 3][:, b * P:(b + 1) * P], ident[:])
                tr.then_inc(t_done, 1)

            def values(n):
                kind, i, h = JOBS[n]
                pe.wait_ge(t_out, last_use(n) + 1)
                need(pe, o_out, n)
                c0 = h * HD if kind == "A" else (HA + h // (HB // KVB)) * HD
                for b in range(blocks_of(n)):
                    mm = nc.tensor.matmul(banks[:, O_BANK, 0:HD], p_t[:, n % 2, b * P:(b + 1) * P],
                                          v_tok[:, b, c0:c0 + HD], start=(b == 0), stop=(b == blocks_of(n) - 1))
                mm.then_inc(pv_done, 1)

            for n in range(NJ + 5):
                if n < NJ:
                    scores(n)
                if 2 <= n < NJ + 2:
                    turn_weights(n - 2, 0)
                if 3 <= n < NJ + 3:
                    values(n - 3)
                if ("w", n - 2, 1) in use_no:
                    turn_weights(n - 2, 1)
                if n >= 4 and (n - 4) % PER == PER - 1:
                    i = (n - 4) // PER
                    pe.wait_ge(o_out, PER * (i + 1))
                    for g in range(3):
                        need(pe, t_out, use_no["o", i, g])
                        for m in range(4 * g, 4 * g + 4):
                            tr = nc.tensor.transpose(banks[:, T_BANK, m % 4 * P:(m % 4 + 1) * P],
                                                     o_tok[:, i % 2, m * P:(m + 1) * P], ident[:])
                        tr.then_inc(t_done, 1)
            pe_sample(pe)

        NK = PAST + SMP
        V0, S0 = A0 + 26112, A0 + 53760
        H0 = S0 + 82176
        kp_t = at("kp_t", [P, HA + KVB, PAST], F32, S0)
        raw0 = (H0, S0 + 24576)
        win_k = [at(f"win_k{i}", [P, PAGES, HA * HD], F32, raw0[i]) for i in range(2)]
        win_v = [at(f"win_v{i}", [P, PAGES, HA * HD], F32, raw0[i] + 16384) for i in range(2)]
        pool_k = [at(f"pool_k{i}", [P, PAGES, KVB * HD], F32, raw0[i] + 32768) for i in range(2)]
        pool_v = [at(f"pool_v{i}", [P, PAGES, KVB * HD], F32, raw0[i] + 40960) for i in range(2)]
        mask_sf = at("mask_sf", [96, PAST + NB * SMP], F32, H0 + 40960)
        rep_f = at("rep_f", [SMP, NB, SMP], F32, H0 + 47104)
        q_s = at("q_s", [P, GRP * HA + HB, SMP], F32, H0 + 49152)
        mask_sb = at("mask_sb", [96, PAST + NB * SMP], BF16, H0 + 54272)
        rep_b = at("rep_b", [SMP, NB, SMP], BF16, H0 + 57344)
        keep_sb = at("keep_sb", [SMP, NK], BF16, H0 + 58368)
        same = at("same", [96, P], F32, H0 + 60544)
        keep_sf = at("keep_sf", [SMP, NK], F32, H0 + 16384)
        qa_pad = at("qa_pad", [P, 2, HA, 96], F32, S0 + 73728)
        qb_own = at("qb_own", [P, 2, HB, NT], F32, S0 + 76800)
        pa_s = at("pa_s", [96, NK], F32, S0 + 77312)
        pb_s = at("pb_s", [SMP, NK], F32, V0)
        pa_t = at("pa_t", [P, PAGES + 1, 32], F32, V0 + 4352)
        pb_t = at("pb_t", [P, PAGES + 1, SMP], F32, V0 + 5504)
        o_s = at("o_s", [P, HA + HB, SMP], F32, V0 + 7808)
        oa_row = at("oa_row", [P, HD], F32, V0 + 10880)
        ob_row = at("ob_row", [SMP, HD], F32, V0 + 11392)
        maskn = at("maskn", [96, 2, SMP], BF16, V0 + 11904)
        rep_own = at("rep_own", [SMP, 2, SMP], BF16, V0 + 12160)
        row_s = at("row_s", [P, 16], F32, V0 + 12416)
        MXA, MXB, MX3, MXC, NMA, NMB, LA, LB, RA, RB = 0, 1, 2, 5, 6, 7, 8, 9, 10, 11

        smp_landed = sem("smp_landed")
        smp_cast = sem("smp_cast")
        k_landed = [sem(f"k_landed{i}") for i in range(2)]
        v_raw_landed = [sem(f"v_raw_landed{i}") for i in range(2)]
        prep_set = sem("prep_set")
        st_done = sem("st_done")
        st_out = [sem(f"st_out{i}") for i in range(2)]
        sa_done = sem("sa_done")
        sb_done = sem("sb_done")
        sa_step = sem("sa_step")
        sb_step = sem("sb_step")
        nma_set = sem("nma_set")
        nmb_set = sem("nmb_set")
        ea_done = sem("ea_done")
        eb_done = sem("eb_done")
        la_sum = sem("la_sum")
        pva_done = sem("pva_done")
        o_row_set = sem("o_row_set")
        ra_set = sem("ra_set")
        rb_set = sem("rb_set")
        so_done = sem("so_done")
        RAW = 16 * (1 + PAGES)
        KU, SU = 12, 18

        def each_sequence(eng, body):
            body(0, 0, 0, False)
            with eng.Fori(0, NB // 2 - 1) as i:
                body(2 * i + 1, 1, i, False)
                body(2 * i + 2, 0, i + 1, False)
            body(NB - 1, 1, NB // 2 - 1, True)

        def load_rows(sp, b, par, win, pool, landed):
            src = ins[win[1]][0, bass.ds(b, 1)][0]
            sp.dma_start(win[0][par][:], src.rearrange("(c p) h d -> p c (h d)", p=P)).then_inc(landed[par], 16)
            for j in range(PAGES):
                page = sp.value_load(pages_n[0:1, bass.ds(b * PAGES + j, 1)], min_val=0, max_val=POOL_PAGES - 1)
                src = ins[pool[1]][0, bass.ds(page, 1)][0]
                sp.dma_start(pool[0][par][:, j, :], src.rearrange("p h d -> p (h d)")).then_inc(landed[par], 16)

        def load_keys(sp, b, par):
            if not isinstance(b, int) or b >= 3:
                sp.wait_ge(st_done, b * SU + (2 * KU - 3 * SU))
            elif b == 2:
                sp.wait_ge(st_done, KU)
            load_rows(sp, b, par, (win_k, "cache_win_k"), (pool_k, "cache_k"), k_landed)

        def load_values(sp, b, par):
            if not isinstance(b, int) or b >= 2:
                sp.wait_ge(so_done, b - 1)
            load_rows(sp, b, par, (win_v, "cache_win_v"), (pool_v, "cache_v"), v_raw_landed)

        def sp_sample_early(sp):
            sp.wait_ge(kv_stored, 16 * 10)
            sp.wait_ge(mask_cast, 1)
            proj = scr["proj"]
            sp.dma_start(mask_sf[:], ins["mask_s"]).then_inc(smp_landed, 16)
            sp.dma_start(rep_f[:], ins["rep"]).then_inc(smp_landed, 16)
            sp.dma_start(keep_sf[:], scr["keep"][len(PICKS) - 1, 0:SMP, :]).then_inc(smp_landed, 16)
            for dst, first, n in ((0, T_QA, GRP * HA), (GRP * HA, T_QB, HB)):
                sp.dma_start(q_s[:, dst:dst + n, :], proj[first:first + n, :, SEQ:TOK].rearrange("m p n -> p m n"))\
                    .then_inc(smp_landed, 16)
            sp.dma_start(same[:], ins["same"]).then_inc(smp_landed, 16)
            load_keys(sp, 0, 0)

        def sp_values_early(sp):
            sp.wait_ge(smp_cast, 3)
            load_values(sp, 0, 0)

        def sp_sample(sp):
            sp.wait_ge(o_out, NJ)
            sp.wait_ge(att_stored[0], 16 * QT // 2)
            sp.wait_ge(att_stored[1], 16 * QT // 2)
            load_keys(sp, 1, 1)
            load_values(sp, 1, 1)
            load_keys(sp, 2, 0)
            with sp.Fori(1, NB // 2 - 1) as i:
                for u in range(2):
                    load_values(sp, 2 * i + u, u)
                    load_keys(sp, 2 * i + (u + 1), 1 - u)
            load_values(sp, NB - 2, 0)
            load_keys(sp, NB - 1, 1)
            load_values(sp, NB - 1, 1)
            sp_merge(sp)

        def cast_sample_mask(pool, x):
            pool.wait_ge(smp_landed, 16 * 6)
            dst, src = ((mask_sb, mask_sf), (rep_b, rep_f), (keep_sb, keep_sf))[x]
            nc.gpsimd.tensor_copy(dst[:], src[:]).then_inc(smp_cast, 1)

        def pool_sample(pool):
            pool.wait_ge(pv_done, NJ)
            nc.gpsimd.memset(qa_pad[:], 0.0).then_inc(smp_cast, 1)
            pool.wait_ge(smp_cast, 4)

            def prepare(b, par, half, last):
                if not isinstance(b, int) or b >= 2:
                    pool.wait_ge(sb_done, b - 1)
                t0 = b * NT
                by_group = q_s[:, 0:GRP * HA, :].rearrange("p (g h) n -> p g h n", g=GRP)
                for h in range(HA):
                    dst = qa_pad[:, par, h, :].rearrange("p (g r) -> p g r", g=GRP)[:, :, h * NT:(h + 1) * NT]
                    nc.gpsimd.tensor_copy(dst, by_group[:, :, h, bass.ds(t0, NT)]).then_inc(prep_set, 1)
                nc.gpsimd.tensor_copy(qb_own[:, par], q_s[:, GRP * HA:, bass.ds(t0, NT)]).then_inc(prep_set, 1)
                nc.gpsimd.tensor_copy(maskn[:, par, :], mask_sb[:, bass.ds(b * SMP + PAST, SMP)]).then_inc(prep_set, 1)
                nc.gpsimd.tensor_copy(rep_own[:, par, :],
                                      rep_b[:, bass.ds(b, 1), :].rearrange("p o n -> p (o n)")).then_inc(prep_set, 1)

            prepare(0, 0, 0, False)
            prepare(1, 1, 0, False)
            with pool.Fori(1, NB // 2) as i:
                prepare(2 * i, 0, i, False)
                prepare(2 * i + 1, 1, i, False)
            pool_merge(pool)

        def key_group(j):
            return j // 2, j % 2

        def act_sample(act):
            def keys_out(base):
                for j in range(1, KU, 2):
                    h, half = key_group(j)
                    act.wait_ge(st_done, base + j + 1)
                    nc.scalar.copy(kp_t[:, h, half * 512:(half + 1) * 512], banks[:, 7, :]).then_inc(st_out[1], 1)

            keys_out(0)

            def body(b, par, half, last):
                act.wait_ge(nma_set, b + 1)
                if not isinstance(b, int) or b >= 1:
                    act.wait_ge(so_done, b)
                nc.scalar.activation(pa_s[:], flat(0, 96, NK), ACT.Exp, bias=row_s[0:96, NMA:NMA + 1], scale=SCALE,
                                     accum_out=row_s[0:96, LA:LA + 1]).then_inc(ea_done, 1)
                act.wait_ge(nmb_set, b + 1)
                nc.scalar.activation(pb_s[:], flat(3, SMP, NK), ACT.Exp, bias=row_s[0:SMP, NMB:NMB + 1], scale=SCALE,
                                     accum_out=row_s[0:SMP, LB:LB + 1]).then_inc(eb_done, 1)
                base = b * SU + KU
                if not last:
                    keys_out(base)
                else:
                    base = base - KU
                act.wait_ge(st_done, base + KU + 3)
                nc.scalar.copy(pb_t[:, 0:PAGES, :], banks[:, 6, :].rearrange("p (c r) -> p c r", c=PAGES))\
                    .then_inc(st_out[0], 1)
                act.wait_ge(st_done, base + KU + 4)
                nc.scalar.copy(pb_t[0:SMP, PAGES, :], banks[0:SMP, 7, 0:SMP]).then_inc(st_out[1], 1)

            each_sequence(act, body)
            act_merge(act)

        def outputs_out(dve, b, use):
            dve.wait_ge(st_done, use + 1)
            for h in range(HA):
                last_i = nc.vector.tensor_copy(o_s[:, h, bass.ds(b * NT, NT)],
                                               banks[:, 6, h * (32 + NT):h * (32 + NT) + NT])
            last_i.then_inc(st_out[0], 1)
            dve.wait_ge(st_done, use + 2)
            nc.vector.tensor_copy(o_s[:, HA:, bass.ds(b * NT, NT)],
                                  banks[:, 7, 0:SMP].rearrange("p (m n) -> p m n", n=NT)).then_inc(st_out[1], 1)

        def dve_sample(dve):
            def keys_out(base):
                for j in range(0, KU, 2):
                    h, half = key_group(j)
                    dve.wait_ge(st_done, base + j + 1)
                    nc.vector.tensor_copy(kp_t[:, h, half * 512:(half + 1) * 512], banks[:, 6, :])\
                        .then_inc(st_out[0], 1)

            keys_out(0)

            def body(b, par, half, last):
                col1 = lambda c, r0=0, r1=96: row_s[r0:r1, c:c + 1]

                def link(ins_, sem_, per, k):
                    ins_.then_inc(sem_, 1)
                    dve.wait_ge(sem_, b * per + k)

                base = b * SU + KU
                if not isinstance(b, int) or b >= 1:
                    outputs_out(dve, b - 1, base - 2)
                dve.wait_ge(sa_done, b + 1)
                link(nc.vector.tensor_reduce(col1(MXA), flat(0, 96, NK), AX, ALU.max), sa_step, 3, 1)
                for g in range(GRP):
                    last_i = nc.vector.tensor_copy(row_s[0:32, MX3 + g:MX3 + g + 1], col1(MXA, 32 * g, 32 * g + 32))
                link(last_i, sa_step, 3, 2)
                link(nc.vector.tensor_reduce(row_s[0:32, MXC:MXC + 1], row_s[0:32, MX3:MX3 + GRP], AX, ALU.max),
                     sa_step, 3, 3)
                for g in range(GRP):
                    last_i = nc.vector.tensor_scalar(col1(NMA, 32 * g, 32 * g + 32), row_s[0:32, MXC:MXC + 1], -SCALE,
                                                     None, ALU.mult)
                last_i.then_inc(nma_set, 1)
                dve.wait_ge(sb_done, b + 1)
                link(nc.vector.tensor_reduce(col1(MXB, 0, SMP), flat(3, SMP, NK), AX, ALU.max), sb_step, 1, 1)
                nc.vector.tensor_scalar(col1(NMB, 0, SMP), col1(MXB, 0, SMP), -SCALE, None, ALU.mult)\
                    .then_inc(nmb_set, 1)
                if not last:
                    keys_out(base)
                else:
                    base = base - KU
                dve.wait_ge(eb_done, b + 1)
                nc.vector.reciprocal(col1(RB, 0, SMP), col1(LB, 0, SMP)).then_inc(rb_set, 1)
                by_group = lambda rows, bank, a, c: banks[0:rows, bank, a:a + 96 * c].rearrange(
                    "p (c g r) -> p c r g", c=c, g=GRP)
                dve.wait_ge(st_done, base + KU + 1)
                nc.vector.tensor_reduce(pa_t[:, 0:5, :], by_group(P, 6, 0, 5), AX, ALU.add).then_inc(st_out[0], 1)
                dve.wait_ge(st_done, base + KU + 2)
                nc.vector.tensor_reduce(pa_t[:, 5:8, :], by_group(P, 7, 0, 3), AX, ALU.add)
                nc.vector.tensor_reduce(pa_t[0:SMP, 8:9, :], by_group(SMP, 7, 288, 1), AX, ALU.add)\
                    .then_inc(st_out[1], 1)
                dve.wait_ge(la_sum, b + 1)
                nc.vector.reciprocal(col1(RA, 0, P), banks[:, 2, 256:257]).then_inc(ra_set, 1)
                dve.wait_ge(ra_set, b + 1)
                dve.wait_ge(pva_done, b + 1)
                nc.vector.tensor_scalar(oa_row[:], banks[:, 1, 0:HD], col1(RA, 0, P), None, ALU.mult)\
                    .then_inc(o_row_set, 1)
                dve.wait_ge(rb_set, b + 1)
                dve.wait_ge(so_done, b + 1)
                nc.vector.tensor_scalar(ob_row[:], banks[0:SMP, 3, 0:HD], col1(RB, 0, SMP), None, ALU.mult)\
                    .then_inc(o_row_set, 1)

            each_sequence(dve, body)
            dve_merge(dve)

        def pe_sample(pe):
            def turn_keys(base, earlier, par):
                for j in range(KU):
                    h, half = key_group(j)
                    if not isinstance(earlier, int) or earlier + j // 2 > 0:
                        pe.wait_ge(st_out[j % 2], earlier + j // 2)
                    src = win_k[par] if h < HA else pool_k[par]
                    c0 = (h if h < HA else h - HA) * HD
                    for q in range(4):
                        tr = nc.tensor.transpose(banks[:, 6 + j % 2, q * P:(q + 1) * P],
                                                 src[:, 4 * half + q, c0:c0 + HD], ident[:])
                    tr.then_inc(st_done, 1)

            pe.wait_ge(t_out, len(USES))
            pe.wait_ge(k_landed[0], RAW)
            turn_keys(0, 0, 0)

            def turn_outputs():
                nc.tensor.transpose(banks[:, 6, 0:P], oa_row[:], ident[:]).then_inc(st_done, 1)
                nc.tensor.transpose(banks[:, 7, 0:SMP], ob_row[:], ident[0:SMP, 0:SMP]).then_inc(st_done, 1)

            def strips():
                return (0, 512, 0), (512, 1024, 1), (1024, NK, 2)

            def body(b, par, half, last):
                pe.wait_ge(prep_set, 7 * b + 7)
                earlier = b * (SU // 2) + KU // 2
                first = isinstance(b, int) and b == 0
                for x in range(2):
                    pe.wait_ge(st_out[x], earlier - (not first))
                if not isinstance(b, int) or b >= 1:
                    pe.wait_ge(o_row_set, b * 2)
                for a, z, bank in strips():
                    dst = banks[0:96, bank, 0:z - a]
                    for h in range(HA):
                        keys = kp_t[:, h, a:z] if a < PAST else k_t[:, h, SEQ:TOK]
                        nc.tensor.matmul(dst, qa_pad[:, par, h, :], keys, start=(h == 0), stop=False)
                    mask = mask_sb[:, a:z] if a < PAST else maskn[:, par, :]
                    mm = nc.tensor.matmul(dst, identb[0:96, 0:96], mask, start=False, stop=True)
                    if bank == 0 and not first:
                        turn_outputs()
                mm.then_inc(sa_done, 1)
                for a, z, bank in strips():
                    for kv in range(KVB):
                        keys = kp_t[:, HA + kv, a:z] if a < PAST else k_t[:, HA + kv, SEQ:TOK]
                        nc.tensor.matmul(banks[32 * kv:32 * kv + 32, 3 + bank, 0:z - a],
                                         qb_own[:, par, 4 * kv:4 * kv + 4, :].rearrange("p h t -> p (h t)"), keys,
                                         start=True, stop=False, skip_group_check=True)
                    mm = nc.tensor.matmul(banks[0:SMP, 3 + bank, 0:z - a], rep_own[:, par, :], keep_sb[:, a:z],
                                          start=False, stop=True, skip_group_check=True)
                mm.then_inc(sb_done, 1)
                if not last:
                    pe.wait_ge(k_landed[1 - par], (half + (1 + par)) * RAW)
                    turn_keys(b * SU + KU, earlier, 1 - par)
                    used = KU // 2
                else:
                    used = 0
                pe.wait_ge(ea_done, b + 1)
                for x, tiles in ((0, range(0, 5)), (1, range(5, 9))):
                    pe.wait_ge(st_out[x], earlier + used)
                    for c in tiles:
                        n = min(P, NK - c * P)
                        tr = nc.tensor.transpose(banks[0:n, 6 + x, (c - tiles[0]) * 96:(c - tiles[0] + 1) * 96],
                                                 pa_s[:, c * P:c * P + n], ident[0:96, 0:96])
                    tr.then_inc(st_done, 1)
                pe.wait_ge(eb_done, b + 1)
                pe.wait_ge(st_out[0], earlier + used + 1)
                nc.tensor.matmul(banks[:, 2, 256:257], same[:], row_s[0:96, LA:LA + 1], start=True, stop=True)\
                    .then_inc(la_sum, 1)
                for c in range(PAGES):
                    tr = nc.tensor.transpose(banks[:, 6, c * SMP:(c + 1) * SMP], pb_s[:, c * P:(c + 1) * P],
                                             ident[0:SMP, 0:SMP])
                tr.then_inc(st_done, 1)
                pe.wait_ge(v_raw_landed[par], half * RAW + RAW)
                pe.wait_ge(st_out[1], earlier + used + 1)
                for h in range(HA):
                    for c in range(PAGES + 1):
                        v = win_v[par][:, c, h * HD:(h + 1) * HD] if c < PAGES else v_tok[0:SMP, QT, h * HD:(h + 1) * HD]
                        w = pa_t[0:P if c < PAGES else SMP, c, :]
                        mm = nc.tensor.matmul(banks[32 * h:32 * h + 32, 1, 0:HD], w, v, start=(c == 0),
                                              stop=(c == PAGES), skip_group_check=True)
                    if h == 0:
                        nc.tensor.transpose(banks[0:SMP, 7, 0:SMP], pb_s[:, PAST:NK], ident[0:SMP, 0:SMP])\
                            .then_inc(st_done, 1)
                mm.then_inc(pva_done, 1)
                for x in range(2):
                    pe.wait_ge(st_out[x], earlier + used + 2)
                for kv in range(KVB):
                    c0 = (HA + kv) * HD
                    for c in range(PAGES + 1):
                        v = pool_v[par][:, c, kv * HD:(kv + 1) * HD] if c < PAGES else v_tok[0:SMP, QT, c0:c0 + HD]
                        w = pb_t[0:P if c < PAGES else SMP, c, kv * 32:(kv + 1) * 32]
                        mm = nc.tensor.matmul(banks[32 * kv:32 * kv + 32, 3, 0:HD], w, v, start=(c == 0),
                                              stop=(c == PAGES), skip_group_check=True)
                mm.then_inc(so_done, 1)

            each_sequence(pe, body)
            pe.wait_ge(o_row_set, 2 * NB)
            for x in range(2):
                pe.wait_ge(st_out[x], NB * SU // 2 - 1)
            turn_outputs()
            pe_merge(pe)

        KA, KB_ = HA, HB
        KO = KA + KB_
        o_hi = at("o_hi", [P, KO, TOK], F32R, A0)
        o_lo = at("o_lo", [P, KO, TOK], F32R, A0 + 52224)
        o_in = [at(f"o_in{i}", [P, SEQ], F32, off) for i, off in enumerate((H0 + 61056, W0 + 8192, W0 + 12288))]
        z_in = [at(f"z_in{i}", [P, SEQ], F32, off) for i, off in enumerate((H0 + 65152, W0 + 24576, W0 + 28672))]
        z_s = at("z_s", [P, KO, SMP], F32, H0)
        og_s = at("og_s", [P, KO, SMP], F32, A0 + 130560)
        og = at("og", [P, 2, SEQ], F32, A0 + 121856)
        ua_g = at("ua_g", [P, 2, 384], F32, A0 + 130560)
        ub_g = at("ub_g", [P, 2, 384], F32, A0 + 133632)
        gates = at("gates", [P, 2, 2, TOK], F32, W0 + 40960)
        merged = at("merged", [P, 2, TOK], F32, W0 + 58368)
        M_GROUPS = (8, 0, 4, 12)
        M_ORDER = [k for g in M_GROUPS for k in range(g, g + 4)]
        m_in = at("m_in", [P, KT, TOK], F32, H_LO)
        x_col = at("x_col", [P, 2, TT, P], F32, W0 + 40960)
        r_col = at("r_col", [P, 2, TOK], F32, W0 + 50176)
        r_tok = at("r_tok", [P, 2, TT, P], F32, W0 + 58880)
        sq_sum = at("sq_sum", [P, KT, TT], F32, W0 + 68096)
        KD = KT - 2
        y_row = at("y_row", [P, TT, D], F32, A0)
        g_row = at("g_row", [P, D], F32, A0 + TT * D * 4)

        oz_landed = [sem(f"oz_landed{i}") for i in range(3)]
        zs_landed = sem("zs_landed")
        og_s_step = sem("og_s_step")
        og_set = sem("og_set")
        o_hi_set = sem("o_hi_set")
        o_lo_set = sem("o_lo_set")
        u_landed = sem("u_landed")
        u_hi_set = sem("u_hi_set")
        u_lo_set = sem("u_lo_set")
        gate_landed = [sem(f"gate_landed{i}") for i in range(2)]
        u_done = sem("u_done")
        u_out = sem("u_out")
        m_set = sem("m_set")
        m_stored = [sem(f"m_stored{i}") for i in range(2)]
        m_landed = [sem(f"m_landed{i}") for i in range(4)]
        m_hi_set = sem("m_hi_set")
        m_lo_set = sem("m_lo_set")
        v_landed = sem("v_landed")
        v_hi_set = sem("v_hi_set")
        v_lo_set = sem("v_lo_set")
        y_done = sem("y_done")
        y_out = sem("y_out")
        r_turned = sem("r_turned")
        r_stored = [sem(f"r_stored{i}") for i in range(2)]
        x_col_landed = [sem(f"x_col_landed{i}") for i in range(2)]
        r_added = sem("r_added")
        r_squared = sem("r_squared")
        r_summed = sem("r_summed")
        row_landed = [sem(f"row_landed{i}") for i in range(TT)]
        g_landed = sem("g_landed")
        y_ssum = sem("y_ssum")
        y_root = sem("y_root")
        y_rstd = sem("y_rstd")
        y_norm = sem("y_norm")
        y_stored = sem("y_stored")

        def column_tiles(eng, body):
            body(0, 0, 0)
            body(1, 1, 0)
            with eng.Fori(1, KT // 2) as i:
                body(2 * i, 0, i)
                body(2 * i + 1, 1, i)

        w_pa, w_pb, w_out = ins["w_pa"][0], ins["w_pb"][0], ins["w_out"][0]
        y_tiles = [(outs["y_prompt"][0, t * P:(t + 1) * P, :], P) for t in range(QT)]
        y_tiles.append((outs["y_sample"].rearrange("b t d -> (b t) d"), SMP))

        def sp_merge(sp):
            sp.wait_ge(so_done, NB - 1)
            sp.dma_start(z_s[:, 0:KA, :], scr["proj"][T_ZA:T_ZA + KA, :, SEQ:TOK].rearrange("m p n -> p m n"))\
                .then_inc(zs_landed, 16)
            sp.dma_start(z_s[:, KA:, :], scr["proj"][T_ZB:T_ZB + KB_, :, SEQ:TOK].rearrange("m p n -> p m n"))\
                .then_inc(zs_landed, 16)
            sp.dma_start(w_raw[:, 0:KA, :], w_pa[:, 0:P].rearrange("(k p) n -> p k n", p=P)).then_inc(u_landed, 16)
            sp.dma_start(w_raw[:, KA:KO, :], w_pb[:, 0:P].rearrange("(k p) n -> p k n", p=P)).then_inc(u_landed, 16)
            for k in range(KO):
                need(sp, og_set, k - 2)
                z = T_ZA + k if k < KA else T_ZB + k - KA
                sp.dma_start(o_in[k % 3][:], scr["att"][k]).then_inc(oz_landed[k % 3], 16)
                sp.dma_start(z_in[k % 3][:], scr["proj"][z, :, 0:SEQ]).then_inc(oz_landed[k % 3], 16)

            def load_merge(c, par, half):
                cols = bass.ds(c * P, P)
                if not isinstance(c, int) or c >= 1:
                    sp.wait_ge(u_lo_set, c)
                    for k0, k1, w in ((0, KA, w_pa), (KA, KO, w_pb)):
                        sp.dma_start(w_raw[:, k0:k1, :], w[:, cols].rearrange("(k p) n -> p k n", p=P))\
                            .then_inc(u_landed, 16)
                need(sp, m_set, (c - 1) * 3)
                if isinstance(c, int) and c == 1:
                    sp.wait_ge(og_set, KO)
                for x in range(2):
                    sp.dma_start(gates[:, par, x, :], scr["proj"][bass.ds(c + (T_G + x * KT), 1)][0])\
                        .then_inc(gate_landed[par], 16)

            column_tiles(sp, load_merge)
            def load_merged(g):
                k = M_GROUPS[g]
                sp.dma_start(m_in[:, k:k + 4, :], scr["merged"][k:k + 4].rearrange("m p n -> p m n"))\
                    .then_inc(m_landed[g], 16)

            sp.wait_ge(u_lo_set, KT)
            sp.dma_start(w_raw[:], w_out[:, 0:P].rearrange("(k p) n -> p k n", p=P)).then_inc(v_landed, 16)
            for i in range(2):
                sp.wait_ge(m_stored[i], 16 * (M_GROUPS[0] + 4) // 2)
            load_merged(0)
            sp.wait_ge(u_done, 3 * KT)
            load_merged(1)
            load_merged(2)
            sp.wait_ge(m_set, 3 * KT)
            for i in range(2):
                sp.wait_ge(m_stored[i], 16 * KT // 2)
            load_merged(3)

            def load_out(c, par, half):
                if not isinstance(c, int) or c >= 1:
                    sp.wait_ge(v_lo_set, c)
                    sp.dma_start(w_raw[:], w_out[:, bass.ds(c * P, P)].rearrange("(k p) n -> p k n", p=P))\
                        .then_inc(v_landed, 16)
                need(sp, r_summed, 2 * c - 2)
                sp.dma_start(x_col[:, par, 0:QT, :], ins["x_prompt"][0][:, bass.ds(c * P, P)]
                             .rearrange("(t p) n -> p t n", p=P)).then_inc(x_col_landed[par], 16)
                sp.dma_start(x_col[0:SMP, par, QT, :], x_tiles[QT][0][:, bass.ds(c * P, P)])\
                    .then_inc(x_col_landed[par], 16)

            column_tiles(sp, load_out)
            sp.wait_ge(y_done, 3 * KT)
            sp.dma_start(g_row[:], ins["g_final"].rearrange("(o n) -> o n", o=1).to_broadcast([P, D])).then_inc(g_landed, 16)
            for i in range(2):
                sp.wait_ge(r_stored[i], 32 * (KD // 2))
            for t in range(TT):
                rows = ROWS_OF(t)
                sp.dma_start(y_row[0:rows, t, 0:KD * P], scr["resid"][t * P:t * P + rows, 0:KD * P]).then_inc(row_landed[t], 16)

        def pool_merge(pool):
            def store_merged(c, par, half):
                pool.wait_ge(m_set, 3 * c + 3)
                pool.dma_start(scr["merged"][bass.ds(c, 1)][0], merged[:, par, :]).then_inc(m_stored[par], 16)

            column_tiles(pool, store_merged)

            def store_resid(c, par, half):
                pool.wait_ge(r_added, 2 * c + 2)
                cols = bass.ds(c * P, P)
                pool.dma_start(scr["resid"][0:SEQ, cols].rearrange("(t p) n -> p t n", p=P), r_tok[:, par, 0:QT, :])\
                    .then_inc(r_stored[par], 16)
                pool.dma_start(scr["resid"][SEQ:TOK, cols], r_tok[0:SMP, par, QT, :]).then_inc(r_stored[par], 16)

            store_resid(0, 0, 0)
            store_resid(1, 1, 0)
            with pool.Fori(1, KD // 2) as i:
                store_resid(2 * i, 0, i)
                store_resid(2 * i + 1, 1, i)
            for t in range(TT):
                rows = ROWS_OF(t)
                pool.wait_ge(y_norm, t + 1)
                pool.dma_start(y_tiles[t][0], y_row[0:rows, t, :]).then_inc(y_stored, 16)
            pool.wait_ge(y_stored, 16 * TT)
            pool.wait_ge(kv_stored, 16 * 10)

        def act_merge(act):
            def split_merge(c, par, half):
                act.wait_ge(u_landed, 32 * c + 32)
                need(act, u_done, (c - 1) * 3)
                nc.scalar.copy(w_hi[:, par, 0:KO, :], w_raw[:, 0:KO, :]).then_inc(u_hi_set, 1)

            split_merge(0, 0, 0)
            act.wait_ge(og_s_step, 1)
            nc.scalar.copy(o_hi[:, :, SEQ:TOK], og_s[:]).then_inc(og_s_step, 1)
            for k in range(KO):
                act.wait_ge(og_set, k + 1)
                nc.scalar.copy(o_hi[:, k, 0:SEQ], og[:, k % 2, :]).then_inc(o_hi_set, 1)

            split_merge(1, 1, 0)
            with act.Fori(1, KT // 2) as i:
                split_merge(2 * i, 0, i)
                split_merge(2 * i + 1, 1, i)
            act.wait_ge(v_landed, 16)
            act.wait_ge(u_done, 3 * (KT - 1))
            nc.scalar.copy(w_hi[:, 0], w_raw[:]).then_inc(v_hi_set, 1)
            act.wait_ge(u_done, 3 * KT)
            for x, k in enumerate(M_ORDER):
                act.wait_ge(m_landed[x // 4], 16)
                nc.scalar.copy(h_hi[:, k, :], m_in[:, k, :]).then_inc(m_hi_set, 1)

            def squares(c, par, half):
                for n, (rows, ts) in enumerate(((P, slice(0, QT)), (SMP, slice(QT, TT)))):
                    act.wait_ge(r_added, 2 * c + (n + 1))
                    nc.scalar.activation(x_col[0:rows, par, ts, :], r_tok[0:rows, par, ts, :], ACT.Square)\
                        .then_inc(r_squared, 1)

            def split_out(c, par):
                act.wait_ge(v_landed, c * 16 + 16)
                need(act, y_done, (c - 1) * 3)
                nc.scalar.copy(w_hi[:, par], w_raw[:]).then_inc(v_hi_set, 1)

            def out_step(c, par, half):
                split_out(c + 2, par)
                squares(c, par, half)

            split_out(1, 1)
            out_step(0, 0, 0)
            out_step(1, 1, 0)
            with act.Fori(1, KT // 2 - 1) as i:
                out_step(2 * i, 0, i)
                out_step(2 * i + 1, 1, i)
            squares(KT - 2, 0, KT // 2 - 1)
            squares(KT - 1, 1, KT // 2 - 1)
            act.wait_ge(y_ssum, 2)
            for rows, a, b in ((P, 0, QT), (SMP, QT, TT)):
                nc.scalar.activation(rstd[0:rows, a:b], ssum[0:rows, a:b], ACT.Sqrt, bias=epst[0:rows, :],
                                     scale=1.0 / D).then_inc(y_root, 1)

        def dve_merge(dve):
            def split_merge(c, par):
                dve.wait_ge(u_hi_set, c + 1)
                nc.vector.tensor_tensor(w_lo[:, par, 0:KO, :], w_raw[:, 0:KO, :], w_hi[:, par, 0:KO, :], ALU.subtract)\
                    .then_inc(u_lo_set, 1)

            split_merge(0, 0)
            outputs_out(dve, NB - 1, NB * SU - 2)
            dve.wait_ge(st_out[0], NB * SU // 2)
            dve.wait_ge(st_out[1], NB * SU // 2)
            dve.wait_ge(zs_landed, 32)
            nc.vector.tensor_tensor(og_s[:], o_s[:], z_s[:], ALU.mult).then_inc(og_s_step, 1)
            for k in range(KO + 1):
                if k < KO:
                    dve.wait_ge(oz_landed[k % 3], 32 * (k // 3 + 1))
                    need(dve, o_lo_set, k - 1)
                    nc.vector.tensor_tensor(og[:, k % 2, :], o_in[k % 3][:], z_in[k % 3][:], ALU.mult)\
                        .then_inc(og_set, 1)
                if k == 0:
                    dve.wait_ge(og_s_step, 2)
                    nc.vector.tensor_tensor(o_lo[:, :, SEQ:TOK], og_s[:], o_hi[:, :, SEQ:TOK], ALU.subtract)\
                        .then_inc(og_s_step, 1)
                else:
                    dve.wait_ge(o_hi_set, k)
                    nc.vector.tensor_tensor(o_lo[:, k - 1, 0:SEQ], og[:, (k - 1) % 2, :], o_hi[:, k - 1, 0:SEQ],
                                            ALU.subtract).then_inc(o_lo_set, 1)

            def merge(c, par, half):
                dve.wait_ge(gate_landed[par], half * 32 + 32)
                if not isinstance(c, int) or c >= 2:
                    dve.wait_ge(m_stored[par], half * 16)
                for x, (a, b) in enumerate(CHUNKS):
                    n, s = b - a, (par + x) % 2
                    dve.wait_ge(u_done, 3 * c + (x + 1))
                    need(dve, m_set, 3 * c + (x - 1))
                    nc.vector.tensor_tensor(ua_g[:, s, 0:n], banks[:, x, 0:n], gates[:, par, 0, a:b], ALU.mult)
                    nc.vector.tensor_tensor(ub_g[:, s, 0:n], banks[:, 3 + x, 0:n], gates[:, par, 1, a:b], ALU.mult)\
                        .then_inc(u_out, 1)
                    dve.wait_ge(u_out, 3 * c + (x + 1))
                    nc.vector.tensor_tensor(merged[:, par, a:b], ua_g[:, s, 0:n], ub_g[:, s, 0:n], ALU.add)\
                        .then_inc(m_set, 1)

            def merge_step(c, par, half):
                split_merge(c + 1, 1 - par)
                merge(c, par, half)

            merge_step(0, 0, 0)
            merge_step(1, 1, 0)
            with dve.Fori(1, KT // 2 - 1) as i:
                merge_step(2 * i, 0, i)
                merge_step(2 * i + 1, 1, i)
            merge_step(KT - 2, 0, KT // 2 - 1)
            dve.wait_ge(v_hi_set, 1)
            nc.vector.tensor_tensor(w_lo[:, 0], w_raw[:], w_hi[:, 0], ALU.subtract).then_inc(v_lo_set, 1)
            merge(KT - 1, 1, KT // 2 - 1)
            for x, k in enumerate(M_ORDER):
                dve.wait_ge(m_hi_set, x + 1)
                nc.vector.tensor_tensor(h_lo[:, k, :], m_in[:, k, :], h_hi[:, k, :], ALU.subtract)\
                    .then_inc(m_lo_set, 1)

            def split_out(c, par):
                dve.wait_ge(v_hi_set, c + 1)
                nc.vector.tensor_tensor(w_lo[:, par], w_raw[:], w_hi[:, par], ALU.subtract).then_inc(v_lo_set, 1)

            def gated(c, par, half):
                need(dve, r_turned, 3 * (c - 1))
                for x, (a, b) in enumerate(CHUNKS):
                    dve.wait_ge(y_done, 3 * c + (x + 1))
                    z = min(b, SEQ)
                    gate = mod_t[:, bass.ds(c + 2 * KT, 1), :].rearrange("p o n -> p (o n)")
                    if x == 2:
                        nc.vector.tensor_tensor(
                            r_col[:, par, SEQ:TOK].rearrange("p (b t) -> p b t", b=NB),
                            banks[:, x, SEQ - a:TOK - a].rearrange("p (b t) -> p b t", b=NB),
                            gate[:, 0:NB, None].to_broadcast([P, NB, NT]), ALU.mult)
                    last = nc.vector.tensor_scalar(r_col[:, par, a:z], banks[:, x, 0:z - a], gate[:, 8:9], None,
                                                   ALU.mult)
                    last.then_inc(y_out, 1)
                    if x == 2:
                        dve.wait_ge(y_out, 3 * c + 3)

            def add_rows(c, par, half):
                dve.wait_ge(x_col_landed[par], half * 32 + 32)
                if not isinstance(c, int) or c >= 2:
                    dve.wait_ge(r_stored[par], half * 32)
                dve.wait_ge(r_turned, 3 * c + 2)
                nc.vector.tensor_tensor(r_tok[:, par, 0:QT, :],
                                        banks[:, 3:5, :].rearrange("p b (t n) -> p (b t) n", n=P),
                                        x_col[:, par, 0:QT, :], ALU.add).then_inc(r_added, 1)
                dve.wait_ge(r_turned, 3 * c + 3)
                nc.vector.tensor_tensor(r_tok[0:SMP, par, QT, :], banks[0:SMP, 5, 0:P], x_col[0:SMP, par, QT, :],
                                        ALU.add).then_inc(r_added, 1)

            def sum_rows(c, par, half):
                for n, (rows, ts) in enumerate(((P, slice(0, QT)), (SMP, slice(QT, TT)))):
                    dve.wait_ge(r_squared, 2 * c + (n + 1))
                    nc.vector.tensor_reduce(sq_sum[0:rows, bass.ds(c, 1), ts].rearrange("p o t -> p (o t)"),
                                            x_col[0:rows, par, ts, :], AX, ALU.add).then_inc(r_summed, 1)

            def out_step(c, par, half):
                sum_rows(c - 2, par, half - 1)
                split_out(c + 1, 1 - par)
                gated(c, par, half)
                add_rows(c - 1, 1 - par, half - 1 + par)

            split_out(1, 1)
            gated(0, 0, 0)
            split_out(2, 0)
            gated(1, 1, 0)
            add_rows(0, 0, 0)
            with dve.Fori(1, KT // 2 - 1) as i:
                out_step(2 * i, 0, i)
                out_step(2 * i + 1, 1, i)
            out_step(KT - 2, 0, KT // 2 - 1)
            sum_rows(KT - 3, 1, KT // 2 - 2)
            gated(KT - 1, 1, KT // 2 - 1)
            add_rows(KT - 2, 0, KT // 2 - 1)
            add_rows(KT - 1, 1, KT // 2 - 1)
            sum_rows(KT - 2, 0, KT // 2 - 1)
            sum_rows(KT - 1, 1, KT // 2 - 1)
            dve.wait_ge(r_summed, 2 * KT)
            for rows, a, b in ((P, 0, QT), (SMP, QT, TT)):
                nc.vector.tensor_reduce(ssum[0:rows, a:b], sq_sum[0:rows, :, a:b].rearrange("p c t -> p t c"), AX,
                                        ALU.add).then_inc(y_ssum, 1)
            for n, (rows, a, b) in enumerate(((P, 0, QT), (SMP, QT, TT))):
                dve.wait_ge(y_root, n + 1)
                nc.vector.reciprocal(rstd[0:rows, a:b], rstd[0:rows, a:b]).then_inc(y_rstd, 1)
            dve.wait_ge(y_rstd, 2)
            dve.wait_ge(g_landed, 16)
            dve.wait_ge(y_done, 3 * KT)
            dve.wait_ge(r_added, 2 * KT)
            for t in range(TT):
                rows = ROWS_OF(t)
                last_cols = lambda ap: ap[:, KD * P:].rearrange("p (c n) -> p c n", n=P)
                nc.vector.scalar_tensor_tensor(out=last_cols(y_row[0:rows, t, :]), in0=r_tok[0:rows, :, t, :],
                                               scalar=rstd[0:rows, t:t + 1], in1=last_cols(g_row[0:rows, :]),
                                               op0=ALU.mult, op1=ALU.mult)
                dve.wait_ge(row_landed[t], 16)
                nc.vector.scalar_tensor_tensor(out=y_row[0:rows, t, 0:KD * P], in0=y_row[0:rows, t, 0:KD * P],
                                               scalar=rstd[0:rows, t:t + 1], in1=g_row[0:rows, 0:KD * P],
                                               op0=ALU.mult, op1=ALU.mult).then_inc(y_norm, 1)

        def pe_merge(pe):
            def three_passes(dst, par, ks, a, b, hi, lo):
                for k in ks:
                    nc.tensor.matmul(dst, w_hi[:, par, k, :], hi[:, k, a:b], start=(k == ks[0]), stop=False)
                    nc.tensor.matmul(dst, w_hi[:, par, k, :], lo[:, k, a:b], start=False, stop=False)
                    mm = nc.tensor.matmul(dst, w_lo[:, par, k, :], hi[:, k, a:b], start=False, stop=(k == ks[-1]))
                return mm

            for x in range(2):
                pe.wait_ge(st_out[x], NB * SU // 2)
            pe.wait_ge(og_s_step, 3)

            def merge(c, par, half):
                pe.wait_ge(u_lo_set, c + 1)
                for x, (a, b) in enumerate(CHUNKS):
                    need(pe, u_out, 3 * c + (x - 2))
                    three_passes(banks[:, x, 0:b - a], par, range(KA), a, b, o_hi, o_lo)
                    three_passes(banks[:, 3 + x, 0:b - a], par, range(KA, KO), a, b, o_hi, o_lo).then_inc(u_done, 1)

            pe.wait_ge(u_lo_set, 1)
            for k in range(KO):
                pe.wait_ge(o_lo_set, k + 1)
                for x, (a, b) in enumerate(CHUNKS):
                    dst = banks[:, x if k < KA else 3 + x, 0:b - a]
                    nc.tensor.matmul(dst, w_hi[:, 0, k, :], o_hi[:, k, a:b], start=(k in (0, KA)), stop=False)
                    nc.tensor.matmul(dst, w_hi[:, 0, k, :], o_lo[:, k, a:b], start=False, stop=False)
                    mm = nc.tensor.matmul(dst, w_lo[:, 0, k, :], o_hi[:, k, a:b], start=False,
                                          stop=(k in (KA - 1, KO - 1)))
                    if k == KO - 1:
                        mm.then_inc(u_done, 1)
            merge(1, 1, 0)
            with pe.Fori(1, KT // 2) as i:
                merge(2 * i, 0, i)
                merge(2 * i + 1, 1, i)

            def project(c, par):
                pe.wait_ge(v_lo_set, c + 1)
                for x, (a, b) in enumerate(CHUNKS):
                    need(pe, y_out, 3 * c + (x - 2))
                    three_passes(banks[:, x, 0:b - a], par, range(KT), a, b, h_hi, h_lo).then_inc(y_done, 1)

            def turn(c, par):
                pe.wait_ge(y_out, 3 * c + 3)
                need(pe, r_added, 2 * c)
                for x in range(3):
                    for t in range(4 * x, min(4 * x + 4, TT)):
                        rows = ROWS_OF(t)
                        tr = nc.tensor.transpose(banks[0:rows, 3 + x, (t % 4) * P:(t % 4 + 1) * P],
                                                 r_col[:, par, t * P:t * P + rows], ident[:])
                    tr.then_inc(r_turned, 1)

            pe.wait_ge(u_out, 3 * KT)
            first_products(pe, v_lo_set, m_lo_set, y_done, M_ORDER)
            project(1, 1)
            turn(0, 0)
            with pe.Fori(1, KT // 2) as i:
                project(2 * i, 0)
                turn(2 * i - 1, 1)
                project(2 * i + 1, 1)
                turn(2 * i, 0)
            turn(KT - 1, 1)

        block = ctx.enter_context(nc.Block())

        def pick_round(dve):
            nc.vector.max(best8[:], work[:])
            dve.drain()
            nc.vector.match_replace(work[:], best8[:], work[:], TAKEN)
            dve.drain()

        def picked(dve, picks):
            nc.vector.tensor_scalar(work[:], work[:], TAKEN, None, ALU.not_equal).then_inc(mask_picked, 1)
            dve.wait_ge(mask_picked, 2 * picks - 1)
            nc.vector.tensor_scalar(work[:], work[:], -BIG, None, ALU.mult).then_inc(mask_picked, 1)

        def index_scores(dve):
            dve.wait_ge(chunk_done, 3 * N_IDX)
            dve.wait_ge(rot_set, 3 * N_IDX)
            dve.wait_ge(col_stored[0], 32)
            dve.wait_ge(col_stored[1], 16)
            nc.vector.memset(ki_hi[ID:P, :], 0.0)
            nc.vector.memset(ki_lo[0:ID, :], 0.0)
            nc.vector.memset(qi_pair[:], 0.0).then_inc(idx_zeroed, 1)
            dve.wait_ge(idx_zeroed, 1)
            dve.wait_ge(idx_landed, 6 * 16)
            for h in range(IH):
                src = qi_t[ID * (h % 2):ID * (h % 2) + ID, h // 2, SEQ:TOK].rearrange(
                    "p (j b t) -> p j b t", b=2, t=NT)
                for b in range(2):
                    for j in range(NB // 2):
                        c0 = (2 * j + b) * NT
                        last = nc.vector.tensor_copy(qi_pair[ID * b:ID * b + ID, h, j, c0:c0 + NT], src[:, j, b, :])
            last.then_inc(idx_pair_set, 1)
            dve.wait_ge(wi_turned, 1)
            nc.vector.tensor_copy(wi_tok[:], banks[:, 5, 0:TT * IH].rearrange("p (t h) -> p t h", h=IH))\
                .then_inc(idx_pair_set, 1)
            dve.wait_ge(idx_pair_set, 2)
            dve.wait_ge(idx_copied, 8)
            n = 0
            for j, t in enumerate(PICKS):
                rows, width = ROWS_OF(t), WIDTH_OF(t)
                need(dve, acc_stored[j % 2], 16 * (j // 2))
                nc.vector.memset(acc[:, j % 2, :], -BIG).then_inc(acc_fill, 1)
                dve.wait_ge(acc_fill, j + 1)
                out = acc[0:rows, j % 2, 0:width]
                for h in range(IH):
                    dve.wait_ge(relu_set, n + 1)
                    need(dve, acc_step, n)
                    if h == 0:
                        nc.vector.tensor_scalar(out, relu_s[0:rows, n % 2, 0:width], wi_tok[0:rows, t, h:h + 1], None,
                                                ALU.mult).then_inc(acc_step, 1)
                    else:
                        nc.vector.scalar_tensor_tensor(out=out, in0=relu_s[0:rows, n % 2, 0:width],
                                                       scalar=wi_tok[0:rows, t, h:h + 1], in1=out, op0=ALU.mult,
                                                       op1=ALU.add).then_inc(acc_step, 1)
                    n += 1
                tail = acc[0:rows, j % 2, width - rows:width]
                dve.wait_ge(acc_step, n)
                nc.vector.tensor_tensor(tail, tail, mask_i[:] if t == QT else diag[:], ALU.add).then_inc(acc_set, 1)

        @block.sync
        def _(sp):
            sp.dma_start(c_rows[0:8, :], ins["c_sample"]).then_inc(small_in, 16)
            sp.dma_start(c_rows[8:9, :], ins["c_prompt"]).then_inc(small_in, 16)
            sp.dma_start(bada_r[:], ins["b_ada"][0].rearrange("(k p) -> k p", p=P)).then_inc(small_in, 16)
            sp.dma_start(gn_r[:], ins["g_norm"][0].rearrange("(k p) -> k p", p=P)).then_inc(small_in, 16)
            sp.dma_start(pages_n[:], ins["page_table"].rearrange("(o b) n -> o (b n)", o=1)).then_inc(small_in, 16)
            sp.dma_start(x_in[0:SMP, 0, :], x_tiles[QT][0]).then_inc(x_landed[0], 16)

            def load_step(t, u, i):
                need(sp, x_turned_bank, 4 * t)
                sp.dma_start(x_in[:, 1 - u, :], ins["x_prompt"][0, bass.ds(t * P, P), :]).then_inc(x_landed[1 - u], 16)
                for n in range(ADA_S):
                    if isinstance(t, int) and t == 0:
                        need(sp, c_turned, n - 1)
                    else:
                        sp.wait_ge(ada_lo_set, (t * ADA_S + n) * 2 - 4)
                    sp.dma_start(ada_w[:, n], w_ada[:, bass.ds(t * (ADA_S * ADA_C) + n * ADA_C, ADA_C)]
                                 .rearrange("(k p) n -> p k n", p=P)).then_inc(ada_landed[n], 16)

            first_steps(sp, load_step)
            sp.dma_start(rot_cos[:], ins["rot"][2]).then_inc(rot_ready, 16)
            sp.dma_start(rot_sin[:], ins["rot"][3]).then_inc(rot_ready, 16)
            sp.wait_ge(ada_used, 2 * ADA_N)
            for t, (src, width) in enumerate(IDX_SRC):
                load_tile(sp, t, src, width)
            sp.wait_ge(chunk_done, 3 * N_IDX)
            sp.wait_ge(idx_copies, 16 * NB * PAGES)
            sp.dma_start(pages_i[:].rearrange("p c b d -> p (c b) d"), scr["pages"].rearrange("n p d -> p n d"))\
                .then_inc(idx_pages, 16)
            sp.wait_ge(rot_set, 3 * N_IDX)
            sp.wait_ge(col_stored[0], 32)
            sp.wait_ge(col_stored[1], 16)
            sp.dma_start(qi_t[:], scr["proj"][0:2].rearrange("m p n -> p m n")).then_inc(idx_landed, 16)
            sp.dma_start(ki_hi[0:ID, :], scr["proj"][2, 0:ID, :]).then_inc(idx_landed, 16)
            sp.dma_start(ki_lo[ID:P, :], scr["proj"][2, 0:ID, :]).then_inc(idx_landed, 16)
            sp.dma_start(wi_r[:], scr["proj"][2, ID:ID + IH, :]).then_inc(idx_landed, 16)
            sp.dma_start(diag[:], ins["mask_p"][:, 14 * P:15 * P]).then_inc(idx_landed, 16)
            sp.dma_start(mask_i[:], ins["mask_i"]).then_inc(idx_landed, 16)
            sp.wait_ge(score_done, len(PICKS) * IH)
            load_tile(sp, N_IDX, w_in[:, 0:P])
            sp.dma_start(rot_cos[:], ins["rot"][0]).then_inc(rot_ready, 16)
            sp.dma_start(rot_sin[:], ins["rot"][1]).then_inc(rot_ready, 16)
            load_tile(sp, N_IDX + 1, w_in[:, P:2 * P])
            with sp.Fori(1, N_MAIN // 2) as i:
                for u in range(2):
                    load_tile(sp, 2 * i + (N_IDX + u), w_in[:, bass.ds(i * (2 * P) + u * P, P)])
            with sp.Fori(0, N_GATE // 2) as i:
                for u in range(2):
                    load_tile(sp, 2 * i + (T_G + u), w_in[:, bass.ds(i * (2 * P) + (COL_G + u * P), P)])
            sp_attention(sp)

        @block.gpsimd
        def _(pool):
            nc.gpsimd.memset(ident[:], 0.0).then_inc(ident_set, 1)
            pool.wait_ge(ident_set, 1)
            nc.gpsimd.affine_select(out=ident[:], in_=ident[:], compare_op=ALU.not_equal, fill=1.0, base=0,
                                    pattern=[[-1, P]], channel_multiplier=1).then_inc(ident_set, 1)
            nc.gpsimd.memset(epst[:], EPS).then_inc(ident_set, 1)
            pool.wait_ge(ident_set, 3)
            nc.gpsimd.tensor_copy(identb[:], ident[:]).then_inc(ident_set, 1)
            nc.gpsimd.tensor_tensor(fold[:], ident[0:18, 0:9], ident[0:18, 9:18], ALU.add).then_inc(ident_set, 1)
            pool.wait_ge(small_in, 80)
            for b in range(NB):
                with pool.Fori(0, PAGES) as j:
                    page = pool.value_load(pages_n[0:1, bass.ds(j + b * PAGES, 1)], min_val=0,
                                           max_val=POOL_PAGES - 1)
                    pool.dma_start(scr["pages"][bass.ds(j * NB + b, 1)][0],
                                   ins["cache_idx_k"][0, bass.ds(page, 1)][0]).then_inc(idx_copies, 16)
            for t in range(N_IDX):
                rows = IDX_SRC[t][1]
                pool.wait_ge(rot_set, 3 * (t + 1))
                pool.dma_start(scr["proj"][t, 0:rows, :], col[0:rows, t % 2, :]).then_inc(col_stored[t % 2], 16)
            for j, t in enumerate(PICKS):
                pool.wait_ge(acc_set, j + 1)
                pool.dma_start(scr["score"][j], acc[:, j % 2, :]).then_inc(acc_stored[j % 2], 16)
            rotated = 3 * N_IDX
            picks = 0
            for first, pairs, how, pick in RUNS:
                if pick:
                    if picks:
                        pool.wait_ge(mask_picked, 2 * picks)
                        pool.dma_start(scr["keep"][picks - 1], work[:]).then_inc(mask_stored, 16)
                        pool.wait_ge(mask_stored, 16 * picks)
                    else:
                        pool.wait_ge(acc_stored[0], 16 * 4)
                        pool.wait_ge(acc_stored[1], 16 * 3)
                    pool.dma_start(work[:], scr["score"][picks]).then_inc(work_landed, 16)
                    picks += 1
                with pool.Fori(0, pairs) as i:
                    for u in range(2):
                        par = (first + u) % 2
                        if how == "rot":
                            pool.wait_ge(rot_set, 6 * i + (rotated + 3 * (u + 1)))
                        else:
                            pool.wait_ge(chunk_free, 6 * i + 3 * (first + u + 1))
                        pool.dma_start(scr["proj"][bass.ds(2 * i + (first + u), 1)][0], col[:, par, :])\
                            .then_inc(col_stored[par], 16)
                if how == "rot":
                    rotated += 6 * pairs
            pool.wait_ge(mask_picked, 2 * picks)
            pool.dma_start(scr["keep"][picks - 1], work[:]).then_inc(mask_stored, 16)
            pool_attention(pool)

        @block.scalar
        def _(act):
            act.wait_ge(small_in, 80)
            nc.scalar.activation(c_silu[:], c_rows[:], ACT.Silu).then_inc(c_act, 1)

            def square(par, half, rows):
                act.wait_ge(x_landed[par], half * 16 + 16)
                nc.scalar.activation(x_sq[0:rows, :], x_in[0:rows, par, :], ACT.Square,
                                     accum_out=ssum[0:rows, par:par + 1]).then_inc(x_ssum, 1)

            def root(s, par, rows):
                act.wait_ge(x_ssum, s + 1)
                nc.scalar.activation(rstd[0:rows, par:par + 1], ssum[0:rows, par:par + 1], ACT.Sqrt,
                                     bias=epst[0:rows, :], scale=1.0 / D).then_inc(x_root, 1)

            def turned_rows(s, cols, rows):
                for q in range(4):
                    act.wait_ge(x_turned_bank, 4 * s + (q + 1))
                    nc.scalar.copy(xn_t[:, 4 * q:4 * q + 4, cols],
                                   banks[:, 4 + q, :].rearrange("p (k r) -> p k r", k=4)[:, :, 0:rows])\
                        .then_inc(x_copied, 1)

            def modulation_rows(c, par):
                act.wait_ge(ada_used, 2 * c + 2)
                need(act, ada_folded, c - 1)
                nc.scalar.copy(mod_r[:, par, :], banks[0:18, 2 + par, 0:ADA_C]).then_inc(mod_r_set, 1)

            act.wait_ge(ident_set, 5)
            square(0, 0, SMP)
            root(0, 0, SMP)

            def step(t, u, i):
                square(1 - u, i + u, P)
                root(t + 1, 1 - u, P)
                for n in range(ADA_S):
                    par = (u + n) % 2
                    act.wait_ge(ada_landed[n], t * 16 + 16)
                    c = t * ADA_S + n
                    for h in range(2):
                        need(act, ada_used, c * 2 + (h - 1))
                        nc.scalar.copy(ada_hi[:, h], ada_w[:, n, KT // 2 * h:KT // 2 * (h + 1), :])\
                            .then_inc(ada_hi_set, 1)
                    if not isinstance(c, int) or c >= 1:
                        modulation_rows(c - 1, 1 - par)
                    if n == 0:
                        if isinstance(t, int) and t == 0:
                            turned_rows(0, slice(SEQ, TOK), SMP)
                        else:
                            turned_rows(t, bass.ds((t - 1) * P, P), P)

            first_steps(act, step)
            modulation_rows(ADA_N - 1, (ADA_N - 1) % 2)
            turned_rows(QT, slice(SEQ - P, SEQ), P)
            act.wait_ge(gmod_set, 1)
            act.wait_ge(x_copied, 4 * TT)
            for k in range(KT):
                need(act, lo_set, k - 1)
                nc.scalar.activation(h_f[:, k % 2, 0:SEQ], xn_t[:, k, 0:SEQ], ACT.Identity,
                                     bias=mod_t[:, k, 8:9], scale=gmod[:, k, 8:9]).then_inc(hp_set, 1)
                act.wait_ge(hp_set, k + 1)
                act.wait_ge(hs_set, k + 1)
                nc.scalar.copy(h_hi[:, k, :], h_f[:, k % 2, :]).then_inc(hi_set, 1)
                if k == 1:
                    split_hi(act, 0, 0)
            for t in range(1, N_IDX):
                split_hi(act, t, t % 2, IDX_SRC[t][1])
            for n in range(NB // 2 * PAGES // 4):
                act.wait_ge(idx_turned, n + 1)
                nc.scalar.copy(past_t[:, n // 2, n % 2 * 512:(n % 2 + 1) * 512], banks[:, 6 + n % 2, :])\
                    .then_inc(idx_copied, 1)
            n = 0
            for t in PICKS:
                rows, width = ROWS_OF(t), WIDTH_OF(t)
                for h in range(IH):
                    act.wait_ge(score_done, n + 1)
                    need(act, acc_step, n - 1)
                    nc.scalar.activation(relu_s[0:rows, n % 2, 0:width],
                                         banks[0:rows, 3 * (n % 2):3 * (n % 2) + 3, :].rearrange(
                                             "p b n -> p (b n)")[:, 0:width],
                                         ACT.Relu, scale=IH ** -0.5 * ID ** -0.5).then_inc(relu_set, 1)
                    n += 1
            act.wait_ge(acc_stored[1], 16 * 3)
            split_hi(act, N_IDX, N_IDX % 2)
            act.wait_ge(acc_stored[0], 16 * 4)
            for first, pairs, how, pick in RUNS:
                last = first + 2 * pairs == N_PROJ
                with act.Fori(0, pairs - last) as i:
                    for u in range(2):
                        t, par = 2 * i + (first + u), (first + u) % 2
                        split_hi(act, t + 1, 1 - par)
                        if how != "rot":
                            leave_act(act, t, par, i + (first + u) // 2, how)
            split_hi(act, N_PROJ - 1, (N_PROJ - 1) % 2)
            for t in (N_PROJ - 2, N_PROJ - 1):
                leave_act(act, t, t % 2, t // 2, ACT.Sigmoid)
            act_attention(act)

        @block.vector
        def _(dve):
            dve.wait_ge(c_turned, 1)
            c_view = banks[:, 0, 0:KT * 9].rearrange("p (k n) -> p k n", k=KT)
            nc.vector.tensor_copy(c_hl[:, :, 0:9], c_view).then_inc(c_copied, 1)
            dve.wait_ge(c_copied, 1)
            nc.vector.tensor_tensor(c_hl[:, :, 9:18], c_view, c_hl[:, :, 0:9], ALU.subtract).then_inc(c_copied, 1)
            nc.vector.tensor_copy(bada_t[:], banks[:, 0, 160:208]).then_inc(c_copied, 1)
            nc.vector.tensor_copy(gn_t[:], banks[:, 0, 144:160]).then_inc(c_copied, 1)

            def scale_rows(s, par, rows):
                dve.wait_ge(x_root, s + 1)
                nc.vector.reciprocal(rstd[0:rows, par:par + 1], rstd[0:rows, par:par + 1]).then_inc(x_rstd, 1)
                dve.wait_ge(x_rstd, s + 1)
                nc.vector.tensor_scalar(x_in[0:rows, par, :], x_in[0:rows, par, :], rstd[0:rows, par:par + 1], None,
                                        ALU.mult).then_inc(x_scaled, 1)

            scale_rows(0, 0, SMP)

            def step(t, u, i):
                scale_rows(t + 1, 1 - u, P)
                for n in range(ADA_S):
                    for h in range(2):
                        dve.wait_ge(ada_hi_set, t * (2 * ADA_S) + (2 * n + h + 1))
                        nc.vector.tensor_tensor(ada_lo[:, h], ada_w[:, n, KT // 2 * h:KT // 2 * (h + 1), :],
                                                ada_hi[:, h], ALU.subtract).then_inc(ada_lo_set, 1)

            first_steps(dve, step)
            dve.wait_ge(ada_folded, ADA_N)
            dve.wait_ge(c_copied, 4)
            nc.vector.tensor_tensor(mod_t[:], banks[:, 1, 0:48 * 9].rearrange("p (k n) -> p k n", k=48),
                                    bada_t[:, :, None].to_broadcast([P, 48, 9]), ALU.add).then_inc(mod_set, 1)
            dve.wait_ge(mod_set, 1)
            nc.vector.scalar_tensor_tensor(out=gmod[:], in0=mod_t[:, KT:2 * KT, :], scalar=1.0,
                                           in1=gn_t[:, :, None].to_broadcast([P, KT, 9]), op0=ALU.add,
                                           op1=ALU.mult).then_inc(gmod_set, 1)
            dve.wait_ge(gmod_set, 1)
            dve.wait_ge(x_copied, 4 * TT)
            for k in range(KT):
                def by_token(small):
                    return small[:, k, 0:NB, None].to_broadcast([P, NB, NT])
                rows_s = h_f[:, k % 2, SEQ:TOK].rearrange("p (b t) -> p b t", b=NB)
                need(dve, lo_set, k - 1)
                nc.vector.tensor_tensor(rows_s, xn_t[:, k, SEQ:TOK].rearrange("p (b t) -> p b t", b=NB),
                                        by_token(gmod), ALU.mult).then_inc(hs_mul, 1)
                dve.wait_ge(hs_mul, k + 1)
                nc.vector.tensor_tensor(rows_s, rows_s, by_token(mod_t), ALU.add).then_inc(hs_set, 1)
                if k >= 1:
                    dve.wait_ge(hi_set, k)
                    nc.vector.tensor_tensor(h_lo[:, k - 1, :], h_f[:, (k - 1) % 2, :], h_hi[:, k - 1, :],
                                            ALU.subtract).then_inc(lo_set, 1)
                if k == 2:
                    split_lo(dve, 0, 0)
            dve.wait_ge(hi_set, KT)
            nc.vector.tensor_tensor(h_lo[:, KT - 1, :], h_f[:, (KT - 1) % 2, :], h_hi[:, KT - 1, :],
                                    ALU.subtract).then_inc(lo_set, 1)
            dve.wait_ge(rot_ready, 32)
            for t in range(N_IDX):
                rows = IDX_SRC[t][1]
                if t + 1 < N_IDX:
                    split_lo(dve, t + 1, (t + 1) % 2, IDX_SRC[t + 1][1])
                leave_rotated(dve, t, t % 2, t // 2, 3 * t, ID // 2, min(rows, P) // ID * ID, rows % ID)
            index_scores(dve)
            split_lo(dve, N_IDX, N_IDX % 2)
            dve.wait_ge(rot_ready, 64)
            rotated = 3 * N_IDX
            picks = 0
            for first, pairs, how, pick in RUNS:
                last = first + 2 * pairs == N_PROJ
                if pick:
                    picks += 1
                    dve.wait_ge(work_landed, 16 * picks)
                with dve.Fori(0, pairs - last) as i:
                    for u in range(2):
                        t, par = 2 * i + (first + u), (first + u) % 2
                        split_lo(dve, t + 1, 1 - par)
                        if how == "rot":
                            leave_rotated(dve, t, par, i + (first + u) // 2, 6 * i + (rotated + 3 * u), HD // 2,
                                          between=pick_round if pick else None)
                        elif pick:
                            for c in range(3):
                                pick_round(dve)
                        if pick:
                            for c in range(ROUNDS - 3):
                                pick_round(dve)
                if how == "rot":
                    rotated += 6 * pairs
                if last:
                    split_lo(dve, N_PROJ - 1, (N_PROJ - 1) % 2)
                    for c in range(2 * ROUNDS):
                        pick_round(dve)
                if pick:
                    picked(dve, picks)
            dve_attention(dve)

        @block.tensor
        def _(pe):
            pe.wait_ge(c_act, 1)
            pe.wait_ge(ident_set, 5)
            pe.wait_ge(small_in, 80)
            for k in range(KT):
                nc.tensor.transpose(banks[:, 0, k * 9:(k + 1) * 9], c_silu[:, k * P:(k + 1) * P], ident[0:9, 0:9])
            nc.tensor.transpose(banks[:, 0, 144:160], gn_r[:], ident[0:KT, 0:KT])
            nc.tensor.transpose(banks[:, 0, 160:208], bada_r[:], ident[0:48, 0:48]).then_inc(c_turned, 1)

            def turn_rows(s, par, rows):
                pe.wait_ge(x_scaled, s + 1)
                for q in range(4):
                    need(pe, x_copied, 4 * s + (q - 3))
                    for k in range(4 * q, 4 * q + 4):
                        tr = nc.tensor.transpose(banks[:, 4 + q, (k % 4) * P:(k % 4) * P + rows],
                                                 x_in[0:rows, par, k * P:(k + 1) * P], ident[0:rows, 0:rows])
                    tr.then_inc(x_turned_bank, 1)

            def fold_rows(c, par):
                pe.wait_ge(mod_r_set, c + 1)
                for m in range(ADA_C // P):
                    mm = nc.tensor.matmul(banks[:, 1, bass.ds(c * 18 + m * 9, 9)], mod_r[:, par, m * P:(m + 1) * P],
                                          fold[:], start=True, stop=True)
                mm.then_inc(ada_folded, 1)

            turn_rows(0, 0, SMP)
            pe.wait_ge(c_copied, 4)

            def step(t, u, i):
                for n in range(ADA_S):
                    c, par = t * ADA_S + n, (u + n) % 2
                    need(pe, mod_r_set, c - 1)
                    for h in range(2):
                        pe.wait_ge(ada_lo_set, c * 2 + (h + 1))
                        for k in range(KT // 2):
                            kk = KT // 2 * h + k
                            nc.tensor.matmul(banks[0:18, 2 + par, 0:ADA_C], c_hl[:, kk, :], ada_hi[:, h, k, :],
                                             start=(kk == 0), stop=False, skip_group_check=True)
                            mm = nc.tensor.matmul(banks[0:9, 2 + par, 0:ADA_C], c_hl[:, kk, 0:9], ada_lo[:, h, k, :],
                                                  start=False, stop=(kk == KT - 1), skip_group_check=True)
                        mm.then_inc(ada_used, 1)
                    if not isinstance(c, int) or c >= 1:
                        fold_rows(c - 1, 1 - par)
                turn_rows(t + 1, 1 - u, P)

            first_steps(pe, step)
            fold_rows(ADA_N - 1, (ADA_N - 1) % 2)
            first_products(pe, w_lo_set, lo_set, chunk_done)
            for t in range(1, N_IDX):
                products(pe, t, t % 2, IDX_SRC[t][1])
            pe.wait_ge(idx_pages, 16)
            for n in range(NB // 2 * PAGES // 4):
                need(pe, idx_copied, n - 1)
                for q in range(4):
                    m = n % 2 * 4 + q
                    tr = nc.tensor.transpose(
                        banks[:, 6 + n % 2, q * P:(q + 1) * P],
                        pages_i[:, m, 2 * (n // 2):2 * (n // 2) + 2, :].rearrange("p b d -> p (b d)"), ident[:])
                tr.then_inc(idx_turned, 1)
            pe.wait_ge(idx_landed, 6 * 16)
            for t in range(TT):
                rows = x_tiles[t][1]
                tr = nc.tensor.transpose(banks[0:rows, 5, t * IH:(t + 1) * IH], wi_r[:, t * P:t * P + rows],
                                         ident[0:IH, 0:IH])
            tr.then_inc(wi_turned, 1)
            pe.wait_ge(idx_pair_set, 2)
            pe.wait_ge(idx_copied, 8)
            n = 0
            for t in PICKS:
                rows, width = ROWS_OF(t), WIDTH_OF(t)
                for h in range(IH):
                    need(pe, relu_set, n - 1)
                    keys = (ki_hi, ki_lo)[h % 2]
                    for a in range(0, width, 512):
                        b = min(a + 512, width)
                        dst = banks[0:rows, 3 * (n % 2) + a // 512, 0:b - a]
                        if t < QT or a == PAST:
                            mm = nc.tensor.matmul(dst, qi_t[:, h // 2, t * P:t * P + rows], keys[:, a:b],
                                                  start=True, stop=True)
                        else:
                            for j in range(NB // 2):
                                mm = nc.tensor.matmul(dst, qi_pair[:, h, j, :], past_t[:, j, a:b], start=(j == 0),
                                                      stop=(j == NB // 2 - 1))
                    mm.then_inc(score_done, 1)
                    n += 1
            pe.wait_ge(relu_set, n)
            with pe.Fori(0, (N_PROJ - N_IDX) // 2) as i:
                for u in range(2):
                    products(pe, 2 * i + (N_IDX + u), (N_IDX + u) % 2)
            pe_attention(pe)


_INS = ["x_prompt", "x_sample", "cache_win_k", "cache_win_v", "cache_k", "cache_v", "cache_idx_k", "page_table",
        "c_prompt", "c_sample", "g_norm", "w_ada", "b_ada", "w_in", "w_pa", "w_pb", "w_out", "g_final"]
_OUTS = [("y_prompt", (1, SEQ, D)), ("y_sample", (NB, NT, D)),
         ("win_k_prompt", (1, 1, SEQ, HA, HD)), ("win_v_prompt", (1, 1, SEQ, HA, HD)),
         ("k_prompt", (1, 1, SEQ, KVB, HD)), ("v_prompt", (1, 1, SEQ, KVB, HD)), ("idx_k_prompt", (1, 1, SEQ, ID)),
         ("win_k_sample", (1, NB, NT, HA, HD)), ("win_v_sample", (1, NB, NT, HA, HD)),
         ("k_sample", (1, NB, NT, KVB, HD)), ("v_sample", (1, NB, NT, KVB, HD)), ("idx_k_sample", (1, NB, NT, ID))]
_SCRATCH = [("proj", (N_PROJ, P, TOK)), ("score", (7, P, TOK)), ("keep", (7, P, TOK)), ("att", (HA + HB, P, SEQ)),
            ("merged", (KT, P, TOK)), ("resid", (TOK, D)),
            ("pages", (PAGES * NB, P, ID))]


def kernel(**inputs):
    import numpy as _np
    import concourse.bacc as _bacc
    from concourse import mybir as _mybir
    from concourse.bass_utils import run_bass_kernel_spmd as _run

    nc = _bacc.Bacc("TRN2", target_bir_lowering=False, num_devices=1)
    arrays, ins, outs = {}, {}, {}
    given = {name: _np.ascontiguousarray(inputs[name]) for name in _INS}
    given.update(shape_tables())
    for name, a in given.items():
        arrays[f"in_{name}"] = a
        ins[name] = nc.dram_tensor(f"in_{name}", a.shape, _mybir.dt.from_np(a.dtype), kind="ExternalInput").ap()
    for name, shape in _OUTS:
        outs[name] = nc.dram_tensor(f"out_{name}", shape, _mybir.dt.float32, kind="ExternalOutput").ap()
    scr = {name: nc.dram_tensor(f"scratch_{name}", shape, _mybir.dt.float32, kind="Internal").ap()
           for name, shape in _SCRATCH}
    decode_step(nc, ins, outs, scr)
    r = _run(nc, [arrays], core_ids=[0])
    return tuple(r.results[0][f"out_{name}"] for name, _ in _OUTS)
```
